# Optimizing a Trainium2 kernel written in Bass

```python
import jax
import jax.numpy as jnp
from jax import lax
import numpy as np

D_MODEL = 1024
BATCH = 1
SEQ = 512
DEPTH = 2

N_META = 16
N_MIXERS = 3
CHUNK = 64
LEAD_PAD = (-N_META) % CHUNK
RMS_EPS = 1e-6
D_FF = 4 * D_MODEL

GDN_QK_HEADS = 8
GDN_V_HEADS = 16
GDN_HEAD_DIM = 128
GDN_CONV = 4
GDN_QK_DIM = GDN_QK_HEADS * GDN_HEAD_DIM
GDN_V_DIM = GDN_V_HEADS * GDN_HEAD_DIM
GDN_CONV_DIM = 2 * GDN_QK_DIM + GDN_V_DIM
GDN_IN = GDN_CONV_DIM + GDN_V_DIM + 2 * GDN_V_HEADS

MLSTM_HEADS = 8
MLSTM_QK_DIM = D_MODEL // 2
MLSTM_V_DIM = D_MODEL
MLSTM_DQK = MLSTM_QK_DIM // MLSTM_HEADS
MLSTM_DV = MLSTM_V_DIM // MLSTM_HEADS
MLSTM_IN = 2 * MLSTM_QK_DIM + 2 * MLSTM_V_DIM + 2 * MLSTM_HEADS
GATE_SOFTCAP = 15.0

MLA_HEADS = 16
MLA_NOPE = 64
MLA_ROPE = 32
MLA_QK = MLA_NOPE + MLA_ROPE
MLA_V = 64
MLA_Q_RANK = 384
MLA_KV_RANK = 256
MLA_IN = MLA_Q_RANK + MLA_KV_RANK + MLA_ROPE
ROPE_THETA = 10000.0
Q_BLOCK = 128

N_GDN_LAYERS = len(range(0, DEPTH, N_MIXERS))
N_MLSTM_LAYERS = len(range(1, DEPTH, N_MIXERS))
N_MLA_LAYERS = len(range(2, DEPTH, N_MIXERS))


def rms_norm(x, w):
    xf = x.astype(jnp.float32)
    y = xf * lax.rsqrt(jnp.mean(xf * xf, axis=-1, keepdims=True) + RMS_EPS)
    return (y * w.astype(jnp.float32)).astype(x.dtype)

def l2_norm(x):
    xf = x.astype(jnp.float32)
    return xf * lax.rsqrt(jnp.sum(xf * xf, axis=-1, keepdims=True) + RMS_EPS)

def to_chunks(x, pad_value=0.0):
    widths = [(0, 0), (LEAD_PAD, 0)] + [(0, 0)] * (x.ndim - 2)
    x = jnp.pad(x, widths, constant_values=pad_value)
    b, tp = x.shape[:2]
    x = x.reshape((b, tp // CHUNK, CHUNK) + x.shape[2:])
    return jnp.moveaxis(x, 3, 1)

def from_chunks(x):
    b, nh, n, c, d = x.shape
    x = jnp.moveaxis(x, 1, 3).reshape(b, n * c, nh, d)
    return x[:, LEAD_PAD:]

def causal_conv_silu(x, w):
    k, c = w.shape
    y = lax.conv_general_dilated(x, w[:, None, :].astype(x.dtype), window_strides=(1,),
                                 padding=[(k - 1, 0)], dimension_numbers=('NWC', 'WIO', 'NWC'),
                                 feature_group_count=c)
    return jax.nn.silu(y)

def chunk_gated_delta_rule(q, k, v, g, beta):
    q, k, v = to_chunks(q), to_chunks(k), to_chunks(v)
    g, beta = to_chunks(g), to_chunks(beta)
    dv = v.shape[-1]
    causal = jnp.tril(jnp.ones((CHUNK, CHUNK), dtype=bool))
    strict = jnp.tril(jnp.ones((CHUNK, CHUNK), dtype=bool), k=-1)
    cum = jnp.cumsum(g, axis=-1)
    decay = jnp.exp(jnp.where(causal, cum[..., :, None] - cum[..., None, :], -jnp.inf))
    k_beta = k * beta[..., None]
    a = jnp.where(strict, jnp.einsum('bhnid,bhnjd->bhnij', k_beta, k) * decay, 0.0)
    eye = jnp.eye(CHUNK, dtype=a.dtype)
    rhs = jnp.concatenate([v * beta[..., None], k_beta * jnp.exp(cum)[..., None]], axis=-1)
    sol = lax.linalg.triangular_solve(a + eye, rhs, left_side=True, lower=True, unit_diagonal=True)
    u, w = sol[..., :dv], sol[..., dv:]
    attn = jnp.einsum('bhnid,bhnjd->bhnij', q, k) * decay
    q_dec = q * jnp.exp(cum)[..., None]
    k_dec = k * jnp.exp(cum[..., -1:] - cum)[..., None]
    last = jnp.exp(cum[..., -1])

    def step(state, xs):
        u_c, w_c, q_c, k_c, attn_c, last_c = xs
        v_new = u_c - jnp.einsum('bhck,bhkv->bhcv', w_c, state)
        o = jnp.einsum('bhck,bhkv->bhcv', q_c, state) + jnp.einsum('bhij,bhjv->bhiv', attn_c, v_new)
        state = state * last_c[..., None, None] + jnp.einsum('bhck,bhcv->bhkv', k_c, v_new)
        return state, o

    xs = tuple(jnp.moveaxis(t, 2, 0) for t in (u, w, q_dec, k_dec, attn, last))
    b, nh = q.shape[:2]
    state0 = jnp.zeros((b, nh, q.shape[-1], dv), jnp.float32)
    _, o = lax.scan(step, state0, xs)
    return from_chunks(jnp.moveaxis(o, 0, 2))

def gated_deltanet(h, w_in, w_conv, a_log, dt_bias, w_norm, w_out):
    b, t, _ = h.shape
    proj = h @ w_in
    qkv, z, beta_pre, a_pre = jnp.split(
        proj, [GDN_CONV_DIM, GDN_CONV_DIM + GDN_V_DIM, GDN_CONV_DIM + GDN_V_DIM + GDN_V_HEADS], axis=-1)
    qkv = causal_conv_silu(qkv, w_conv)
    q, k, v = jnp.split(qkv, [GDN_QK_DIM, 2 * GDN_QK_DIM], axis=-1)
    rep = GDN_V_HEADS // GDN_QK_HEADS
    q = l2_norm(q.reshape(b, t, GDN_QK_HEADS, GDN_HEAD_DIM)) * (GDN_HEAD_DIM ** -0.5)
    k = l2_norm(k.reshape(b, t, GDN_QK_HEADS, GDN_HEAD_DIM))
    q = jnp.repeat(q, rep, axis=2)
    k = jnp.repeat(k, rep, axis=2)
    v = v.reshape(b, t, GDN_V_HEADS, GDN_HEAD_DIM).astype(jnp.float32)
    beta = jax.nn.sigmoid(beta_pre.astype(jnp.float32))
    g = -jnp.exp(a_log.astype(jnp.float32)) * jax.nn.softplus(a_pre.astype(jnp.float32) + dt_bias.astype(jnp.float32))
    o = chunk_gated_delta_rule(q, k, v, g, beta)
    o = rms_norm(o, w_norm) * jax.nn.silu(z.reshape(b, t, GDN_V_HEADS, GDN_HEAD_DIM).astype(jnp.float32))
    return o.reshape(b, t, GDN_V_DIM).astype(h.dtype) @ w_out

def chunk_mlstm(q, k, v, i_pre, log_f):
    q, k, v = to_chunks(q), to_chunks(k), to_chunks(v)
    i_pre = to_chunks(i_pre, -jnp.inf)
    log_f = to_chunks(log_f)
    causal = jnp.tril(jnp.ones((CHUNK, CHUNK), dtype=bool))
    cum = jnp.cumsum(log_f, axis=-1)
    log_w = jnp.where(causal, cum[..., :, None] - cum[..., None, :] + i_pre[..., None, :], -jnp.inf)
    log_w_end = cum[..., -1:] - cum + i_pre
    qk = jnp.einsum('bhnid,bhnjd->bhnij', q, k)

    def step(carry, xs):
        c_mat, n_vec, m = carry
        q_c, k_c, v_c, cum_c, lw_c, lwe_c, qk_c = xs
        log_inter = cum_c + m[..., None]
        m_row = jnp.maximum(log_inter, jnp.max(lw_c, axis=-1))
        s_inter = jnp.exp(log_inter - m_row)
        w_intra = jnp.exp(lw_c - m_row[..., None]) * qk_c
        num = s_inter[..., None] * jnp.einsum('bhck,bhkv->bhcv', q_c, c_mat) \
            + jnp.einsum('bhij,bhjv->bhiv', w_intra, v_c)
        den = s_inter * jnp.einsum('bhck,bhk->bhc', q_c, n_vec) + jnp.sum(w_intra, axis=-1)
        h_c = num / jnp.maximum(jnp.abs(den), jnp.exp(-m_row))[..., None]
        log_keep = cum_c[..., -1] + m
        m_new = jnp.maximum(log_keep, jnp.max(lwe_c, axis=-1))
        s_keep = jnp.exp(log_keep - m_new)
        w_end = jnp.exp(lwe_c - m_new[..., None])
        c_mat = s_keep[..., None, None] * c_mat + jnp.einsum('bhc,bhck,bhcv->bhkv', w_end, k_c, v_c)
        n_vec = s_keep[..., None] * n_vec + jnp.einsum('bhc,bhck->bhk', w_end, k_c)
        return (c_mat, n_vec, m_new), h_c

    xs = tuple(jnp.moveaxis(t, 2, 0) for t in (q, k, v, cum, log_w, log_w_end, qk))
    b, nh, _, _, dk = q.shape
    dv = v.shape[-1]
    carry0 = (jnp.zeros((b, nh, dk, dv), jnp.float32), jnp.zeros((b, nh, dk), jnp.float32),
              jnp.zeros((b, nh), jnp.float32))
    _, hs = lax.scan(step, carry0, xs)
    return from_chunks(jnp.moveaxis(hs, 0, 2))

def mlstm(h, w_in, gate_bias, w_norm, w_out):
    b, t, _ = h.shape
    q, k, v, o, gates = jnp.split(
        h @ w_in, [MLSTM_QK_DIM, 2 * MLSTM_QK_DIM, 2 * MLSTM_QK_DIM + MLSTM_V_DIM,
                   2 * MLSTM_QK_DIM + 2 * MLSTM_V_DIM], axis=-1)
    q = q.reshape(b, t, MLSTM_HEADS, MLSTM_DQK).astype(jnp.float32)
    k = k.reshape(b, t, MLSTM_HEADS, MLSTM_DQK).astype(jnp.float32) * (MLSTM_DQK ** -0.5)
    v = v.reshape(b, t, MLSTM_HEADS, MLSTM_DV).astype(jnp.float32)
    gates = gates.astype(jnp.float32) + gate_bias.astype(jnp.float32)
    gates = GATE_SOFTCAP * jnp.tanh(gates / GATE_SOFTCAP)
    i_pre, f_pre = gates[..., :MLSTM_HEADS], gates[..., MLSTM_HEADS:]
    hs = chunk_mlstm(q, k, v, i_pre, jax.nn.log_sigmoid(f_pre))
    hs = rms_norm(hs, w_norm.reshape(MLSTM_HEADS, MLSTM_DV)) \
        * jax.nn.sigmoid(o.reshape(b, t, MLSTM_HEADS, MLSTM_DV).astype(jnp.float32))
    return hs.reshape(b, t, MLSTM_V_DIM).astype(h.dtype) @ w_out

def rope_tables(t):
    pos = jnp.arange(t, dtype=jnp.float32)
    inv_freq = ROPE_THETA ** (-jnp.arange(0, MLA_ROPE, 2, dtype=jnp.float32) / MLA_ROPE)
    ang = pos[:, None] * inv_freq[None, :]
    return jnp.cos(ang), jnp.sin(ang)

def apply_rope(x, cos, sin):
    x_pass, x_rot = x[..., :MLA_NOPE], x[..., MLA_NOPE:]
    x1, x2 = x_rot[..., :MLA_ROPE // 2], x_rot[..., MLA_ROPE // 2:]
    c = cos[None, :, None, :].astype(x.dtype)
    s = sin[None, :, None, :].astype(x.dtype)
    return jnp.concatenate([x_pass, x1 * c - x2 * s, x2 * c + x1 * s], axis=-1)

def causal_block_attention(q, k, v):
    b, t, nh, dq = q.shape
    dv = v.shape[-1]
    n_blk = -(-t // Q_BLOCK)
    qp = jnp.pad(q, ((0, 0), (0, n_blk * Q_BLOCK - t), (0, 0), (0, 0)))
    scale = dq ** -0.5
    k_pos = jnp.arange(t)

    def one_block(i):
        start = i * Q_BLOCK
        qb = lax.dynamic_slice_in_dim(qp, start, Q_BLOCK, axis=1)
        s = jnp.einsum('bqhd,bkhd->bhqk', qb, k).astype(jnp.float32) * scale
        q_pos = start + jnp.arange(Q_BLOCK)
        s = jnp.where(k_pos[None, :] <= q_pos[:, None], s, -jnp.inf)
        p = jax.nn.softmax(s, axis=-1).astype(v.dtype)
        return jnp.einsum('bhqk,bkhd->bqhd', p, v)

    o = lax.map(one_block, jnp.arange(n_blk))
    return jnp.moveaxis(o, 0, 1).reshape(b, n_blk * Q_BLOCK, nh, dv)[:, :t]

def mla(h, w_in, q_norm, w_uq, kv_norm, w_ukv, q_head_norm, k_head_norm, w_out):
    b, t, _ = h.shape
    c_q, c_kv, k_rope = jnp.split(h @ w_in, [MLA_Q_RANK, MLA_Q_RANK + MLA_KV_RANK], axis=-1)
    q = (rms_norm(c_q, q_norm) @ w_uq).reshape(b, t, MLA_HEADS, MLA_QK)
    kv = (rms_norm(c_kv, kv_norm) @ w_ukv).reshape(b, t, MLA_HEADS, MLA_NOPE + MLA_V)
    k_nope, v = kv[..., :MLA_NOPE], kv[..., MLA_NOPE:]
    k_rope = jnp.broadcast_to(k_rope[:, :, None, :], (b, t, MLA_HEADS, MLA_ROPE))
    k = jnp.concatenate([k_nope, k_rope], axis=-1)
    cos, sin = rope_tables(t)
    q = apply_rope(rms_norm(q, q_head_norm), cos, sin)
    k = apply_rope(rms_norm(k, k_head_norm), cos, sin)
    o = causal_block_attention(q, k, v)
    return o.reshape(b, t, MLA_HEADS * MLA_V) @ w_out

def squared_relu_mlp(h, w_up, w_down):
    a = jax.nn.relu(h @ w_up)
    return (a * a) @ w_down

def first_inputs(seed: int = 0) -> dict:
    key = jax.random.key(seed)
    keys = iter(jax.random.split(key, 40))
    f32 = jnp.float32

    def dense(shape, fan_in):
        return jax.random.normal(next(keys), shape, f32) * (fan_in ** -0.5)

    def gain(shape):
        return 1.0 + 0.02 * jax.random.normal(next(keys), shape, f32)

    x = jax.random.normal(next(keys), (BATCH, SEQ, D_MODEL), f32)
    meta_tokens = jax.random.normal(next(keys), (N_META, D_MODEL), f32)
    attn_norm = gain((DEPTH, D_MODEL))
    ffn_norm = gain((DEPTH, D_MODEL))
    ff_up = dense((DEPTH, D_MODEL, D_FF), D_MODEL)
    ff_down = dense((DEPTH, D_FF, D_MODEL), D_FF)
    gdn_in = dense((N_GDN_LAYERS, D_MODEL, GDN_IN), D_MODEL)
    gdn_conv = dense((N_GDN_LAYERS, GDN_CONV, GDN_CONV_DIM), GDN_CONV)
    gdn_a_log = jnp.log(jax.random.uniform(next(keys), (N_GDN_LAYERS, GDN_V_HEADS), f32, 1.0, 16.0))
    dt = jnp.exp(jax.random.uniform(next(keys), (N_GDN_LAYERS, GDN_V_HEADS), f32,
                                    np.float32(np.log(1e-3)), np.float32(np.log(1e-1))))
    gdn_dt_bias = dt + jnp.log(-jnp.expm1(-dt))
    gdn_norm = gain((N_GDN_LAYERS, GDN_HEAD_DIM))
    gdn_out = dense((N_GDN_LAYERS, GDN_V_DIM, D_MODEL), GDN_V_DIM)
    mlstm_in = dense((N_MLSTM_LAYERS, D_MODEL, MLSTM_IN), D_MODEL)
    ig_bias = 0.1 * jax.random.normal(next(keys), (N_MLSTM_LAYERS, MLSTM_HEADS), f32)
    fg_bias = jnp.linspace(3.0, 6.0, MLSTM_HEADS, dtype=f32)[None, :] \
        + 0.1 * jax.random.normal(next(keys), (N_MLSTM_LAYERS, MLSTM_HEADS), f32)
    mlstm_gate_bias = jnp.concatenate([ig_bias, fg_bias], axis=-1)
    mlstm_norm = gain((N_MLSTM_LAYERS, MLSTM_V_DIM))
    mlstm_out = dense((N_MLSTM_LAYERS, MLSTM_V_DIM, D_MODEL), MLSTM_V_DIM)
    mla_in = dense((N_MLA_LAYERS, D_MODEL, MLA_IN), D_MODEL)
    mla_q_norm = gain((N_MLA_LAYERS, MLA_Q_RANK))
    mla_uq = dense((N_MLA_LAYERS, MLA_Q_RANK, MLA_HEADS * MLA_QK), MLA_Q_RANK)
    mla_kv_norm = gain((N_MLA_LAYERS, MLA_KV_RANK))
    mla_ukv = dense((N_MLA_LAYERS, MLA_KV_RANK, MLA_HEADS * (MLA_NOPE + MLA_V)), MLA_KV_RANK)
    mla_q_head_norm = gain((N_MLA_LAYERS, MLA_QK))
    mla_k_head_norm = gain((N_MLA_LAYERS, MLA_QK))
    mla_out = dense((N_MLA_LAYERS, MLA_HEADS * MLA_V, D_MODEL), MLA_HEADS * MLA_V)
    return {'x': x, 'meta_tokens': meta_tokens, 'attn_norm': attn_norm, 'ffn_norm': ffn_norm,
            'ff_up': ff_up, 'ff_down': ff_down,
            'gdn_in': gdn_in, 'gdn_conv': gdn_conv, 'gdn_a_log': gdn_a_log, 'gdn_dt_bias': gdn_dt_bias,
            'gdn_norm': gdn_norm, 'gdn_out': gdn_out,
            'mlstm_in': mlstm_in, 'mlstm_gate_bias': mlstm_gate_bias, 'mlstm_norm': mlstm_norm,
            'mlstm_out': mlstm_out,
            'mla_in': mla_in, 'mla_q_norm': mla_q_norm, 'mla_uq': mla_uq, 'mla_kv_norm': mla_kv_norm,
            'mla_ukv': mla_ukv, 'mla_q_head_norm': mla_q_head_norm, 'mla_k_head_norm': mla_k_head_norm,
            'mla_out': mla_out}

def first_block(x, meta_tokens, attn_norm, ffn_norm, ff_up, ff_down,
              gdn_in, gdn_conv, gdn_a_log, gdn_dt_bias, gdn_norm, gdn_out,
              mlstm_in, mlstm_gate_bias, mlstm_norm, mlstm_out,
              mla_in, mla_q_norm, mla_uq, mla_kv_norm, mla_ukv, mla_q_head_norm, mla_k_head_norm,
              mla_out):
    b = x.shape[0]
    meta = jnp.broadcast_to(meta_tokens[None].astype(x.dtype), (b, N_META, x.shape[-1]))
    h = jnp.concatenate([meta, x], axis=1)
    for layer in range(DEPTH):
        kind, j = layer % N_MIXERS, layer // N_MIXERS
        hn = rms_norm(h, attn_norm[layer])
        if kind == 0:
            mix = gated_deltanet(hn, gdn_in[j], gdn_conv[j], gdn_a_log[j], gdn_dt_bias[j],
                                 gdn_norm[j], gdn_out[j])
        elif kind == 1:
            mix = mlstm(hn, mlstm_in[j], mlstm_gate_bias[j], mlstm_norm[j], mlstm_out[j])
        else:
            mix = mla(hn, mla_in[j], mla_q_norm[j], mla_uq[j], mla_kv_norm[j], mla_ukv[j],
                      mla_q_head_norm[j], mla_k_head_norm[j], mla_out[j])
        h = h + mix
        h = h + squared_relu_mlp(rms_norm(h, ffn_norm[layer]), ff_up[layer], ff_down[layer])
    return h[:, N_META:]


DEPTH_2 = 1

CTX_LEN = 256
GRID_W = 64

RET_HEADS = 4
RET_DK = 128
RET_DV = 128
RET_CHUNK = 128
RET_W = RET_HEADS * RET_DV
RET_SCALE = RET_DK ** -0.5

ATT_HEADS = 8
ATT_KV_HEADS = 2
ATT_GROUP = ATT_HEADS // ATT_KV_HEADS
ATT_HD = 64
ATT_W = ATT_HEADS * ATT_HD
ATT_SCALE = ATT_HD ** -0.5

MIX_W = RET_W + ATT_W
D_FF_2 = 4 * D_MODEL
ROPE_BASE = 10000.0
EPS = 1e-6

RQ_OFF = 0
RK_OFF = RQ_OFF + RET_HEADS * RET_DK
RV_OFF = RK_OFF + RET_HEADS * RET_DK
RG_OFF = RV_OFF + RET_W
AQ_OFF = RG_OFF + RET_W
AK_OFF = AQ_OFF + ATT_W
AV_OFF = AK_OFF + ATT_KV_HEADS * ATT_HD
D_IN = AV_OFF + ATT_KV_HEADS * ATT_HD
SPLIT_IDX = [RK_OFF, RV_OFF, RG_OFF, AQ_OFF, AK_OFF, AV_OFF]


def _rmsnorm(x, g):
    xf = x.astype(jnp.float32)
    y = xf * lax.rsqrt(jnp.mean(xf * xf, axis=-1, keepdims=True) + EPS)
    return (y * g.astype(jnp.float32)).astype(x.dtype)

def _modulate(h, shift, scale):
    return h * (1 + scale) + shift

def _freqs(n_pairs):
    return ROPE_BASE ** (-jnp.arange(n_pairs, dtype=jnp.float32) / n_pairs)

def _apply_rope(x, cos, sin):
    x1, x2 = jnp.split(x, 2, axis=-1)
    return jnp.concatenate([x1 * cos - x2 * sin, x1 * sin + x2 * cos], axis=-1).astype(x.dtype)

def _heads(t, n_heads):
    B, L, W = t.shape
    return t.reshape(B, L, n_heads, W // n_heads).transpose(0, 2, 1, 3)

def _retention_chunkwise(q, k, v, log_gamma, s0):
    B, H, L, dk = q.shape
    dv = v.shape[-1]
    n_chunks = L // RET_CHUNK

    def chunks(t):
        return jnp.moveaxis(t.reshape(B, H, n_chunks, RET_CHUNK, t.shape[-1]), 2, 0)

    idx = jnp.arange(RET_CHUNK, dtype=jnp.float32)
    lg = log_gamma.astype(jnp.float32)[:, None]
    rel = idx[:, None] - idx[None, :]
    intra = jnp.where(rel >= 0, jnp.exp(lg[:, :, None] * jnp.maximum(rel, 0.0)), 0.0)
    q_dec = jnp.exp(lg * (idx + 1.0))[:, :, None]
    k_dec = jnp.exp(lg * (RET_CHUNK - 1.0 - idx))[:, :, None]
    c_dec = jnp.exp(lg * RET_CHUNK)[:, :, None]

    def step(state, qkv):
        qf, kf, vf = (t.astype(jnp.float32) for t in qkv)
        scores = jnp.einsum('bhid,bhjd->bhij', qf, kf) * intra
        o = (jnp.einsum('bhij,bhjv->bhiv', scores, vf)
             + jnp.einsum('bhid,bhdv->bhiv', qf, state) * q_dec)
        state = state * c_dec + jnp.einsum('bhjd,bhjv->bhdv', kf * k_dec, vf)
        return state, o

    s_fin, o = lax.scan(step, s0, (chunks(q), chunks(k), chunks(v)))
    o = jnp.moveaxis(o, 0, 2).reshape(B, H, L, dv)
    return o, s_fin

def _retention_final_state(k, v, log_gamma):
    L = k.shape[2]
    pos = jnp.arange(L, dtype=jnp.float32)
    w = jnp.exp(log_gamma.astype(jnp.float32)[:, None] * (L - 1.0 - pos))
    return jnp.einsum('bhld,bhlv->bhdv', k.astype(jnp.float32) * w[:, :, None], v.astype(jnp.float32))

def _flip(t):
    return jnp.flip(t, axis=2)

def _bidir_retention(q, k, v, log_gamma, s0_fwd, s0_bwd):
    o_f, s_f = _retention_chunkwise(q, k, v, log_gamma[0], s0_fwd)
    o_b, s_b = _retention_chunkwise(_flip(q), _flip(k), _flip(v), log_gamma[1], s0_bwd)
    return o_f + _flip(o_b), s_f, s_b

def _ret_out(o, gate, gn_g):
    B, H, L, dv = o.shape
    mu = jnp.mean(o, axis=-1, keepdims=True)
    var = jnp.mean(jnp.square(o - mu), axis=-1, keepdims=True)
    o = ((o - mu) * lax.rsqrt(var + EPS)).transpose(0, 2, 1, 3).reshape(B, L, H * dv)
    o = o * gn_g.astype(jnp.float32)
    return (o * jax.nn.silu(gate.astype(jnp.float32))).astype(gate.dtype)

def _dense_attention(q, k, v):
    s = jnp.einsum('bqkgd,bskd->bkgqs', q, k).astype(jnp.float32) * ATT_SCALE
    p = jax.nn.softmax(s, axis=-1).astype(v.dtype)
    return jnp.einsum('bkgqs,bskd->bqkgd', p, v)

def _latent_attention(q, k_lat, v_lat, k_ctx, v_ctx):
    B, L = q.shape[:2]
    k_all = jnp.concatenate([k_ctx, k_lat], axis=1)
    v_all = jnp.concatenate([v_ctx, v_lat], axis=1)
    qb = jnp.moveaxis(q.reshape(B, L // Q_BLOCK, Q_BLOCK, ATT_KV_HEADS, ATT_GROUP, ATT_HD), 1, 0)
    o = lax.map(lambda qblk: _dense_attention(qblk, k_all, v_all), qb)
    return jnp.moveaxis(o, 0, 1).reshape(B, L, ATT_W)

def _sqrelu_mlp(h, w1, w2):
    return jnp.square(jax.nn.relu(h @ w1)) @ w2

def _layer(x, xc, c_act, cc_act, w_mod, b_mod, norm1_g, norm2_g, w_in, w_out,
           ret_log_rate, ret_gn_g, q_norm_g, k_norm_g, w_ff1, w_ff2,
           ret_cs, att_cs, ctx_out):
    B, L, _ = x.shape
    Lc = xc.shape[1]
    mod = (c_act @ w_mod + b_mod)[:, None, :]
    mod_c = (cc_act @ w_mod + b_mod)[None, None, :]
    sh1, sc1, g1, sh2, sc2, g2 = jnp.split(mod, 6, axis=-1)
    csh1, csc1, cg1, csh2, csc2, cg2 = jnp.split(mod_c, 6, axis=-1)
    log_gamma = jnp.log1p(-jnp.exp(ret_log_rate.astype(jnp.float32)))

    h = _modulate(_rmsnorm(x, norm1_g), sh1, sc1)
    hc = _modulate(_rmsnorm(xc, norm1_g), csh1, csc1)
    rq, rk, rv, rg, aq, ak, av = jnp.split(h @ w_in, SPLIT_IDX, axis=-1)
    if ctx_out:
        crq, crk, crv, crg, caq, cak, cav = jnp.split(hc @ w_in, SPLIT_IDX, axis=-1)
    else:
        crk, crv = jnp.split(hc @ w_in[:, RK_OFF:RG_OFF], 2, axis=-1)
        cak, cav = jnp.split(hc @ w_in[:, AK_OFF:D_IN], 2, axis=-1)

    crk_h = _heads(crk, RET_HEADS) * RET_SCALE
    crv_h = _heads(crv, RET_HEADS)
    if ctx_out:
        zeros = jnp.zeros((B, RET_HEADS, RET_DK, RET_DV), jnp.float32)
        ret_c, s_f, s_b = _bidir_retention(_heads(crq, RET_HEADS), crk_h, crv_h, log_gamma, zeros, zeros)
    else:
        s_f = _retention_final_state(crk_h, crv_h, log_gamma[0])
        s_b = _retention_final_state(_flip(crk_h), _flip(crv_h), log_gamma[1])
    rq_h = _apply_rope(_heads(rq, RET_HEADS), *ret_cs)
    rk_h = _apply_rope(_heads(rk, RET_HEADS), *ret_cs) * RET_SCALE
    ret, _, _ = _bidir_retention(rq_h, rk_h, _heads(rv, RET_HEADS), log_gamma, s_f, s_b)
    ret = _ret_out(ret, rg, ret_gn_g)

    q = _apply_rope(_rmsnorm(aq.reshape(B, L, ATT_HEADS, ATT_HD), q_norm_g), *att_cs)
    k = _apply_rope(_rmsnorm(ak.reshape(B, L, ATT_KV_HEADS, ATT_HD), k_norm_g), *att_cs)
    v = av.reshape(B, L, ATT_KV_HEADS, ATT_HD)
    kc = _rmsnorm(cak.reshape(B, Lc, ATT_KV_HEADS, ATT_HD), k_norm_g)
    vc = cav.reshape(B, Lc, ATT_KV_HEADS, ATT_HD)
    att = _latent_attention(q.reshape(B, L, ATT_KV_HEADS, ATT_GROUP, ATT_HD), k, v, kc, vc)

    x = x + g1 * (jnp.concatenate([ret, att], axis=-1) @ w_out)

    h2 = _modulate(_rmsnorm(x, norm2_g), sh2, sc2)
    x = x + g2 * _sqrelu_mlp(h2, w_ff1, w_ff2)

    if ctx_out:
        ret_c = _ret_out(ret_c, crg, ret_gn_g)
        qc = _rmsnorm(caq.reshape(B, Lc, ATT_KV_HEADS, ATT_GROUP, ATT_HD), q_norm_g)
        att_c = _dense_attention(qc, kc, vc).reshape(B, Lc, ATT_W)
        xc = xc + cg1 * (jnp.concatenate([ret_c, att_c], axis=-1) @ w_out)
        hc2 = _modulate(_rmsnorm(xc, norm2_g), csh2, csc2)
        xc = xc + cg2 * _sqrelu_mlp(hc2, w_ff1, w_ff2)
    return x, xc

def second_inputs(seed: int = 0) -> dict:
    key = jax.random.key(seed)
    ks = jax.random.split(key, 17)
    f32 = jnp.float32
    nrm = lambda k, shape, s: jax.random.normal(k, shape, f32) * s
    base_rate = -(5.0 + jnp.arange(RET_HEADS, dtype=f32)) * np.float32(np.log(2.0))
    return {
        "x": nrm(ks[0], (BATCH, SEQ, D_MODEL), 1.0),
        "c": nrm(ks[1], (BATCH, D_MODEL), 1.0),
        "ctx": nrm(ks[2], (BATCH, CTX_LEN, D_MODEL), 1.0),
        "c_ctx": nrm(ks[3], (D_MODEL,), 1.0),
        "w_mod": nrm(ks[4], (DEPTH_2, D_MODEL, 6 * D_MODEL), 0.01),
        "b_mod": nrm(ks[5], (DEPTH_2, 6 * D_MODEL), 0.02),
        "norm1_g": 1.0 + nrm(ks[6], (DEPTH_2, D_MODEL), 0.02),
        "norm2_g": 1.0 + nrm(ks[7], (DEPTH_2, D_MODEL), 0.02),
        "w_in": nrm(ks[8], (DEPTH_2, D_MODEL, D_IN), D_MODEL ** -0.5),
        "w_out": nrm(ks[9], (DEPTH_2, MIX_W, D_MODEL), MIX_W ** -0.5),
        "ret_log_rate": base_rate[None, None, :] + nrm(ks[10], (DEPTH_2, 2, RET_HEADS), 0.05),
        "ret_gn_g": 1.0 + nrm(ks[11], (DEPTH_2, RET_W), 0.02),
        "q_norm_g": 1.0 + nrm(ks[12], (DEPTH_2, ATT_HD), 0.02),
        "k_norm_g": 1.0 + nrm(ks[13], (DEPTH_2, ATT_HD), 0.02),
        "w_ff1": nrm(ks[14], (DEPTH_2, D_MODEL, D_FF_2), D_MODEL ** -0.5),
        "w_ff2": nrm(ks[15], (DEPTH_2, D_FF_2, D_MODEL), D_FF_2 ** -0.5),
        "final_norm_g": 1.0 + nrm(ks[16], (D_MODEL,), 0.02),
    }

def second_block(x, c, ctx, c_ctx, w_mod, b_mod, norm1_g, norm2_g, w_in, w_out,
              ret_log_rate, ret_gn_g, q_norm_g, k_norm_g, w_ff1, w_ff2, final_norm_g):
    L = x.shape[1]
    ROWS = L // GRID_W
    t = jnp.arange(L, dtype=jnp.float32)
    ret_ang = t[:, None] * _freqs(RET_DK // 2)
    ret_cs = (jnp.cos(ret_ang), jnp.sin(ret_ang))
    row = jnp.repeat(jnp.arange(ROWS, dtype=jnp.float32), GRID_W)
    col = jnp.tile(jnp.arange(GRID_W, dtype=jnp.float32), ROWS)
    af = _freqs(ATT_HD // 4)
    att_ang = jnp.concatenate([row[:, None] * af, col[:, None] * af], axis=-1)[:, None, :]
    att_cs = (jnp.cos(att_ang), jnp.sin(att_ang))

    c_act = jax.nn.silu(c)
    cc_act = jax.nn.silu(c_ctx)
    xc = ctx
    for l in range(DEPTH_2):
        x, xc = _layer(x, xc, c_act, cc_act, w_mod[l], b_mod[l], norm1_g[l], norm2_g[l],
                       w_in[l], w_out[l], ret_log_rate[l], ret_gn_g[l], q_norm_g[l], k_norm_g[l],
                       w_ff1[l], w_ff2[l], ret_cs, att_cs, l < DEPTH_2 - 1)
    return _rmsnorm(x, final_norm_g)


def setup_inputs(seed=0):
    out = dict(first_inputs(seed))
    for name, value in second_inputs(seed + 1).items():
        if name != "x":
            out[name + "_2"] = value
    return out


def reference(
    x, meta_tokens, attn_norm, ffn_norm, ff_up, ff_down, gdn_in, gdn_conv, gdn_a_log,
    gdn_dt_bias, gdn_norm, gdn_out, mlstm_in, mlstm_gate_bias, mlstm_norm, mlstm_out, mla_in,
    mla_q_norm, mla_uq, mla_kv_norm, mla_ukv, mla_q_head_norm, mla_k_head_norm, mla_out, c_2,
    ctx_2, c_ctx_2, w_mod_2, b_mod_2, norm1_g_2, norm2_g_2, w_in_2, w_out_2, ret_log_rate_2,
    ret_gn_g_2, q_norm_g_2, k_norm_g_2, w_ff1_2, w_ff2_2, final_norm_g_2,
):
    x = first_block(
        x, meta_tokens, attn_norm, ffn_norm, ff_up, ff_down, gdn_in, gdn_conv, gdn_a_log,
        gdn_dt_bias, gdn_norm, gdn_out, mlstm_in, mlstm_gate_bias, mlstm_norm, mlstm_out,
        mla_in, mla_q_norm, mla_uq, mla_kv_norm, mla_ukv, mla_q_head_norm, mla_k_head_norm,
        mla_out,
    )
    return second_block(
        x, c_2, ctx_2, c_ctx_2, w_mod_2, b_mod_2, norm1_g_2, norm2_g_2, w_in_2, w_out_2,
        ret_log_rate_2, ret_gn_g_2, q_norm_g_2, k_norm_g_2, w_ff1_2, w_ff2_2, final_norm_g_2,
    )


_drawn_inputs = setup_inputs


def setup_inputs(seed=0):
    import zlib

    import numpy as np

    out = dict(_drawn_inputs(seed))
    spreads = {}
    factors = {'gdn_norm': 3.801,
     'mlstm_norm': 8.0,
     'ctx_2': 5.472,
     'c_ctx_2': 8.0,
     'b_mod_2': 3.922,
     'norm1_g_2': 8.0,
     'norm2_g_2': 22.69,
     'ret_log_rate_2': 32.576,
     'ret_gn_g_2': 25.42,
     'q_norm_g_2': 8.0,
     'k_norm_g_2': 8.0,
     'final_norm_g_2': 7.536}
    for name, (base, spread) in spreads.items():
        noise = np.random.default_rng([zlib.crc32(name.encode()), seed]).standard_normal(out[name].shape)
        drawn = base * np.exp(spread * noise) if base else spread * noise
        out[name] = jnp.asarray(drawn.astype(out[name].dtype))
    for name, factor in factors.items():
        out[name] = (out[name] * factor).astype(out[name].dtype)
    return out
```

```python
from contextlib import ExitStack

import numpy as np

import concourse.bass as bass
from concourse import mybir

F32 = mybir.dt.float32
F32R = mybir.dt.float32r
U32 = mybir.dt.uint32
ALU = mybir.AluOpType
ACT = mybir.ActivationFunctionType
AX_X = mybir.AxisListType.X

P = 128
D = 1024
KT = D // P
N_META, SEQ, CTX = 16, 512, 256
T = N_META + SEQ
DFF = 4 * D
EPS = 1e-6

CH = 106
NCH = -(-T // CH)
TP = CH * NCH
LEVELS = 7

GH, GQK = 16, 8
MH, MDK = 8, 64
GATE_CAP = 15.0
RH = 4
AH, AKV, AHD = 8, 2, 64
KEYS = SEQ + CTX

HB_COLS = 256
HB_ELEMS = KT * HB_COLS
N_STAGES = 30
HB_GDN_GATES = 0
HB_GDN_IN = HB_GDN_GATES + 1
N_GDN_IN = 4096 // HB_COLS
HB_GDN_OUT = HB_GDN_IN + N_GDN_IN
HB_MLP0 = HB_GDN_OUT + 16
HB_MLS_GATES = HB_MLP0 + 32
HB_MLS_IN = HB_MLS_GATES + 1
N_MLS_IN = 3072 // HB_COLS
HB_MLS_OUT = HB_MLS_IN + N_MLS_IN
HB_MLP1 = HB_MLS_OUT + 4
HB_B2_IN = HB_MLP1 + 32
N_B2_IN = 2816 // HB_COLS
HB_B2_OUT = HB_B2_IN + N_B2_IN
HB_MLP2 = HB_B2_OUT + 4
N_HB = HB_MLP2 + 32
MOD_GROUPS = 4

PARAMS = {}


def _param(name, n):
    PARAMS[name] = (sum(w for _, w in PARAMS.values()), n)


for _name, _n in [("attn_norm0", 8), ("attn_norm1", 8), ("ffn_norm0", 8), ("ffn_norm1", 8), ("conv", 128),
                  ("gdn_norm", 1), ("mls_norm", 8), ("a_log", 1), ("dt_bias", 1), ("gate_bias", 1),
                  ("norm1_g", 8), ("norm2_g", 8), ("final_g", 8), ("ret_gn", 4), ("qk_norm", 6),
                  ("b_mod", 48), ("ret_rate", 8), ("l2_gain", 16)]:
    _param(_name, _n)
N_PARAMS = sum(w for _, w in PARAMS.values())

SB0 = 16512
SB_RAW = SB0
SB_WHI = SB_RAW + 2 * HB_ELEMS * 4
SB_WLO = SB_WHI + 2 * HB_ELEMS * 4
SB_H = SB_WLO + 2 * HB_ELEMS * 4
SB_CONST = SB_H + KT * T * 4
CONST_BYTES = 5376
SB_XA = SB_CONST + CONST_BYTES
X_BYTES = KT * T * 4
SB_XB = SB_XA + 2 * X_BYTES
SB_G = SB_XB + 2 * X_BYTES
SB_END = 229368


class HalfBlock:

    def __init__(self, first, i=0, step=0):
        assert step % 2 == 0
        self.index = first + i * step if step else first
        self.turn = first // 2 + i * (step // 2) if step else first // 2
        self.slot = first % 2
        self.first, self.fixed = first, step == 0

    def after(self, n):
        out = HalfBlock(self.first + n)
        if not self.fixed:
            out.index, out.turn = self.index + n, self.turn - self.first // 2 + (self.first + n) // 2
            out.fixed = False
        return out

    def exists(self):
        return not self.fixed or self.first < N_HB


def build_program(nc, A, out):
    with ExitStack() as ctx:
        sems = {}

        def S(name):
            if name not in sems:
                sems[name] = ctx.enter_context(nc.semaphore(name))
            return sems[name]

        def at(name, shape, offset, dt=F32):
            assert offset + int(np.prod(shape[1:])) * 4 <= SB_END, (name, offset)
            return nc.alloc_sbuf_tensor_at(name, shape, dt, offset=offset)

        class Region:

            def __init__(self, start, end):
                self.next, self.end = start, end

            def take(self, name, shape, dt=F32):
                t = at(name, shape, self.next, dt)
                self.next += -(-int(np.prod(shape[1:])) * 4 // 32) * 32
                assert self.next <= self.end, (name, self.next - self.end)
                return t

        raw = at("raw", [P, 2, KT, HB_COLS], SB_RAW)
        whi = at("whi", [P, 2, KT, HB_COLS], SB_WHI, F32R)
        wlo = at("wlo", [P, 2, KT, HB_COLS], SB_WLO, F32R)
        h = at("h", [P, KT, T], SB_H)
        con = Region(SB_CONST, SB_XA)
        ident = con.take("ident", [P, P])
        ones = con.take("ones", [P, P])
        par = con.take("par", [P, N_PARAMS])
        rstd = con.take("rstd", [P, T])
        misc = con.take("misc", [P, 8])
        stat = con.take("stat", [P, 8])
        head_stat = con.take("head_stat", [P, 96])
        head_st = [con.take(f"head_st{c}", [P, 8]) for c in range(2)]
        xa_hi = at("xa_hi", [P, KT, T], SB_XA, F32R)
        xa_lo = at("xa_lo", [P, KT, T], SB_XA + X_BYTES, F32R)
        xb_hi = at("xb_hi", [P, KT, T], SB_XB, F32R)
        xb_lo = at("xb_lo", [P, KT, T], SB_XB + X_BYTES, F32R)
        ps = ctx.enter_context(nc.psum_tensor("ps", [P, 8, 512], F32))

        def prm(name, i=None):
            a, n = PARAMS[name]
            return par[:, a:a + n] if i is None else par[:, a + i:a + i + 1]

        def prm_dyn(name, i):
            return par[:, bass.ds(i + PARAMS[name][0], 1)]

        qkv = at("qkv", [P, 32, TP], SB_G)
        conv_r = Region(SB_XB, SB_G)
        conv_in = conv_r.take("conv_in", [P, 2, 3 + T])
        conv_acc = conv_r.take("conv_acc", [P, 2, T])
        l2_sq = conv_r.take("l2_sq", [P, 2, T])
        gt_a = conv_r.take("gt_a", [P, T])
        gt_r2 = conv_r.take("gt_r", [P, T])
        gt_g = conv_r.take("gt_g", [P, TP])
        gt_one = conv_r.take("gt_one", [P, CH])
        gt_e = conv_r.take("gt_e", [P, GH, NCH])
        GATE_BYTES = 5120
        gate_r = Region(SB_G - GATE_BYTES, SB_G)
        g_row = gate_r.take("g_row", [P, TP])
        g_tok = gate_r.take("g_tok", [P, NCH, P])
        g_lastB = gate_r.take("g_lastB", [P, GH, NCH])
        assert conv_r.next <= SB_G - GATE_BYTES
        on_sq = at("on_sq", [P, GH, T], SB_XB)
        at_r = Region(SB_XA, SB_G - GATE_BYTES)
        g_maskU = at_r.take("g_maskU", [P, LEVELS, CH], U32)
        g_neg = at_r.take("g_neg", [P, CH])
        g_kst = at_r.take("g_kst", [P, GQK, CH])
        g_vst = at_r.take("g_vst", [P, GH, CH])
        g_rst = at_r.take("g_rst", [P, CH])
        g_S = at_r.take("g_S", [P, GH, P])
        g_B1, g_AT, g_AN, g_TV, g_U, g_EC, g_VT, g_KD = ([at_r.take(f"g_{n}{x}", [P, 4, w]) for x in range(2)]
                                                        for n, w in (("B1", P), ("AT", CH), ("AN", CH), ("TV", P), ("U", CH),
                                                                     ("EC", CH), ("VT", P), ("KD", P)))
        nt_r = Region(SB_G, SB_END)
        n_sq = nt_r.take("n_sq", [P, KT, T])
        n_y = nt_r.take("n_y", [P, 2, T])
        m_act = nt_r.take("m_act", [P, 2, T])
        m_y = nt_r.take("m_y", [P, 2, T])

        block = ctx.enter_context(nc.Block())

        ENGINES = ("PE", "ACT", "DVE", "POOL")

        class Stages:

            def __init__(self, eng, name):
                self.eng, self.name, self.n = eng, name, 0

            def end(self):
                self.eng.drain().then_inc(S("stage_" + self.name), 1)
                self.n += 1
                for other in ENGINES:
                    if other != self.name:
                        self.eng.wait_ge(S("stage_" + other), self.n)

        FULL = [(0, 0, T // 2), (1, T // 2, T // 2)]
        LATE = [(0, N_META, SEQ)]

        IN_ALL = (3 + 2 + 3 + 2 + 6) * 16
        IN_FIRST = 3 * 16

        def fixed_wait(eng):
            eng.wait_ge(S("in"), IN_FIRST)

        def pair(c, pieces):
            n = pieces[0][2]
            return ps[:, 2 * c:2 * c + len(pieces), 0:n]

        def cols(x, pieces):
            a, n = pieces[0][1], pieces[0][2]
            return x[:, a:a + n * len(pieces)].rearrange("p (a b) -> p a b", b=n)

        def flat(x, pieces):
            a = pieces[0][1]
            return x[:, a:a + pieces[0][2] * len(pieces)]

        def pe_hb(pe, hb, xhi, xlo, pieces, evac, tile, tiles=2, per_k=None, extra=None):
            pe.wait_ge(S("w_lo"), hb.index + 1)
            for c in range(tiles):
                pe.wait_ge(S(evac), tile + c + 1)
                for k in range(KT):
                    if per_k is not None and c == 0:
                        pe.wait_ge(S(per_k[0]), per_k[1] + k + 1)
                    terms = [(whi, xhi), (whi, xlo), (wlo, xhi)]
                    for n, (w, x) in enumerate(terms):
                        for bank, t0, tn in pieces:
                            mm = pe.matmul(ps[:, 2 * c + bank, 0:tn], w[:, hb.slot, k, c * P:(c + 1) * P],
                                           x[:, k, t0:t0 + tn], start=(k == 0 and n == 0), stop=(k == KT - 1 and n == 2))
                        if extra is not None:
                            ehi, elo, en = extra
                            mm = pe.matmul(ps[:, 2 * c + 1, 0:en], w[:, hb.slot, k, c * P:(c + 1) * P],
                                           (elo if n == 1 else ehi)[:, k, 0:en],
                                           start=(k == 0 and n == 0), stop=(k == KT - 1 and n == 2))
                mm.then_inc(S("tiles_done"), 1 if tiles == 2 else 2)

        def act_split(act, hb):
            if not hb.exists():
                return
            act.wait_ge(S(f"w_raw{hb.slot}"), hb.turn * 16 + 16)
            if not (hb.fixed and hb.first < 2):
                act.wait_ge(S("tiles_done"), hb.index * 2 - 2)
            act.activation(whi[:, hb.slot], raw[:, hb.slot], ACT.Copy).then_inc(S("w_hi"), 1)

        def dve_split(dve, hb):
            if not hb.exists():
                return
            dve.wait_ge(S("w_hi"), hb.index + 1)
            dve.tensor_tensor(wlo[:, hb.slot], raw[:, hb.slot], whi[:, hb.slot].bitcast(F32),
                              ALU.subtract).then_inc(S("w_lo"), 1)

        def token_chunks(pieces):
            n = pieces[0][2]
            size = next(n // m for m in range(1, n) if n % m == 0 and n // m <= P)
            return [(bank, a, t0 + a) for bank, t0, tn in pieces for a in range(0, tn, size)], size

        def pe_norm(pe, turn, pieces, sq=n_sq, to=6):
            chunks, size = token_chunks(pieces)
            pe.wait_ge(S("norm_sq"), turn[0] * KT + KT)
            pe.wait_ge(S("norm_acc"), turn[0] * (KT - 2) + KT - 2)
            for n, (_, _, t) in enumerate(chunks):
                for k in (0, KT - 1):
                    mm = pe.matmul(ps[0:size, 4, n:n + 1], sq[:, k, t:t + size], ones[:, 0:1], start=(k == 0), stop=(k != 0))
            mm.then_inc(S("norm_sum"), 1)
            pe.wait_ge(S("norm_rstd"), turn[0] + 1)
            for n, (bank, a, _) in enumerate(chunks):
                mm = pe.matmul(ps[:, to + bank, a:a + size], stat[0:size, n:n + 1].to_broadcast([size, P]), ident[0:size, 0:size],
                               start=True, stop=True)
            mm.then_inc(S("norm_all"), 1)

        def pool_norm(pool, turn, pieces, sq=n_sq):
            for k in range(1, KT - 1):
                pool.wait_ge(S("norm_sq"), turn * KT + k + 1)
                if k > 1:
                    pool.wait_ge(S("norm_acc"), turn * (KT - 2) + k - 1)
                pool.tensor_tensor(flat(sq[:, 0], pieces), flat(sq[:, 0], pieces), flat(sq[:, k], pieces), ALU.add)\
                    .then_inc(S("norm_acc"), 1)

        def act_norm_stats(act, turn, src, pieces, ready=None, sq=n_sq):
            chunks, size = token_chunks(pieces)
            for k in range(KT):
                if ready:
                    act.wait_ge(S(ready[0]), ready[1] + k + 1)
                act.activation(flat(sq[:, k], pieces), flat(src[:, k], pieces), ACT.Square).then_inc(S("norm_sq"), 1)
            act.wait_ge(S("norm_inv"), turn[0] * 2 + 2)
            act.activation(stat[0:size, 0:len(chunks)], stat[0:size, 0:len(chunks)], ACT.Sqrt).then_inc(S("norm_rstd"), 1)

        def act_norm(act, turn, src, pieces, stats=True, dst=None, ready=None, sq=n_sq):
            hi = (dst or (xa_hi, xa_lo))[0]
            if stats:
                act_norm_stats(act, turn, src, pieces, ready, sq)
            for k in range(KT):
                act.wait_ge(S("norm_y"), turn[1] * KT + k + 1)
                act.activation(flat(hi[:, k], pieces), flat(n_y[:, k % 2], pieces), ACT.Copy).then_inc(S("norm_hi"), 1)

        def dve_norm_stats(dve, turn, pieces):
            chunks, size = token_chunks(pieces)
            x = stat[0:size, 0:len(chunks)]
            dve.wait_ge(S("norm_sum"), turn[0] + 1)
            dve.tensor_scalar(x, ps[0:size, 4, 0:len(chunks)], 1.0 / D, EPS, ALU.mult, ALU.add).then_inc(S("norm_inv"), 1)
            dve.wait_ge(S("norm_inv"), turn[0] * 2 + 1)
            dve.reciprocal(x, x).then_inc(S("norm_inv"), 1)
            dve.wait_ge(S("norm_all"), turn[0] + 1)

        def root(pieces, at_=6):
            return ps[:, at_:at_ + len(pieces), 0:pieces[0][2]]

        def dve_norm(dve, turn, src, pieces, gain, shift=None, stats=True, keep=False, dst=None, at_=6):
            hi, lo = dst or (xa_hi, xa_lo)
            if stats:
                dve_norm_stats(dve, turn, pieces)
            r = root(pieces, at_) if stats else cols(rstd, pieces)
            if keep:
                dve.tensor_copy(cols(rstd, pieces), r)

            def low(k):
                dve.wait_ge(S("norm_hi"), turn[1] * KT + k + 1)
                dve.tensor_tensor(flat(lo[:, k], pieces), flat(n_y[:, k % 2], pieces),
                                  flat(hi[:, k], pieces).bitcast(F32), ALU.subtract).then_inc(S("norm_lo"), 1)

            for k in range(KT):
                y = flat(n_y[:, k % 2], pieces)
                if k >= 2:
                    dve.wait_ge(S("norm_lo"), turn[1] * KT + k - 1)
                ins = dve.scalar_tensor_tensor(cols(n_y[:, k % 2], pieces), cols(src[:, k], pieces), gain(k), r, ALU.mult, ALU.mult)
                if shift is not None:
                    ins.then_inc(S("norm_scaled"), 1)
                    dve.wait_ge(S("norm_scaled"), shift[1] * KT + k + 1)
                    ins = dve.tensor_scalar(y, y, shift[0](k), None, ALU.add)
                ins.then_inc(S("norm_y"), 1)
                if k:
                    low(k - 1)
            low(KT - 1)

        def pe_head_sums(pe, base, i, first, sq, buf, pieces, heads=1):
            chunks, size = token_chunks(pieces)
            w = len(chunks) * heads
            pe.wait_ge(S("head_sq"), base)
            for j, (_, _, t) in enumerate(chunks):
                mm = pe.matmul(ps[0:size, 4, bass.ds(i * (2 * w) + (first * w + j * heads), heads)], sq[:, buf, t:t + size],
                               ones[:, 0:1] if heads == 1 else b_half[:, :], start=True, stop=True)
            mm.then_inc(S("head_sums"), 1)

        def pe_headnorm(pe, base, n, sq, pieces, heads=1, bufs=2, sums=True):
            chunks, size = token_chunks(pieces)
            if sums:
                with pe.Fori(0, n // bufs) as i:
                    for c in range(bufs):
                        pe_head_sums(pe, i * bufs + (base + c + 1), i * (bufs // 2), c, sq, c, pieces, heads)
            if base == 0:
                pe.sem_inc(S("head_all"), 2)
            with pe.Fori(0, n // 2) as i:
                for c in range(2):
                    pe.wait_ge(S("head_st"), i * 2 + (base + c + 1))
                    pe.wait_ge(S("head_out"), i * 2 + (base + c + 1))
                    for j, (bank, a, _) in enumerate(chunks):
                        for y in range(heads):
                            rows = slice(y * (P // heads), (y + 1) * (P // heads))
                            mm = pe.matmul(ps[rows, 4 + 2 * c + bank, a:a + size],
                                           head_st[c][0:size, j * heads + y:j * heads + y + 1].to_broadcast([size, P // heads]),
                                           ident[0:size, 0:size], start=True, stop=True)
                    mm.then_inc(S("head_all"), 1)

        def act_head_squares(act, base, n, src, first, sq, pieces, bufs=2):
            with act.Fori(0, n // bufs) as i:
                for c in range(bufs):
                    if bufs != n:
                        fixed_wait(act)
                        act.wait_ge(S("head_sums"), i * bufs + (base + c + 1 - bufs))
                    act.activation(flat(sq[:, c], pieces), flat(src[:, bass.ds(i * bufs + (first + c), 1)].rearrange("p a t -> p (a t)"), pieces),
                                   ACT.Square).then_inc(S("head_sq"), 1)

        def act_headnorm(act, turn, base, n, pieces, heads=1):
            chunks, size = token_chunks(pieces)
            w = len(chunks) * heads
            act.wait_ge(S("head_inv"), 2 * turn + 2)
            act.activation(head_stat[0:size, 0:n * w], head_stat[0:size, 0:n * w], ACT.Sqrt).then_inc(S("head_rstd"), 1)
            act.wait_ge(S("head_rstd"), turn + 1)
            with act.Fori(0, n // 2) as i:
                for c in range(2):
                    fixed_wait(act)
                    act.wait_ge(S("head_all"), i * 2 + (base + c + 1))
                    act.activation(head_st[c][0:size, 0:w], head_stat[0:size, bass.ds(i * (2 * w) + c * w, w)], ACT.Copy)\
                        .then_inc(S("head_st"), 1)

        def dve_headnorm(dve, turn, base, n, src, first, pieces, mean, gain, heads=1):
            chunks, size = token_chunks(pieces)
            x = head_stat[0:size, 0:n * len(chunks) * heads]
            if turn == 0:
                dve.sem_inc(S("head_out"), 2)
            dve.wait_ge(S("head_sums"), base + n)
            dve.tensor_scalar(x, ps[0:size, 4, 0:n * len(chunks) * heads], mean, EPS, ALU.mult, ALU.add).then_inc(S("head_inv"), 1)
            dve.wait_ge(S("head_inv"), 2 * turn + 1)
            dve.reciprocal(x, x).then_inc(S("head_inv"), 1)
            with dve.Fori(0, n // 2) as i:
                for c in range(2):
                    dve.wait_ge(S("head_all"), i * 2 + (base + c + 3))
                    x = cols(src[:, bass.ds(i * 2 + (first + c), 1)].rearrange("p a t -> p (a t)"), pieces)
                    dve.scalar_tensor_tensor(x, x, gain(i * 2 + c), ps[:, 4 + 2 * c:4 + 2 * c + len(pieces), 0:pieces[0][2]],
                                             ALU.mult, ALU.mult).then_inc(S("head_out"), 1)

        def after_group(n):
            return ("two_ev", 16 * n - KT + 2)

        def pe_two_layers(pe, base, first, groups, pieces, norm, peel=False):
            def group(i, hb):
                for j in range(4):
                    pe_hb(pe, hb.after(j), xa_hi, xa_lo, pieces, "two_ev", i * 16 + (16 * base + 2 * j),
                          per_k=("norm_lo", norm * KT) if j == 0 else None)
                for j in range(4):
                    pe_hb(pe, hb.after(4 + j), xb_hi, xb_lo, pieces, "two_ev", i * 16 + (16 * base + 8 + 2 * j),
                          per_k=("two_lo", i * 8 + (8 * base + 2)) if j == 0 else None)
            run_groups(pe, group, first, groups, peel)

        def run_groups(eng, group, first, groups, peel):
            with eng.Fori(0, groups - peel) as i:
                group(i, HalfBlock(first, i, 8))
            if peel:
                group(groups - 1, HalfBlock(first + 8 * (groups - 1)))

        def act_two_layers(act, base, first, groups, pieces, func, peel=False, beside=None):
            def group(i, hb):
                for j in range(4):
                    for c in range(2):
                        t = 2 * j + c
                        act.wait_ge(S("tiles_done"), hb.index * 2 + (t + 1))
                        act.wait_ge(S("two_ev"), i * 16 + (16 * base + t + 1))
                        act.activation(cols(m_act[:, c], pieces), pair(c, pieces), func).then_inc(S("two_act"), 1)
                        act.wait_ge(S("two_ev"), i * 16 + (16 * base + t + 3))
                        act.activation(flat(xb_hi[:, t], pieces), flat(m_y[:, c], pieces), ACT.Copy).then_inc(S("two_hi"), 1)
                    act_split(act, hb.after(j + 2))
                    if beside:
                        beside(act, i, j)
                for j in range(4):
                    act_split(act, hb.after(4 + j + 2))
                    if beside:
                        beside(act, i, 4 + j)
            run_groups(act, group, first, groups, peel)

        def dve_two_layers(dve, base, first, groups, pieces, gate=None, scale=None, peel=False, beside=None):
            if gate:
                dve.wait_ge(S("head_out"), 32 + 2)
            if base == 0:
                dve.sem_inc(S("two_ev"), 2)
                dve.sem_inc(S("two_lo"), 2)

            def group(i, hb):
                for j in range(4):
                    for c in range(2):
                        t = 2 * j + c
                        dve.wait_ge(S("two_act"), i * 8 + (8 * base + t + 1))
                        dve.wait_ge(S("two_lo"), i * 8 + (8 * base + t + 1))
                        other = pair(c, pieces) if gate is None else cols(gate(i, t), pieces)
                        dve.tensor_tensor(cols(m_y[:, c], pieces), cols(m_act[:, c], pieces), other, ALU.mult)\
                            .then_inc(S("two_ev"), 1)
                        dve.wait_ge(S("two_hi"), i * 8 + (8 * base + t + 1))
                        dve.tensor_tensor(flat(xb_lo[:, t], pieces), flat(m_y[:, c], pieces),
                                          flat(xb_hi[:, t], pieces).bitcast(F32), ALU.subtract).then_inc(S("two_lo"), 1)
                    dve_split(dve, hb.after(j + 2))
                    if beside:
                        beside(dve, i, j)
                for j in range(4):
                    dve_down(dve, "two_ev", hb.after(4 + j), j, pieces, scale)
                    if beside:
                        beside(dve, i, 4 + j)
            run_groups(dve, group, first, groups, peel)

        def dve_down(dve, evac, hb, j, pieces, scale=None):
            for c in range(2):
                dve.wait_ge(S("tiles_done"), hb.index * 2 + (c + 1))
                x = cols(h[:, 2 * j + c], pieces)
                if scale is None:
                    ins = dve.tensor_tensor(x, pair(c, pieces), x, ALU.add)
                else:
                    ins = dve.scalar_tensor_tensor(x, pair(c, pieces), scale(2 * j + c), x, ALU.mult, ALU.add)
                ins.then_inc(S(evac), 1)
            dve_split(dve, hb.after(2))

        def chunk_of(x, i):
            return x[:, :, bass.ds(i * CH, CH)]

        def heads4(x, w=CH):
            return x.rearrange("p (a t) -> p a t", a=4)

        HALF_IN = N_GDN_IN // 4

        def gdn_hb(i, s):
            return HalfBlock(HB_GDN_IN, i, 2).after(s) if not isinstance(i, int) else HalfBlock(HB_GDN_IN + 2 * i + s)

        def pe_gdn_in(pe):
            def project(i, s):
                pe_hb(pe, gdn_hb(i, s), xa_hi, xa_lo, FULL, "conv_x", i * 4 + 2 * s)

            def sums(i, s, ahead=0):
                for c in range(2):
                    n = 2 * s + c - ahead
                    pe_head_sums(pe, i * 4 + (n + 1), i * 2, n, l2_sq, c, FULL)

            pe_hb(pe, HalfBlock(HB_GDN_GATES), xa_hi, xa_lo, FULL, "conv_x", 0, tiles=1, per_k=("norm_lo", 0))
            pe.wait_ge(S("gates_a"), 6)
            project(0, 0)
            project(0, 1)
            sums(0, 0)
            with pe.Fori(1, HALF_IN) as i:
                project(i, 0)
                sums(i, 1, ahead=4)
                project(i, 1)
                sums(i, 0)
            project(HALF_IN, 0)
            sums(HALF_IN, 1, ahead=4)
            pe_gdn_gates(pe)
            project(HALF_IN, 1)
            with pe.Fori(HALF_IN + 1, 2 * HALF_IN) as i:
                project(i, 0)
                project(i, 1)

        def act_gdn_in(act):
            act.sem_inc(S("conv_x"), 2)
            act.sem_inc(S("conv_silu"), 2)
            act.wait_ge(S("tiles_done"), 2 * HB_GDN_GATES + 2)
            act_split(act, HalfBlock(HB_GDN_GATES + 2))
            act_gdn_gates(act)

            def convolved(i, s, squares):
                hb = gdn_hb(i, s)
                for c in range(2):
                    act.wait_ge(S("tiles_done"), hb.index * 2 + (c + 1))
                    act.wait_ge(S("conv_out"), i * 4 + (2 * s + c + 1))
                    act.activation(cols(conv_in[:, c, 3:], FULL), pair(c, FULL), ACT.Copy).then_inc(S("conv_x"), 1)
                for c in range(2):
                    fixed_wait(act)
                    act.wait_ge(S("conv_out"), i * 4 + (2 * s + c + 3))
                    act.activation(qkv[:, bass.ds(i * 4 + (2 * s + c), 1), 0:T].rearrange("p a t -> p (a t)"),
                                   conv_acc[:, c, :], ACT.Silu).then_inc(S("conv_silu"), 1)
                if squares and (s or not isinstance(i, int)):
                    act.wait_ge(S("head_sums"), i * 4 + 2 * s)
                act_split(act, hb.after(2))
                if squares:
                    for c in range(2):
                        n = 2 * s + c
                        fixed_wait(act)
                        act.wait_ge(S("conv_silu"), i * 4 + (n + 3))
                        act.activation(l2_sq[:, c, :], qkv[:, bass.ds(i * 4 + n, 1), 0:T].rearrange("p a t -> p (a t)"), ACT.Square)\
                            .then_inc(S("head_sq"), 1)

            for s in range(2):
                convolved(0, s, True)
            with act.Fori(1, HALF_IN) as i:
                for s in range(2):
                    convolved(i, s, True)
            act_gdn_gates_rows(act)
            with act.Fori(HALF_IN, 2 * HALF_IN) as i:
                for s in range(2):
                    convolved(i, s, False)

        def dve_gdn_in(dve):
            dve.sem_inc(S("conv_out"), 2)
            dve_split(dve, HalfBlock(HB_GDN_GATES + 2))
            dve_gdn_gates(dve)
            for first in (0, HALF_IN):
                if first:
                    dve_gdn_gates_tokens(dve)
                with dve.Fori(first, first + HALF_IN) as i:
                    for s in range(2):
                        for c in range(2):
                            dve.wait_ge(S("conv_x"), i * 4 + (2 * s + c + 3))
                            dve.wait_ge(S("conv_silu"), i * 4 + (2 * s + c + 1))
                            for j in range(4):
                                w = prm_dyn("conv", i * 16 + (4 * (2 * s + c) + 3 - j))
                                x = conv_in[:, c, 3 - j:3 - j + T]
                                if j == 0:
                                    ins = dve.tensor_scalar(conv_acc[:, c, :], x, w, None, ALU.mult)
                                else:
                                    dve.wait_ge(S("conv_part"), i * 12 + (3 * (2 * s + c) + j))
                                    ins = dve.scalar_tensor_tensor(conv_acc[:, c, :], x, w, conv_acc[:, c, :], ALU.mult, ALU.add)
                                ins.then_inc(S("conv_out" if j == 3 else "conv_part"), 1)
                        dve_split(dve, gdn_hb(i, s).after(2))

        def by_chunk(x):
            return x.rearrange("p (n t) -> p n t", n=NCH)

        def pool_gdn_gates(pool):
            pool.memset(g_row[:, :], 0.0).then_inc(S("set"), 1)
            pool.memset(gt_g[0:GH, :], 0.0).then_inc(S("set"), 1)
            pool.memset(gt_one[0:GH, :], 1.0).then_inc(S("set"), 1)

        def act_gdn_gates(act):
            a_pre, b_pre = ps[0:GH, 0:2, 0:T // 2], ps[32:32 + GH, 0:2, 0:T // 2]
            dt = prm("dt_bias", 0)[0:GH]
            act.activation(cols(gt_a[0:GH], FULL), a_pre, ACT.Abs, bias=dt).then_inc(S("gates_a"), 1)
            act.wait_ge(S("gates_a"), 1)
            act.activation(gt_a[0:GH, :], gt_a[0:GH, :], ACT.Exp, scale=-1.0).then_inc(S("gates_a"), 1)
            act.wait_ge(S("gates_a"), 2)
            act.activation(gt_a[0:GH, :], gt_a[0:GH, :], ACT.Ln, bias=1.0).then_inc(S("gates_a"), 1)
            act.activation(cols(gt_r2[0:GH], FULL), a_pre, ACT.Relu, bias=dt).then_inc(S("gates_a"), 1)
            act.activation(cols(gt_r2[32:32 + GH], FULL), b_pre, ACT.Sigmoid).then_inc(S("gates_a"), 1)
            act.activation(misc[0:GH, 0:1], prm("a_log", 0)[0:GH], ACT.Exp).then_inc(S("gates_a"), 1)

        def act_gdn_gates_rows(act):
            act.wait_ge(S("gates_d"), 10)
            act.activation(g_row[64:64 + GH, :], g_row[0:GH, :], ACT.Exp).then_inc(S("gates_a"), 1)
            act.activation(g_row[96:96 + GH, :], gt_g[0:GH, :], ACT.Exp).then_inc(S("gates_a"), 1)

        def dve_gdn_gates(dve):
            dve.wait_ge(S("set"), 2 + 3)
            dve.wait_ge(S("gates_a"), 6)
            dve.tensor_scalar(misc[0:GH, 1:2], misc[0:GH, 0:1], -1.0, None, ALU.mult).then_inc(S("gates_d"), 1)
            dve.tensor_tensor(gt_a[0:GH, :], gt_a[0:GH, :], gt_r2[0:GH, :], ALU.add).then_inc(S("gates_d"), 1)
            dve.wait_ge(S("gates_d"), 2)
            dve.tensor_scalar(gt_g[0:GH, 0:T], gt_a[0:GH, :], misc[0:GH, 1:2], None, ALU.mult).then_inc(S("gates_d"), 1)
            dve.wait_ge(S("gates_d"), 3)
            for n in range(NCH):
                t = slice(n * CH, n * CH + CH)
                dve.tensor_tensor_scan(g_row[0:GH, t], gt_one[0:GH, :], gt_g[0:GH, t], 0.0, ALU.mult, ALU.add)\
                    .then_inc(S("gates_d"), 1)
            dve.tensor_scalar(g_row[32:32 + GH, 0:T], gt_r2[32:32 + GH, :], -1.0, None, ALU.mult).then_inc(S("gates_d"), 1)
            dve.wait_ge(S("gates_d"), 8)
            cum = by_chunk(g_row[0:GH, :])
            dve.tensor_tensor(by_chunk(gt_g[0:GH, :]), cum[:, :, CH - 1:CH].to_broadcast([GH, NCH, CH]), cum,
                              ALU.subtract).then_inc(S("gates_d"), 1)

        def dve_gdn_gates_tokens(dve):
            dve.wait_ge(S("gates_a"), 7)
            dve.tensor_tensor(gt_e[64:64 + GH], ident[64:64 + GH, 64:64 + GH, None].to_broadcast([GH, GH, NCH]),
                              by_chunk(g_row[64:64 + GH, :])[:, None, :, CH - 1].to_broadcast([GH, GH, NCH]),
                              ALU.mult).then_inc(S("gates_d"), 1)
            dve.wait_ge(S("gates_p"), 1)
            dve.tensor_copy(g_tok[0:CH, 0:4, :], ps[0:CH, 5, :].rearrange("p (n q) -> p n q", n=4))
            dve.tensor_copy(g_tok[0:CH, 4, :], ps[0:CH, 6, 0:P])
            dve.tensor_copy(g_lastB[:, :, :], ps[:, 7, 0:GH * NCH].rearrange("p (h n) -> p h n", h=GH))

        def act_gdn_masks(act):
            act.dma_start(g_maskU[0:CH], A["mask_u"]).then_inc(S("in"), 16)
            act.dma_start(g_neg[0:CH, :], A["neg"]).then_inc(S("in"), 16)

        def pe_gdn_gates(pe):
            pe.wait_ge(S("gates_a"), 8)
            pe.wait_ge(S("gates_d"), 11)
            for n in range(NCH):
                pe.transpose(ps[0:CH, 5 + n // 4, (n % 4) * P:(n % 4 + 1) * P], g_row[:, n * CH:(n + 1) * CH], ident[:, :])
            pe.matmul(ps[:, 7, 0:GH * NCH], ones[64:64 + GH, :], gt_e[64:64 + GH].rearrange("p h n -> p (h n)"),
                      start=True, stop=True).then_inc(S("gates_p"), 1)

        GROUPS = [(p, x) for p in range(2) for x in range(2)]

        def pe_gdn(pe):
            pe.sem_inc(S("g_Tr"), 1)
            with pe.Fori(0, NCH) as i:
                pe.wait_ge(S("g_kst"), i + 1)
                pe.wait_ge(S("g_rst"), i + 1)
                for p in range(2):
                    gs = [(x, 2 * p + x) for x in range(2)]
                    pe.wait_ge(S("g_state"), i * 4 + 2 * p + 1)
                    pe.wait_ge(S("g_oev"), i * 4 + 2 * p + 1)
                    for x, g in gs:
                        for q in range(4):
                            hd = 4 * g + q
                            mm = pe.matmul(ps[:, 4 * x, q * CH:(q + 1) * CH], ident[0:GH, hd:hd + 1].to_broadcast([GH, P]),
                                           g_rst[0:GH, :], start=True, stop=True)
                        mm.then_inc(S("g_cum"), 1)
                    for x, g in gs:
                        for m in range(2):
                            k = g_kst[:, 2 * g + m, :]
                            pe.matmul(ps[0:CH, 4 * x + 1, m * CH:(m + 1) * CH], k, k, start=True, stop=True)
                            mm = pe.matmul(ps[0:CH, 4 * x + 1, (2 + m) * CH:(3 + m) * CH], k,
                                           qkv[:, 2 * g + m, bass.ds(i * CH, CH)], start=True, stop=True)
                        mm.then_inc(S("g_kq"), 1)
                    for x, g in gs:
                        if x == 0:
                            pe.wait_ge(S("g_vst"), i + 1)
                        for q in range(4):
                            mm = pe.transpose(ps[0:CH, 4 * x + 3, q * P:(q + 1) * P], g_vst[:, 4 * g + q, :], ident[:, :])
                        mm.then_inc(S("g_vT"), 1)
                        for m in range(2):
                            mm = pe.transpose(ps[0:CH, 4 * x + 2, m * P:(m + 1) * P], g_kst[:, 2 * g + m, :], ident[:, :])
                        mm.then_inc(S("g_kT"), 1)
                    def transposed(l):
                        for x, g in gs:
                            if l:
                                pe.wait_ge(S("g_Uup"), i * 24 + (12 * p + 2 * (l - 1) + x + 1))
                            else:
                                pe.wait_ge(S("g_U0"), i * 4 + g + 1)
                            for q in range(4):
                                mm = pe.transpose(ps[0:CH, 4 * x + 1, q * CH:(q + 1) * CH], g_U[x][0:CH, q, :], ident[0:CH, 0:CH])
                            mm.then_inc(S("g_uT"), 1)

                    transposed(0)
                    for l in range(1, LEVELS):
                        for x, g in gs:
                            pe.wait_ge(S("g_T"), i * 24 + (12 * p + 2 * (l - 1) + x + 1))
                            for q in range(4):
                                mm = pe.matmul(ps[0:CH, 4 * x, q * CH:(q + 1) * CH], g_AT[x][0:CH, q, :], g_TV[x][0:CH, q, 0:CH],
                                               start=True, stop=True)
                            mm.then_inc(S("g_P"), 1)
                        for x, g in gs:
                            pe.wait_ge(S("g_Pc"), i * 24 + (12 * p + 2 * (l - 1) + x + 1))
                            if l == 1:
                                pe.wait_ge(S("g_kd"), i * 4 + g + 1)
                            for q in range(4):
                                mm = pe.matmul(ps[0:CH, 4 * x + 2, q * CH:(q + 1) * CH], g_B1[x][0:CH, q, 0:CH],
                                               g_U[x][0:CH, q, :], start=True, stop=True)
                            mm.then_inc(S(f"g_XU{l}"), 1)
                        if l < LEVELS - 1:
                            transposed(l)
                    for x, g in gs:
                        for q in range(4):
                            mm = pe.matmul(ps[0:CH, 4 * x, q * P:(q + 1) * P], g_kst[:, 2 * g + q // 2, :], g_S[:, 4 * g + q, :],
                                           start=True, stop=True)
                        mm.then_inc(S("g_kS"), 1)
                    for x, g in gs:
                        pe.wait_ge(S("g_r"), i * 4 + g + 1)
                        pe.wait_ge(S("g_Uup"), i * 24 + (12 * p + 2 * (LEVELS - 2) + x + 1))
                        for q in range(4):
                            mm = pe.matmul(ps[0:CH, 4 * x + 2, q * P:(q + 1) * P], g_U[x][0:CH, q, :], g_B1[x][0:CH, q, :],
                                           start=True, stop=True)
                        mm.then_inc(S("g_Tr"), 1)
                    for x, g in gs:
                        pe.wait_ge(S("g_vn"), i * 4 + g + 1)
                        pe.wait_ge(S("g_qd"), i * 4 + g + 1)
                        for q in range(4):
                            o = ps[:, 4 * x + 3, q * CH:(q + 1) * CH]
                            pe.matmul(o, g_S[:, 4 * g + q, :], g_EC[x][:, q, :], start=True, stop=False)
                            mm = pe.matmul(o, g_TV[x][0:CH, q, :], g_AN[x][0:CH, q, :], start=False, stop=True)
                        mm.then_inc(S("g_o"), 1)
                        for q in range(4):
                            mm = pe.matmul(ps[:, 4 * x, q * P:(q + 1) * P], g_KD[x][0:CH, q, :], g_TV[x][0:CH, q, :],
                                           start=True, stop=True)
                        mm.then_inc(S("g_inc"), 1)

        def act_gdn(act):
            act.sem_inc(S("g_oev"), 1)
            with act.Fori(0, NCH) as i:
                fixed_wait(act)
                act.wait_ge(S("g_Tr"), i * 4 + 1)
                act.activation(g_vst[:, :, :], chunk_of(qkv[:, 16:32], i), ACT.Copy).then_inc(S("g_vst"), 1)
                for p in range(2):
                    gs = [(x, 2 * p + x) for x in range(2)]
                    act.wait_ge(S("g_state"), i * 4 + 2 * p + 1)
                    for x, g in gs:
                        act.wait_ge(S("g_cum"), i * 4 + g + 1)
                        act.activation(g_EC[x][:, :, :], ps[:, 4 * x, 0:4 * CH].rearrange("p (a t) -> p a t", a=4), ACT.Exp)\
                            .then_inc(S("g_ec"), 1)
                        act.wait_ge(S("g_dif"), i * 4 + g + 1)
                        act.activation(g_B1[x][0:CH, :, 0:CH], g_B1[x][0:CH, :, 0:CH], ACT.Exp).then_inc(S("g_dec"), 1)
                    for x, g in gs:
                        act.wait_ge(S("g_vT"), i * 4 + g + 1)
                        act.activation(g_VT[x][0:CH], ps[0:CH, 4 * x + 3, :].rearrange("p (a t) -> p a t", a=4), ACT.Copy)\
                            .then_inc(S("g_vt"), 1)
                    for l in range(LEVELS - 1):
                        for x, g in gs:
                            act.wait_ge(S("g_uT"), i * 24 + (12 * p + 2 * l + x + 1))
                            act.activation(g_TV[x][0:CH, :, 0:CH], ps[0:CH, 4 * x + 1, 0:4 * CH].rearrange("p (a t) -> p a t", a=4),
                                           ACT.Copy).then_inc(S("g_T"), 1)
                        for x, g in gs:
                            act.wait_ge(S("g_P"), i * 24 + (12 * p + 2 * l + x + 1))
                            act.activation(g_B1[x][0:CH, :, 0:CH], ps[0:CH, 4 * x, 0:4 * CH].rearrange("p (a t) -> p a t", a=4),
                                           ACT.Copy).then_inc(S("g_Pc"), 1)
                    for x, g in gs:
                        fixed_wait(act)
                        act.wait_ge(S("g_o"), i * 4 + g + 1)
                        act.activation(chunk_of(qkv[:, 16 + 4 * g:20 + 4 * g], i),
                                       ps[:, 4 * x + 3, 0:4 * CH].rearrange("p (a t) -> p a t", a=4), ACT.Copy)\
                            .then_inc(S("g_oev"), 1)

        def dve_gdn(dve):
            dve.sem_inc(S("g_state"), 1)
            dve.wait_ge(S("in"), IN_FIRST + 32)

            def tok(i, row, g, w):
                return g_tok[0:CH, bass.ds(i, 1), row + 4 * g:row + 4 * g + 4].rearrange("p n a -> p (n a)")[:, :, None]\
                    .to_broadcast([CH, 4, w])

            def per_pair(x):
                return x.rearrange("p (m t) -> p m t", m=2)[:, :, None, :]

            with dve.Fori(0, NCH) as i:
                for p in range(2):
                    gs = [(x, 2 * p + x) for x in range(2)]
                    for x, g in gs:
                        d = g_B1[x][0:CH, :, 0:CH]
                        dve.wait_ge(S("g_ec"), i * 4 + g + 1)
                        dve.tensor_tensor(d, ps[0:CH, 4 * x, 0:4 * CH].rearrange("p (a t) -> p a t", a=4), tok(i, 0, g, CH),
                                          ALU.subtract).then_inc(S("g_dif0"), 1)
                        dve.wait_ge(S("g_dif0"), i * 4 + g + 1)
                        dve.tensor_tensor(d, d, g_neg[0:CH, None, :].to_broadcast([CH, 4, CH]), ALU.add).then_inc(S("g_dif"), 1)
                    for x, g in gs:
                        dec = g_B1[x][0:CH, :, 0:CH].rearrange("p (m r) t -> p m r t", m=2)
                        dve.wait_ge(S("g_kq"), i * 4 + g + 1)
                        dve.wait_ge(S("g_dec"), i * 4 + g + 1)
                        dve.tensor_tensor(g_AT[x][0:CH].rearrange("p (m r) t -> p m r t", m=2),
                                          per_pair(ps[0:CH, 4 * x + 1, 0:2 * CH]).to_broadcast([CH, 2, 2, CH]), dec, ALU.mult)\
                            .then_inc(S("g_A0"), 1)
                        dve.tensor_copy(g_U[x][0:CH], ident[0:CH, None, 0:CH].to_broadcast([CH, 4, CH]))
                        dve.wait_ge(S("g_A0"), i * 4 + g + 1)
                        dve.tensor_tensor(g_AT[x][0:CH], g_AT[x][0:CH], tok(i, 32, g, CH), ALU.mult).then_inc(S("g_A"), 1)
                        dve.tensor_tensor(g_AN[x][0:CH].rearrange("p (m r) t -> p m r t", m=2),
                                          per_pair(ps[0:CH, 4 * x + 1, 2 * CH:4 * CH]).to_broadcast([CH, 2, 2, CH]), dec, ALU.mult)
                        fixed_wait(dve)
                        dve.wait_ge(S("g_A"), i * 4 + g + 1)
                        dve.copy_predicated(g_U[x][0:CH], g_maskU[0:CH, 0:1, :].to_broadcast([CH, 4, CH]), g_AT[x][0:CH])\
                            .then_inc(S("g_U0"), 1)
                        dve.wait_ge(S("g_kT"), i * 4 + g + 1)
                        dve.tensor_tensor(g_KD[x][0:CH].rearrange("p (m r) t -> p m r t", m=2),
                                          per_pair(ps[0:CH, 4 * x + 2, 0:2 * P]).to_broadcast([CH, 2, 2, P]),
                                          tok(i, 96, g, P).rearrange("p (m r) t -> p m r t", m=2), ALU.mult).then_inc(S("g_kd"), 1)
                    for x, g in gs:
                        dve.wait_ge(S("g_ec"), i * 4 + g + 1)
                        ec = g_EC[x][:, :, :].rearrange("p (m r) t -> p m r t", m=2)
                        dve.tensor_tensor(ec, qkv[:, 2 * g:2 * g + 2, bass.ds(i * CH, CH)][:, :, None, :].to_broadcast([P, 2, 2, CH]),
                                          ec, ALU.mult).then_inc(S("g_qd"), 1)
                    for l in range(1, LEVELS):
                        for x, g in gs:
                            fixed_wait(dve)
                            dve.wait_ge(S(f"g_XU{l}"), i * 4 + g + 1)
                            dve.copy_predicated(g_U[x][0:CH], g_maskU[0:CH, l:l + 1, :].to_broadcast([CH, 4, CH]),
                                                ps[0:CH, 4 * x + 2, 0:4 * CH].rearrange("p (a t) -> p a t", a=4))\
                                .then_inc(S("g_Uup"), 1)
                    for x, g in gs:
                        r = g_B1[x][0:CH]
                        dve.wait_ge(S("g_kS"), i * 4 + g + 1)
                        dve.tensor_tensor(r, ps[0:CH, 4 * x, :].rearrange("p (a t) -> p a t", a=4), tok(i, 64, g, P), ALU.mult)\
                            .then_inc(S("g_r0"), 1)
                        dve.wait_ge(S("g_r0"), i * 4 + g + 1)
                        dve.wait_ge(S("g_vt"), i * 4 + g + 1)
                        dve.tensor_tensor(r, r, g_VT[x][0:CH], ALU.subtract).then_inc(S("g_r"), 1)
                    for x, g in gs:
                        dve.wait_ge(S("g_Tr"), i * 4 + g + 2)
                        dve.tensor_tensor(g_TV[x][0:CH], ps[0:CH, 4 * x + 2, :].rearrange("p (a t) -> p a t", a=4),
                                          tok(i, 32, g, P), ALU.mult).then_inc(S("g_vn"), 1)
                    for x, g in gs:
                        dve.wait_ge(S("g_inc"), i * 4 + g + 1)
                        dve.wait_ge(S("g_sdec"), i * 4 + g + 1)
                        dve.tensor_tensor(g_S[:, 4 * g:4 * g + 4, :], ps[:, 4 * x, :].rearrange("p (a t) -> p a t", a=4),
                                          g_S[:, 4 * g:4 * g + 4, :], ALU.add).then_inc(S("g_state"), 1)

        def pool_gdn(pool):
            with pool.Fori(0, NCH) as i:
                pool.wait_ge(S("g_Tr"), i * 4 + 1)
                pool.tensor_copy(g_kst[:, :, :], chunk_of(qkv[:, 8:16], i)).then_inc(S("g_kst"), 1)
                pool.tensor_copy(g_rst[:, :], g_row[:, bass.ds(i * CH, CH)]).then_inc(S("g_rst"), 1)
                for g in range(4):
                    pool.wait_ge(S("g_o"), i * 4 + g + 1)
                    pool.tensor_tensor(g_S[:, 4 * g:4 * g + 4, :], g_S[:, 4 * g:4 * g + 4, :],
                                       g_lastB[:, 4 * g:4 * g + 4, bass.ds(i, 1)].to_broadcast([P, 4, P]), ALU.mult)\
                        .then_inc(S("g_sdec"), 1)

        ml = at("ml", [P, 24, TP], SB_G)
        mh_sq = at("mh_sq", [P, 8, T], SB_XA)
        mh_y = at("mh_y", [P, 2, T], SB_XA + 8 * T * 4)
        ma_r = Region(SB_XA, SB_XB)
        mg_r = Region(SB_XB, SB_G)
        c_neg = mg_r.take("c_neg", [P, CH])
        c_sel = mg_r.take("c_sel", [P, P + 4])
        c_pair = mg_r.take("c_pair", [P, 4, P])
        c_R1 = mg_r.take("c_R1", [P, TP])
        c_R2 = mg_r.take("c_R2", [P, TP])
        c_tok = mg_r.take("c_tok", [P, NCH, 64])
        c_keep = mg_r.take("c_keep", [P, NCH, 4])
        c_qst = ma_r.take("c_qst", [P, 8, CH])
        c_kst = ma_r.take("c_kst", [P, 4, CH])
        c_vst = ma_r.take("c_vst", [P, 8, CH])
        c_rst = ma_r.take("c_rst", [P, CH])
        c_C = ma_r.take("c_C", [P, 4, 2 * P])
        c_DA = [mg_r.take(f"c_DA{x}", [P, 4, CH]) for x in range(2)]
        c_B1, c_W, c_QS, c_VA, c_KW = ([ma_r.take(f"c_{n}{x}", [P] + w) for x in range(2)]
                                             for n, w in (("B1", [4, CH]), ("W", [4, CH]), ("QS", [4, CH]), ("VA", [4, 2 * P]),
                                                          ("KW", [4, MDK])))
        c_i, c_f, c_ln, c_mn, c_cum, c_M, c_t = (mg_r.take("c_" + n, [P, TP]) for n in ("i", "f", "ln", "mn", "cum", "M", "t"))
        c_one = mg_r.take("c_one", [P, CH])
        c_mp = mg_r.take("c_mp", [P, 8])
        c_kp = mg_r.take("c_kp", [P, NCH])
        c_kd = mg_r.take("c_kd", [P, NCH, 4])

        def pe_mls_in(pe):
            pe_hb(pe, HalfBlock(HB_MLS_GATES), xa_hi, xa_lo, FULL, "in_ev", 0, tiles=1, per_k=("norm_lo", 3 * KT))
            pe.wait_ge(S("gates_a"), GDN_A + 2)
            for first, last in ((0, 2), (2, N_MLS_IN // 2)):
                if first:
                    pe_mls_gates(pe)
                with pe.Fori(first, last) as i:
                    for s in range(2):
                        pe_hb(pe, HalfBlock(HB_MLS_IN, i, 2).after(s), xa_hi, xa_lo, FULL, "in_ev", i * 4 + 2 * s)

        def act_mls_in(act):
            act.sem_inc(S("in_ev"), 2)
            act_mls_consts(act)
            act.wait_ge(S("tiles_done"), 2 * HB_MLS_GATES + 2)
            act_split(act, HalfBlock(HB_MLS_GATES + 2))
            act_mls_gates(act)

            def evacuate(first, loops, func, scale):
                with act.Fori(0, loops) as i:
                    for s in range(2):
                        hb = HalfBlock(HB_MLS_IN + first, i, 2).after(s)
                        for c in range(2):
                            fixed_wait(act)
                            act.wait_ge(S("tiles_done"), hb.index * 2 + (c + 1))
                            dst = ml[:, bass.ds(i * 4 + (2 * first + 2 * s + c), 1), 0:T].rearrange("p a t -> p (a t)")
                            act.activation(cols(dst, FULL), pair(c, FULL), func, scale=scale).then_inc(S("in_ev"), 1)
                        act_split(act, hb.after(2))
            evacuate(0, 1, ACT.Copy, MDK ** -0.5)
            evacuate(2, 1, ACT.Copy, 1.0)
            act_mls_gates_rows(act)
            evacuate(4, 2, ACT.Copy, 1.0)
            evacuate(8, 2, ACT.Sigmoid, 1.0)

        def dve_mls_in(dve):
            dve_split(dve, HalfBlock(HB_MLS_GATES + 2))
            dve_mls_gates(dve)
            for first, last in ((0, 2), (2, N_MLS_IN // 2)):
                if first:
                    dve_mls_gates_tokens(dve)
                with dve.Fori(first, last) as i:
                    for s in range(2):
                        dve_split(dve, HalfBlock(HB_MLS_IN, i, 2).after(s + 2))

        GDN_A, GDN_D, GDN_P = 8, 11, 1

        def pool_mls_gates(pool):
            pool.memset(c_R1[:, :], 0.0).then_inc(S("set"), 1)
            pool.memset(c_R2[:, :], 0.0).then_inc(S("set"), 1)
            pool.memset(c_i[:, :], 0.0).then_inc(S("set"), 1)
            pool.memset(c_ln[:, :], 0.0).then_inc(S("set"), 1)
            pool.memset(c_mn[:, :], 0.0).then_inc(S("set"), 1)
            pool.memset(c_one[:, :], 1.0).then_inc(S("set"), 1)
            pool.memset(c_mp[:, :], 0.0).then_inc(S("set"), 1)

        def pool_mls_state(pool):
            pool.memset(c_C[:, :, :], 0.0)
            pool.memset(c_qst[:, :, :], 0.0)
            for x in range(2):
                pool.memset(c_VA[x][:, :, P:2 * P], 1.0)
            pool.memset(ml[:, :, T:TP], 0.0).then_inc(S("set"), 1)

        def act_mls_consts(act):
            act.dma_start(c_neg[0:CH, :], A["neg"]).then_inc(S("in"), 16)
            act.dma_start(c_sel[0:MH, :], A["mls_sel"]).then_inc(S("in"), 16)
            act.dma_start(c_pair[32:32 + MH], A["mls_pair"]).then_inc(S("in"), 16)

        def act_mls_gates(act):
            act.wait_ge(S("set"), 7 + 7)
            act.wait_ge(S("gates_d"), GDN_D + 1)
            for a in (0, 32):
                act.activation(cols((c_i if a == 0 else c_f)[a:a + MH], FULL), ps[a:a + MH, 0:2, 0:T // 2], ACT.Tanh,
                               bias=misc[a:a + MH, 2:3], scale=1.0 / GATE_CAP).then_inc(S("gates_a"), 1)
            f, ln = c_f[32:40, 0:T], c_ln[32:40, 0:T]
            act.wait_ge(S("gates_a"), GDN_A + 2)
            act.activation(ln, f, ACT.Abs, scale=GATE_CAP).then_inc(S("gates_a"), 1)
            act.wait_ge(S("gates_a"), GDN_A + 3)
            act.activation(ln, ln, ACT.Exp, scale=-1.0).then_inc(S("gates_a"), 1)
            act.wait_ge(S("gates_a"), GDN_A + 4)
            act.activation(ln, ln, ACT.Ln, bias=1.0).then_inc(S("gates_a"), 1)

        def act_mls_gates_rows(act):
            act.wait_ge(S("gates_d"), GDN_D + 26)
            act.activation(c_R1[32:40, :], c_t[0:8, :], ACT.Exp).then_inc(S("gates_a"), 1)
            act.activation(c_R1[64:72, :], c_cum[0:8, :], ACT.Exp, scale=-1.0).then_inc(S("gates_a"), 1)
            act.activation(c_R2[32:40, :], c_f[0:8, :], ACT.Exp).then_inc(S("gates_a"), 1)
            act.activation(c_kp[0:8, :], c_kp[0:8, :], ACT.Exp).then_inc(S("gates_a"), 1)

        def dve_mls_gates(dve):
            dve.tensor_scalar(misc[0:40, 2:3], prm("gate_bias", 0)[0:40], 1.0 / GATE_CAP, None, ALU.mult).then_inc(S("gates_d"), 1)
            dve.wait_ge(S("set"), 7 + 7)
            dve.wait_ge(S("gates_a"), GDN_A + 2)
            dve.tensor_scalar(c_i[0:8, 0:T], c_i[0:8, 0:T], GATE_CAP, None, ALU.mult).then_inc(S("gates_d"), 1)
            dve.tensor_scalar(c_mn[32:40, 0:T], c_f[32:40, 0:T], GATE_CAP, 0.0, ALU.mult, ALU.min).then_inc(S("gates_d"), 1)
            dve.wait_ge(S("gates_a"), GDN_A + 5)
            dve.wait_ge(S("gates_d"), GDN_D + 3)
            dve.tensor_tensor(c_mn[32:40, :], c_mn[32:40, :], c_ln[32:40, :], ALU.subtract).then_inc(S("gates_d"), 1)
            dve.wait_ge(S("gates_d"), GDN_D + 4)
            for n in range(NCH):
                t = slice(n * CH, n * CH + CH)
                dve.tensor_tensor_scan(c_cum[0:8, t], c_one[32:40, :], c_mn[32:40, t], 0.0, ALU.mult, ALU.add)\
                    .then_inc(S("gates_d"), 1)
            dve.wait_ge(S("gates_d"), GDN_D + 9)
            dve.tensor_tensor(c_i[0:8, :], c_i[0:8, :], c_cum[0:8, :], ALU.subtract).then_inc(S("gates_d"), 1)
            for n in range(NCH):
                t = slice(n * CH, n * CH + CH)
                dve.wait_ge(S("gates_d"), GDN_D + 10 + 2 * n)
                dve.tensor_tensor_scan(c_M[0:8, t], c_i[0:8, t], c_i[0:8, t], c_mp[0:8, n:n + 1], ALU.max, ALU.max)\
                    .then_inc(S("gates_d"), 1)
                dve.wait_ge(S("gates_d"), GDN_D + 11 + 2 * n)
                last = (n + 1) * CH - 1
                dve.tensor_tensor(c_mp[0:8, n + 1:n + 2], c_cum[0:8, last:last + 1], c_M[0:8, last:last + 1], ALU.add)\
                    .then_inc(S("gates_d"), 1)
            dve.wait_ge(S("gates_d"), GDN_D + 20)
            top = by_chunk(c_M[0:8, :])[:, :, CH - 1:CH]
            dve.tensor_scalar(c_R1[0:8, :], c_M[0:8, :], -1.0, None, ALU.mult).then_inc(S("gates_d"), 1)
            dve.tensor_tensor(by_chunk(c_t[0:8, :]), c_mp[0:8, 0:NCH, None].to_broadcast([8, NCH, CH]), by_chunk(c_M[0:8, :]),
                              ALU.subtract).then_inc(S("gates_d"), 1)
            dve.tensor_tensor(c_cum[0:8, :], c_cum[0:8, :], c_M[0:8, :], ALU.add).then_inc(S("gates_d"), 1)
            dve.tensor_tensor(by_chunk(c_f[0:8, :]), by_chunk(c_i[0:8, :]), top.to_broadcast([8, NCH, CH]), ALU.subtract)\
                .then_inc(S("gates_d"), 1)
            dve.tensor_tensor(c_kp[0:8, :], c_mp[0:8, 0:NCH], top.rearrange("p n t -> p (n t)"), ALU.subtract).then_inc(S("gates_d"), 1)
            dve.tensor_copy(c_R2[0:8, :], c_i[0:8, :]).then_inc(S("gates_d"), 1)

        def dve_mls_gates_tokens(dve):
            dve.wait_ge(S("gates_a"), GDN_A + 9)
            dve.wait_ge(S("in"), IN_FIRST + 32 + 48)
            dve.tensor_tensor(c_kd[0:8], c_kp[0:8, :, None].to_broadcast([8, NCH, 4]),
                              c_sel[0:8, None, P:P + 4].to_broadcast([8, NCH, 4]), ALU.mult).then_inc(S("gates_d"), 1)
            dve.wait_ge(S("gates_p"), GDN_P + 1)
            dve.tensor_copy(c_tok[0:CH], ps[0:CH, 4, 0:NCH * 64].rearrange("p (n q) -> p n q", n=NCH))
            dve.tensor_copy(c_keep[:, :, :], ps[:, 5, 0:NCH * 4].rearrange("p (n m) -> p n m", n=NCH))

        def pe_mls_gates(pe):
            pe.wait_ge(S("gates_a"), GDN_A + 9)
            pe.wait_ge(S("gates_d"), GDN_D + 27)
            for n in range(NCH):
                pe.transpose(ps[0:CH, 4, n * 64:(n + 1) * 64], c_R2[0:64, n * CH:(n + 1) * CH], ident[0:64, 0:64])
            pe.matmul(ps[:, 5, 0:NCH * 4], c_sel[0:8, 0:P], c_kd[0:8].rearrange("p n m -> p (n m)"),
                      start=True, stop=True).then_inc(S("gates_p"), 1)

        def four(bank, w=CH, rows=P):
            return ps[0:rows, bank, 0:4 * w].rearrange("p (a t) -> p a t", a=4)

        def pe_mls(pe):
            with pe.Fori(0, NCH) as i:
                pe.wait_ge(S("c_st"), i * 4 + 4)
                pe.wait_ge(S("c_state"), i * 2 + 1)
                pe.wait_ge(S("c_hs"), i * 2 + 1)
                for x in range(2):
                    for q in range(4):
                        mm = pe.matmul(ps[0:CH, 4 * x, q * CH:(q + 1) * CH],
                                       ident[0:8, 4 * x + q:4 * x + q + 1].to_broadcast([8, CH]), c_rst[0:8, :], start=True, stop=True)
                    mm.then_inc(S("c_nm"), 1)
                    for m in range(2):
                        mm = pe.matmul(ps[:, 4 * x + 1, m * CH:(m + 1) * CH],
                                       c_pair[32:40, 2 * x + m, :], c_rst[32:40, :], start=True, stop=True)
                    mm.then_inc(S("c_si"), 1)
                    for q in range(4):
                        mm = pe.matmul(ps[0:CH, 4 * x + 3, q * CH:(q + 1) * CH], c_kst[:, 2 * x + q // 2, :],
                                       c_qst[:, 4 * x + q, :], start=True, stop=True)
                    mm.then_inc(S("c_qk"), 1)
                    for q in range(4):
                        mm = pe.matmul(ps[:, 4 * x + 2, q * CH:(q + 1) * CH],
                                       ident[64:72, 64 + 4 * x + q:65 + 4 * x + q].to_broadcast([8, P]), c_rst[64:72, :],
                                       start=True, stop=True)
                    mm.then_inc(S("c_fl"), 1)
                pe.wait_ge(S("c_vst"), i + 1)
                for x in range(2):
                    pe.wait_ge(S("c_qs"), i * 2 + x + 1)
                    for m in range(2):
                        mm = pe.transpose(ps[0:CH, 4 * x + 1, m * P:(m + 1) * P], c_kst[:, 2 * x + m, :], ident[:, :])
                    mm.then_inc(S("c_kT"), 1)
                    pe.wait_ge(S("c_d0"), i * 2 + x + 1)
                    for q in range(4):
                        mm = pe.transpose(ps[0:CH, 4 * x, q * P:(q + 1) * P], c_vst[:, 4 * x + q, :], ident[:, :])
                    mm.then_inc(S("c_vT"), 1)
                for x in range(2):
                    pe.wait_ge(S("c_va"), i * 2 + x + 1)
                    pe.wait_ge(S("c_w"), i * 2 + x + 1)
                    for bank, col, name in ((3, 0, "c_num"), (0, P, "c_den")):
                        for q in range(4):
                            o = ps[:, 4 * x + bank, q * CH:(q + 1) * CH]
                            pe.matmul(o, c_C[:, 2 * x + q // 2, col:col + P], c_QS[x][:, q, :], start=True, stop=False)
                            mm = pe.matmul(o, c_VA[x][0:CH, q, col:col + P], c_W[x][0:CH, q, :], start=False, stop=True)
                        mm.then_inc(S(name), 1)
                    pe.wait_ge(S("c_kw"), i * 2 + x + 1)
                    for q in range(4):
                        y = 64 * (q % 2)
                        mm = pe.matmul(ps[y:y + 64, 4 * x + 1, (q // 2) * 2 * P:(q // 2 + 1) * 2 * P], c_KW[x][0:CH, q, :],
                                       c_VA[x][0:CH, q, :], start=True, stop=True)
                    mm.then_inc(S("c_inc"), 1)

        def act_mls(act):
            with act.Fori(0, NCH) as i:
                fixed_wait(act)
                act.wait_ge(S("c_state"), i * 2 + 1)
                act.activation(c_vst[:, :, :], chunk_of(ml[:, 8:16], i), ACT.Copy).then_inc(S("c_vst"), 1)
                for x in range(2):
                    act.wait_ge(S("c_d"), i * 2 + x + 1)
                    act.activation(c_B1[x][0:CH], c_B1[x][0:CH], ACT.Exp).then_inc(S("c_e"), 1)
                for x in range(2):
                    act.wait_ge(S("c_vT"), i * 2 + x + 1)
                    act.activation(c_VA[x][0:CH, :, 0:P], four(4 * x, P, CH), ACT.Copy).then_inc(S("c_va"), 1)
                for x in range(2):
                    act.wait_ge(S("c_den"), i * 2 + x + 1)
                    act.activation(c_DA[x][:, :, :], four(4 * x), ACT.Abs).then_inc(S("c_da"), 1)

        def dve_mls(dve):
            dve.sem_inc(S("c_state"), 1)
            dve.sem_inc(S("c_hs"), 1)

            def tok(i, row, x, w):
                return c_tok[0:CH, bass.ds(i, 1), row + 4 * x:row + 4 * x + 4].rearrange("p n a -> p (n a)")[:, :, None]\
                    .to_broadcast([CH, 4, w])

            with dve.Fori(0, NCH) as i:
                for x in range(2):
                    n = i * 2 + x + 1
                    dve.wait_ge(S("c_nm"), n)
                    dve.tensor_tensor(c_B1[x][0:CH], four(4 * x, CH, CH), tok(i, 0, x, CH), ALU.add).then_inc(S("c_d0"), 1)
                    dve.wait_ge(S("c_d0"), n)
                    dve.tensor_tensor(c_B1[x][0:CH], c_B1[x][0:CH], c_neg[0:CH, None, :].to_broadcast([CH, 4, CH]), ALU.add)\
                        .then_inc(S("c_d"), 1)
                    dve.wait_ge(S("c_si"), n)
                    dve.tensor_tensor(c_QS[x][:, :, :].rearrange("p (m r) t -> p m r t", m=2),
                                      ps[:, 4 * x + 1, 0:2 * CH].rearrange("p (a t) -> p a t", a=2)[:, :, None, :].to_broadcast([P, 2, 2, CH]),
                                      c_qst[:, 4 * x:4 * x + 4, :].rearrange("p (m r) t -> p m r t", m=2), ALU.mult).then_inc(S("c_qs"), 1)
                for x in range(2):
                    n = i * 2 + x + 1
                    dve.wait_ge(S("c_qk"), n)
                    dve.wait_ge(S("c_e"), n)
                    dve.tensor_tensor(c_W[x][0:CH], four(4 * x + 3, CH, CH), c_B1[x][0:CH], ALU.mult).then_inc(S("c_w"), 1)
                    dve.wait_ge(S("c_kT"), n)
                    dve.tensor_tensor(c_KW[x][0:CH], ps[0:CH, 4 * x + 1, 0:4 * MDK].rearrange("p (a t) -> p a t", a=4),
                                      tok(i, 32, x, MDK), ALU.mult).then_inc(S("c_kw"), 1)
                for x in range(2):
                    n = i * 2 + x + 1
                    dve.wait_ge(S("c_da"), n)
                    dve.wait_ge(S("c_fl"), n)
                    dve.tensor_tensor(c_DA[x][:, :, :], four(4 * x + 2), c_DA[x][:, :, :], ALU.max).then_inc(S("c_mx"), 1)
                    dve.wait_ge(S("c_mx"), n)
                    dve.reciprocal(c_DA[x][:, :, :], c_DA[x][:, :, :]).then_inc(S("c_rc"), 1)
                    dve.wait_ge(S("c_inc"), n)
                    for m in range(2):
                        s = c_C[:, 2 * x + m, :]
                        ins = dve.scalar_tensor_tensor(s, s, c_keep[:, bass.ds(i, 1), 2 * x + m:2 * x + m + 1].rearrange("p n a -> p (n a)"),
                                                       ps[:, 4 * x + 1, m * 2 * P:(m + 1) * 2 * P], ALU.mult, ALU.add)
                    ins.then_inc(S("c_state"), 1)
                    dve.wait_ge(S("c_rc"), n)
                    dve.tensor_tensor(chunk_of(ml[:, 8 + 4 * x:12 + 4 * x], i), four(4 * x + 3), c_DA[x][:, :, :], ALU.mult)\
                        .then_inc(S("c_hs"), 1)

        def pool_mls(pool):
            with pool.Fori(0, NCH) as i:
                pool.wait_ge(S("c_state"), i * 2 + 1)
                pool.tensor_copy(c_kst[:, :, :], chunk_of(ml[:, 4:8], i)).then_inc(S("c_st"), 1)
                pool.tensor_copy(c_rst[:, :], c_R1[:, bass.ds(i * CH, CH)]).then_inc(S("c_st"), 1)
                pool.wait_ge(S("c_st"), i * 4 + 2)
                for y in range(2):
                    half = slice(64 * y, 64 * y + 64)
                    pool.tensor_copy(c_qst[half].rearrange("p (m r) t -> p m r t", m=4)[:, :, y, :], chunk_of(ml[half, 0:4], i))\
                        .then_inc(S("c_st"), 1)

        def act_mls_out(act):
            for t in range(8):
                act.wait_ge(S("gated_y"), t + 1)
                act.activation(flat(xb_hi[:, t], LATE), flat(mh_y[:, t % 2], LATE), ACT.Copy).then_inc(S("gated_hi"), 1)
            act_mod(act)
            for j in range(4):
                act_split(act, HalfBlock(HB_MLS_OUT + j + 2))

        def dve_mls_out(dve):
            dve.sem_inc(S("out_ev"), 2)
            dve.wait_ge(S("head_out"), 40 + 2)
            for t in range(8):
                if t >= 2:
                    dve.wait_ge(S("gated_lo"), t - 1)
                dve.tensor_tensor(flat(mh_y[:, t % 2], LATE), ml[:, 8 + t, N_META:T], ml[:, 16 + t, N_META:T], ALU.mult)\
                    .then_inc(S("gated_y"), 1)
                dve.wait_ge(S("gated_hi"), t + 1)
                dve.tensor_tensor(flat(xb_lo[:, t], LATE), flat(mh_y[:, t % 2], LATE), flat(xb_hi[:, t], LATE).bitcast(F32),
                                  ALU.subtract).then_inc(S("gated_lo"), 1)
            for j in range(4):
                dve_down(dve, "out_ev", HalfBlock(HB_MLS_OUT + j), j, LATE)

        def pe_mls_out(pe):
            for j in range(4):
                pe_hb(pe, HalfBlock(HB_MLS_OUT + j), xb_hi, xb_lo, LATE, "out_ev", 2 * j, per_k=("gated_lo", 0) if j == 0 else None)

        TOK = [(0, 0, SEQ)]
        CTXP = [(0, 0, CTX)]
        b2_r = Region(SB_G, SB_END)
        b_rope = b2_r.take("b_rope", [P, 4, SEQ])
        b2_r = Region(SB_G + 4 * 2 * T * 2, SB_END)
        b_q = b2_r.take("b_q", [P, RH, SEQ])
        b_kv = b2_r.take("b_kv", [P, RH, 2 * KEYS])
        b_g = b2_r.take("b_g", [P, RH, SEQ])
        b_qk = b2_r.take("b_qk", [P, 6, SEQ])
        b_av = b2_r.take("b_av", [P, KEYS])
        b_ctx_at = b2_r.next
        b_ctx = b2_r.take("b_ctx", [P, KT, CTX])
        b_mod = b2_r.take("b_mod", [P, MOD_GROUPS, 12])
        b_modc = b2_r.take("b_modc", [P, MOD_GROUPS, 4])
        mod_r = b2_r.take("mod_r", [P, 16])
        b_gain = b2_r.take("b_gain", [P, 3, KT])
        bc_r = Region(b_ctx_at, b_ctx_at + KT * CTX * 4)
        b_pos = bc_r.take("b_pos", [P, 2, SEQ])
        b_lpos = bc_r.take("b_lpos", [P, 2, 2])
        b_dec = bc_r.take("b_dec", [P, 2, RH, 2])
        b_lg = bc_r.take("b_lg", [P, 2 * RH])
        b_e, b_s, b_big = (bc_r.take("b_" + n, [P, 2 * RH]) for n in ("e", "s", "big"))
        b_half = bc_r.take("b_half", [P, 2])
        md_r = Region(SB_G + (KT + 6) * T * 4, SB_END)
        mod_w = md_r.take("mod_w", [P, 3, 2, D])
        mod_c = md_r.take("mod_c", [P, 2, D])
        mod_x = at("mod_x", [P, 2, D], SB_G)
        assert md_r.next <= b_ctx_at
        ctx_sq = at("ctx_sq", [P, KT, CTX], SB_G + (KT + 6) * T * 4)
        bc_hi = at("bc_hi", [P, KT, CTX], SB_XB, F32R)
        bc_lo = at("bc_lo", [P, KT, CTX], SB_XB + KT * CTX * 4, F32R)
        bt_r = Region(SB_XB + 2 * KT * CTX * 4, SB_G)
        b_tau = bt_r.take("b_tau", [P, 2, SEQ + 3 * P])
        b_perm = bt_r.take("b_perm", [P, 2, P])
        r_qd = [[bt_r.take(f"r_qd{x}{d}", [P, SEQ]) for d in range(2)] for x in range(2)]
        r_w = [at(f"r_w{x}", [P, 4, SEQ], SB_XB + x * 4 * SEQ * 4) for x in range(2)]
        rt_r = Region(SB_XA, SB_XB)
        r_st, r_tt, r_vT, r_ck, r_cv, r_S = ([rt_r.take(f"r_{n}{x}", [P] + w) for x in range(2)]
                                             for n, w in (("st", [2 * KEYS]), ("tt", [SEQ + 3 * P]), ("vT", [4, P]), ("ck", [2, 2, P]),
                                                          ("cv", [2, P]), ("S", [2, P])))
        rr_r = Region(SB_XA, SB_XB)
        rope_c = rr_r.take("rope_c", [P, 2, SEQ])
        rope_s = rr_r.take("rope_s", [P, 2, SEQ])
        hn_sq = rr_r.take("hn_sq", [P, 6, T])
        hn_y = rr_r.take("hn_y", [P, 2, T])
        aa_r = Region(SB_XA, SB_XB)
        a_kd = aa_r.take("a_kd", [P, AKV, KEYS])
        a_vt = aa_r.take("a_vt", [P, KEYS // P, P])
        a_qst = [aa_r.take(f"a_qst{y}", [P, SEQ]) for y in range(2)]
        a_vst = aa_r.take("a_vst", [P, KEYS // P, AHD])
        a_p = [aa_r.take(f"a_p{c}", [P, KEYS]) for c in range(2)]
        a_mx, a_nm, a_sum, a_inv = ([aa_r.take(f"a_{n}{c}", [P, 1]) for c in range(2)] for n in ("mx", "nm", "sum", "inv"))
        a_pT = [at(f"a_pT{y}", [P, KEYS // P, SEQ], SB_G + 4 * 2 * T * 2 + RH * SEQ * 4 + y * KEYS // P * SEQ * 4) for y in range(2)]

        MOD_SUMS = 16
        MOD_LOADS = 6

        def act_mod(act):
            act.dma_start(b_ctx[:, :, :], A["ctx_in"]).then_inc(S("in"), 16)
            act.dma_start(mod_c[:, :, :], A["c_in"]).then_inc(S("in"), 16)

        def act_mod_c(act):
            act.wait_ge(S("in"), IN_FIRST + 32 + 48 + 32)
            act.activation(mod_c[:, :, :], mod_c[:, :, :], ACT.Silu).then_inc(S("mod_c"), 1)

        def mod_sums_before(m):
            return 4 * m if m < 2 else 2 * m + 4

        def act_mod_load(act, i, j):
            if j < MOD_LOADS:
                if j >= 3:
                    act.wait_ge(S("mod_sum"), i * MOD_SUMS + (mod_sums_before(j - 2) + 4))
                else:
                    act.wait_ge(S("mod_sum"), i * MOD_SUMS + (mod_sums_before(j + 4) - MOD_SUMS + 4))
                act.dma_start(mod_w[:, j % 3].rearrange("p a n -> p (a n)"),
                              A["weights_mod"][bass.ds(i * MOD_LOADS + j, 1), :, :].rearrange("a p n -> (a p) n"))\
                    .then_inc(S(f"mod_w{j % 3}"), 16)

        def dve_mod_start(dve):
            dve.sem_inc(S("mod_sum"), 4)
            dve.wait_ge(S("mod_c"), 1)

        def dve_mod_sums(dve, i, j):
            m = j // 2 if j < 4 else j - 2
            if j >= 4 or j % 2 == 0:
                dve.wait_ge(S(f"mod_w{m % 3}"), i * 32 + 16 * (m // 3 + 1))
            for x in range(2):
                c, who = (j % 2, x) if j < 4 else (x, 0)
                n = 2 * j + x
                to = 12 + 2 * m + c if who else 2 * m + c
                dve.wait_ge(S("mod_sum"), i * MOD_SUMS + (n + 3))
                dve.scalar_tensor_tensor(mod_x[:, n % 2] if j < 4 else mod_w[:, m % 3, c], mod_w[:, m % 3, c], 1.0, mod_c[:, who], ALU.mult, ALU.mult,
                                         accum_out=mod_r[:, to:to + 1]).then_inc(S("mod_sum"), 1)
            if j == 7:
                dve.wait_ge(S("mod_sum"), i * MOD_SUMS + (MOD_SUMS + 4))
                bias = prm("b_mod").rearrange("p (g n) -> p g n", g=MOD_GROUPS)[:, bass.ds(i, 1), :].rearrange("p a n -> p (a n)")
                dve.tensor_tensor(b_mod[:, bass.ds(i, 1), :].rearrange("p a n -> p (a n)"), mod_r[:, 0:12], bias, ALU.add)\
                    .then_inc(S("mod_d"), 1)
                dve.tensor_tensor(b_modc[:, bass.ds(i, 1), :].rearrange("p a n -> p (a n)"), mod_r[:, 12:16], bias[:, 0:4], ALU.add)\
                    .then_inc(S("mod_d"), 1)

        def mod_tiles(what):
            if what in ("shift1", "scale1"):
                g = 0 if what == "shift1" else 2
                return b_mod[:, g:g + 2, 0:4]
            return b_mod[:, ["gate1", "shift2", "scale2", "gate2"].index(what), None, 4:12]

        def mod_col(what, k):
            x = mod_tiles(what)
            w = x.shape[2]
            return x[:, k // w, k % w:k % w + 1]

        def ctx_shift(k):
            return b_modc[:, k // 4, k % 4:k % 4 + 1]

        def gain_col(n, k):
            return b_gain[:, n, k:k + 1]

        def dve_mod(dve):
            dve.wait_ge(S("mod_d"), 2 * MOD_GROUPS)
            for n, (scale, g) in enumerate(((mod_tiles("scale1"), "norm1_g"), (b_modc[:, 2:4, :], "norm1_g"), (mod_tiles("scale2"), "norm2_g"))):
                w = scale.shape[2]
                dve.scalar_tensor_tensor(b_gain[:, n, :].rearrange("p (a b) -> p a b", b=w), scale, 1.0,
                                         prm(g).rearrange("p (a b) -> p a b", b=w), ALU.add, ALU.mult).then_inc(S("mod_d"), 1)
            dve.wait_ge(S("mod_d"), 2 * MOD_GROUPS + 3)

        N_IN_BEFORE = 2 * N_MLS_IN

        def pe_b2_in(pe):
            ctx_of = (bc_hi, bc_lo, CTX)
            pe_hb(pe, HalfBlock(HB_B2_IN), xa_hi, xa_lo, LATE, "in_ev", N_IN_BEFORE, per_k=("norm_lo", 5 * KT))
            pe_norm(pe, (5, 6), CTXP, sq=ctx_sq, to=5)
            pe_hb(pe, HalfBlock(HB_B2_IN + 1), xa_hi, xa_lo, LATE, "in_ev", N_IN_BEFORE + 2)
            pe.wait_ge(S("norm_lo"), 7 * KT)
            with pe.Fori(0, 2) as i:
                for s in range(2):
                    pe_hb(pe, HalfBlock(HB_B2_IN + 2, i, 2).after(s), xa_hi, xa_lo, LATE, "in_ev", i * 4 + (N_IN_BEFORE + 4 + 2 * s), extra=ctx_of)
            with pe.Fori(0, 2) as i:
                for s in range(2):
                    pe_hb(pe, HalfBlock(HB_B2_IN + 6, i, 2).after(s), xa_hi, xa_lo, LATE, "in_ev", i * 4 + (N_IN_BEFORE + 12 + 2 * s))
            pe_hb(pe, HalfBlock(HB_B2_IN + 10), xa_hi, xa_lo, LATE, "in_ev", N_IN_BEFORE + 20, extra=ctx_of)

        def act_b2_in(act):
            for n, (to, name) in enumerate(((b_rope, "rope"), (b_tau, "tau"), (b_perm, "perm"), (b_pos, "pos"),
                                            (b_lpos, "lpos"), (b_half, "half"))):
                act.dma_start(to[:, :, :] if len(to.shape) == 3 else to[:, :], A[name]).then_inc(S("in"), 16)
            for t in range(2 * N_B2_IN):
                n, func, scale, ctx_to = t % 4, ACT.Copy, 1.0, None
                if t < 4:
                    to, scale = b_q[:, n, :], P ** -0.5
                elif t < 8:
                    to, ctx_to = b_kv[:, n, 0:SEQ], b_kv[:, n, 2 * SEQ:2 * SEQ + CTX]
                elif t < 12:
                    to, ctx_to = b_kv[:, n, SEQ:2 * SEQ], b_kv[:, n, 2 * SEQ + CTX:2 * KEYS]
                elif t < 16:
                    to, func = b_g[:, n, :], ACT.Silu
                elif t < 20:
                    to = b_qk[:, n, :]
                elif t == 20:
                    to, ctx_to = b_qk[:, 4, :], b_qk[:, 5, 0:CTX]
                else:
                    to, ctx_to = b_av[:, CTX:KEYS], b_av[:, 0:CTX]
                act.wait_ge(S("tiles_done"), (HB_B2_IN * 2 + t + 1))
                if ctx_to is not None:
                    act.activation(ctx_to, ps[:, 2 * (t % 2) + 1, 0:CTX], ACT.Copy)
                act.activation(to, ps[:, 2 * (t % 2), :], func, scale=scale).then_inc(S("in_ev"), 1)
                if t % 2:
                    act_split(act, HalfBlock(HB_B2_IN + t // 2 + 2))

        def dve_b2_in(dve):
            for j in range(N_B2_IN):
                dve_split(dve, HalfBlock(HB_B2_IN + j + 2))

        def pool_b2_in(pool):
            pool.memset(b_qk[:, 5, CTX:SEQ], 0.0)

        MLS_A, MLS_D = GDN_A + 9, GDN_D + 27

        def act_decays(act):
            act.wait_ge(S("in"), IN_ALL)
            act.activation(b_e[:, :], prm("ret_rate"), ACT.Exp).then_inc(S("gates_a"), 1)
            act.wait_ge(S("gates_a"), MLS_A + 1)
            act.activation(b_lg[:, :], b_e[:, :], ACT.Ln, bias=1.0, scale=-1.0).then_inc(S("gates_a"), 1)
            act.wait_ge(S("gates_d"), MLS_D + N_SERIES + 6)
            act.activation(b_dec[:, :, :, :], b_dec[:, :, :, :], ACT.Exp).then_inc(S("gates_a"), 1)

        N_SERIES = 8

        def dve_decays(dve):
            dve.wait_ge(S("in"), IN_ALL)
            dve.wait_ge(S("gates_a"), MLS_A + 2)
            dve.tensor_scalar(b_big[:, :], b_e[:, :], 0.0625, None, ALU.is_ge).then_inc(S("gates_d"), 1)
            dve.tensor_scalar(b_s[:, :], b_e[:, :], 1.0 / N_SERIES, None, ALU.mult).then_inc(S("gates_d"), 1)
            for n in range(N_SERIES - 1, 0, -1):
                dve.wait_ge(S("gates_d"), MLS_D + N_SERIES - n + 1)
                dve.scalar_tensor_tensor(b_s[:, :], b_s[:, :], 1.0 / n, b_e[:, :], ALU.add, ALU.mult).then_inc(S("gates_d"), 1)
            dve.wait_ge(S("gates_d"), MLS_D + N_SERIES + 1)
            dve.tensor_tensor(b_lg[:, :], b_lg[:, :], b_s[:, :], ALU.add).then_inc(S("gates_d"), 1)
            dve.wait_ge(S("gates_d"), MLS_D + N_SERIES + 2)
            dve.tensor_tensor(b_lg[:, :], b_lg[:, :], b_big[:, :], ALU.mult).then_inc(S("gates_d"), 1)
            dve.wait_ge(S("gates_d"), MLS_D + N_SERIES + 3)
            dve.tensor_tensor(b_lg[:, :], b_lg[:, :], b_s[:, :], ALU.subtract).then_inc(S("gates_d"), 1)
            dve.wait_ge(S("gates_d"), MLS_D + N_SERIES + 4)
            for d in range(2):
                dve.tensor_tensor(b_dec[:, d], b_lg[:, d * RH:(d + 1) * RH, None].to_broadcast([P, RH, 2]),
                                  b_lpos[:, d, None, :].to_broadcast([P, RH, 2]), ALU.mult).then_inc(S("gates_d"), 1)

        ROPES = [(b_q[:, t, :], 0) for t in range(RH)] + [(b_kv[:, t, 0:SEQ], 0) for t in range(RH)] + \
                [(b_qk[:, t, :], 1) for t in range(5)]

        def pe_rope(pe):
            for t, (x, kind) in enumerate(ROPES):
                if t >= 4:
                    pe.wait_ge(S("rope_s"), t - 3)
                pe.matmul(ps[:, t % 4, :], b_perm[:, kind, :], x, start=True, stop=True).then_inc(S("rope_x"), 1)

        def pool_rope(pool):
            for t, (x, kind) in enumerate(ROPES):
                if t >= 2:
                    pool.wait_ge(S("rope_o"), t - 1)
                pool.tensor_tensor(rope_c[:, t % 2], x, b_rope[:, 2 * kind], ALU.mult).then_inc(S("rope_c"), 1)

        def dve_rope(dve):
            for t, (x, kind) in enumerate(ROPES):
                dve.wait_ge(S("rope_x"), t + 1)
                if t >= 2:
                    dve.wait_ge(S("rope_o"), t - 1)
                dve.tensor_tensor(rope_s[:, t % 2], ps[:, t % 4, :], b_rope[:, 2 * kind + 1], ALU.mult).then_inc(S("rope_s"), 1)
                dve.wait_ge(S("rope_s"), t + 1)
                dve.wait_ge(S("rope_c"), t + 1)
                dve.tensor_tensor(x, rope_c[:, t % 2], rope_s[:, t % 2], ALU.add).then_inc(S("rope_o"), 1)

        def pool_ret(pool):
            with pool.Fori(0, RH // 2) as i:
                for x in range(2):
                    hd = i * 2 + x
                    pool.wait_ge(S("r_o"), i * 2 + (x + 1))
                    pool.tensor_copy(r_st[x][:, :], b_kv[:, bass.ds(hd, 1), :].rearrange("p a t -> p (a t)")).then_inc(S("r_st"), 1)
                for x in range(2):
                    q = b_q[:, bass.ds(i * 2 + x, 1), :].rearrange("p a t -> p (a t)")
                    pool.wait_ge(S("r_qe"), i * 4 + (2 * x + 2))
                    pool.sem_inc(S("pool_steps"), 1)
                    for d in range(2):
                        pool.tensor_tensor(r_qd[x][d][:, :], r_qd[x][d][:, :], q, ALU.mult).then_inc(S("r_qd"), 1)

        def act_ret(act):
            act.sem_inc(S("r_out"), 2)
            with act.Fori(0, RH // 2) as i:
                for x in range(2):
                    act.wait_ge(S("r_o"), i * 2 + (x + 1))
                    for d in range(2):
                        act.activation(r_qd[x][d][:, :], b_pos[:, d, :], ACT.Exp, scale=b_lg[:, bass.ds(i * 2 + (RH * d + x), 1)])\
                            .then_inc(S("r_qe"), 1)
                    act.wait_ge(S("r_t"), i * 2 + (x + 1))
                    act.activation(r_tt[x][:, :], r_tt[x][:, :], ACT.Exp).then_inc(S("r_te"), 1)
                for x in range(2):
                    act.wait_ge(S("r_vT"), i * 2 + (x + 1))
                    act.activation(r_vT[x][:, :, :], ps[:, 4 * x, :].rearrange("p (a t) -> p a t", a=4), ACT.Copy).then_inc(S("r_v"), 1)
                for x in range(2):
                    act.wait_ge(S("r_sd"), i * 2 + (x + 1))
                    act.activation(r_S[x][:, :, :], ps[:, 4 * x, 0:2 * P].rearrange("p (a t) -> p a t", a=2), ACT.Copy).then_inc(S("r_S"), 1)
                for x in range(2):
                    fixed_wait(act)
                    act.wait_ge(S("r_o"), i * 2 + (x + 3))
                    act.activation(b_q[:, bass.ds(i * 2 + x, 1), :].rearrange("p a t -> p (a t)"), ps[:, 4 * x + 1, :], ACT.Copy)\
                        .then_inc(S("r_out"), 1)

        def dve_ret(dve):
            with dve.Fori(0, RH // 2) as i:
                for x in range(2):
                    lg = [b_lg[:, bass.ds(i * 2 + (RH * d + x), 1)] for d in range(2)]
                    dve.wait_ge(S("r_o"), i * 2 + (x + 1))
                    dve.tensor_scalar(r_tt[x][:, :], b_tau[:, 0, :], lg[0], None, ALU.mult).then_inc(S("r_t0"), 1)
                    dve.wait_ge(S("r_t0"), i * 2 + (x + 1))
                    dve.scalar_tensor_tensor(r_tt[x][:, :], b_tau[:, 1, :], lg[1], r_tt[x][:, :], ALU.mult, ALU.add).then_inc(S("r_t"), 1)
                for x in range(2):
                    c = ps[:, 4 * x + 1, :].rearrange("p (a l t) -> p a l t", a=2, l=2)
                    dve.wait_ge(S("r_cT"), i * 2 + (x + 1))
                    for d in range(2):
                        w = b_dec[:, d, bass.ds(i * 2 + x, 1), :].rearrange("p a l -> p (a l)")[:, :, None].to_broadcast([P, 2, P])
                        dve.tensor_tensor(r_ck[x][:, d], c[:, 0], w, ALU.mult)
                    dve.tensor_copy(r_cv[x][:, :, :], c[:, 1]).then_inc(S("r_c"), 1)
                    dve.wait_ge(S("r_te"), i * 2 + (x + 1))
                    dve.tensor_tensor(r_tt[x][:, 3 * P:4 * P], r_tt[x][:, 3 * P:4 * P], ident[:, :], ALU.add).then_inc(S("r_tab"), 1)
                for j in range(4):
                    for x in range(2):
                        dve.wait_ge(S("r_s"), i * 8 + (2 * j + x + 1))
                        if j == 0:
                            dve.wait_ge(S("r_tab"), i * 2 + (x + 1))
                        dve.tensor_tensor(r_w[x][:, j, :], ps[:, 4 * x + 2 + j % 2, :], r_tt[x][:, (3 - j) * P:(3 - j) * P + SEQ], ALU.mult)\
                            .then_inc(S("r_w"), 1)

        def pe_ret(pe):
            pe.sem_inc(S("r_o"), 2)
            with pe.Fori(0, RH // 2) as i:
                for x in range(2):
                    pe.wait_ge(S("r_st"), i * 2 + (x + 1))
                    if x == 0:
                        pe.wait_ge(S("r_out"), i * 2 + 2)
                    for j in range(4):
                        mm = pe.transpose(ps[:, 4 * x, j * P:(j + 1) * P], r_st[x][:, SEQ + j * P:SEQ + (j + 1) * P], ident[:, :])
                    mm.then_inc(S("r_vT"), 1)
                    for j in range(4):
                        mm = pe.transpose(ps[:, 4 * x + 1, j * P:(j + 1) * P], r_st[x][:, 2 * SEQ + j * P:2 * SEQ + (j + 1) * P], ident[:, :])
                    mm.then_inc(S("r_cT"), 1)
                for j in range(4):
                    for x in range(2):
                        if j >= 2:
                            pe.wait_ge(S("r_w"), i * 8 + (2 * (j - 2) + x + 1))
                        pe.matmul(ps[:, 4 * x + 2 + j % 2, :], r_st[x][:, j * P:(j + 1) * P],
                                  b_q[:, bass.ds(i * 2 + x, 1), :].rearrange("p a t -> p (a t)"), start=True, stop=True).then_inc(S("r_s"), 1)
                    if j == 1:
                        for x in range(2):
                            pe.wait_ge(S("r_v"), i * 2 + (x + 1))
                            pe.wait_ge(S("r_c"), i * 2 + (x + 1))
                            for d in range(2):
                                for l in range(2):
                                    mm = pe.matmul(ps[:, 4 * x, d * P:(d + 1) * P], r_ck[x][:, d, l, :], r_cv[x][:, l, :],
                                                   start=(l == 0), stop=(l == 1))
                            mm.then_inc(S("r_sd"), 1)
                for x in range(2):
                    pe.wait_ge(S("r_S"), i * 2 + (x + 1))
                    pe.wait_ge(S("r_qd"), i * 4 + (2 * x + 2))
                    for d in range(2):
                        pe.matmul(ps[:, 4 * x + 1, :], r_S[x][:, d, :], r_qd[x][d][:, :], start=(d == 0), stop=False)
                    for j in range(4):
                        pe.wait_ge(S("r_w"), i * 8 + (2 * j + x + 1))
                        mm = pe.matmul(ps[:, 4 * x + 1, :], r_vT[x][:, j, :], r_w[x][:, j, :], start=False, stop=(j == 3))
                    mm.then_inc(S("r_o"), 1)

        def pe_centre(pe):
            for t in range(RH):
                pe.matmul(ps[:, t, :], ones[:, :], b_q[:, t, :], start=True, stop=True).then_inc(S("rn_sum"), 1)

        def dve_centre(dve):
            for t in range(RH):
                dve.wait_ge(S("rn_sum"), t + 1)
                dve.scalar_tensor_tensor(b_q[:, t, :], ps[:, t, :], -1.0 / P, b_q[:, t, :], ALU.mult, ALU.add).then_inc(S("rn_c"), 1)
            dve.wait_ge(S("rn_c"), RH)

        HEAD_TILES = 50

        def act_ret_gate(act):
            for t in range(RH):
                act.wait_ge(S("gated_y"), KT + t + 1)
                act.activation(flat(xb_hi[:, t], LATE), flat(hn_y[:, t % 2], TOK), ACT.Copy).then_inc(S("gated_hi"), 1)

        def dve_ret_gate(dve):
            dve.wait_ge(S("head_out"), HEAD_TILES + 2)
            for t in range(RH):
                y = flat(hn_y[:, t % 2], TOK)
                if t >= 2:
                    dve.wait_ge(S("gated_lo"), KT + t - 1)
                dve.tensor_tensor(y, b_q[:, t, :], b_g[:, t, :], ALU.mult).then_inc(S("gated_y"), 1)
                dve.wait_ge(S("gated_hi"), KT + t + 1)
                dve.tensor_tensor(flat(xb_lo[:, t], LATE), y, flat(xb_hi[:, t], LATE).bitcast(F32), ALU.subtract).then_inc(S("gated_lo"), 1)

        def pe_att_keys(pe):
            for t in range(KEYS // P):
                mm = pe.transpose(ps[:, t // 4, (t % 4) * P:(t % 4 + 1) * P], b_av[:, t * P:(t + 1) * P], ident[:, :])
            mm.then_inc(S("at_vT"), 1)

        def act_att_keys(act):
            for kv in range(AKV):
                for y in range(2):
                    to, at_ = slice(64 * y, 64 * y + 64), slice(64 * kv, 64 * kv + 64)
                    act.activation(a_kd[to, kv, 0:CTX], b_qk[at_, 5, 0:CTX], ACT.Copy)
                    act.activation(a_kd[to, kv, CTX:KEYS], b_qk[at_, 4, :], ACT.Copy)
            act.wait_ge(S("at_vT"), 1)
            for n, m in ((0, 4), (1, 2)):
                act.activation(a_vt[:, 4 * n:4 * n + m, :], ps[:, n, 0:m * P].rearrange("p (a t) -> p a t", a=m), ACT.Copy).then_inc(S("at_keys"), 1)

        UNITS = [(y, b) for y in range(2) for b in range(4)]

        def pool_att(pool):
            pool.wait_ge(S("at_keys"), 2)
            with pool.Fori(0, AKV) as kv:
                with pool.Fori(0, 2) as m:
                    it = kv * 2 + m
                    pool.wait_ge(S("at_o"), it * 2 + 2)
                    pool.sem_inc(S("pool_steps"), 1)
                    for y in range(2):
                        pool.tensor_tensor(a_qst[y][:, :], b_qk[:, bass.ds(it, 1), :].rearrange("p a t -> p (a t)"),
                                           b_half[:, y:y + 1].to_broadcast([P, SEQ]), ALU.mult).then_inc(S("at_q"), 1)
                    pool.tensor_copy(a_vst[:, :, :], a_vt[:, :, bass.ds(kv * AHD, AHD)]).then_inc(S("at_q"), 1)

        def pe_att(pe):
            pe.wait_ge(S("at_keys"), 2)
            pe.sem_inc(S("at_o"), 2)
            pe.sem_inc(S("at_T"), 2)
            with pe.Fori(0, AKV) as kv:
                with pe.Fori(0, 2) as m:
                    it = kv * 2 + m

                    def scores(u):
                        y, b = UNITS[u]
                        pe.wait_ge(S("at_q"), it * 3 + (1 if u < 4 else 2))
                        pe.wait_ge(S("at_e"), it * 8 + (u + 1))
                        for n in range(2):
                            mm = pe.matmul(ps[:, 2 * (u % 2) + n, 0:KEYS // 2], a_qst[y][:, b * P:(b + 1) * P],
                                           a_kd[:, bass.ds(kv, 1), n * (KEYS // 2):(n + 1) * (KEYS // 2)].rearrange("p a t -> p (a t)"),
                                           start=True, stop=True)
                        mm.then_inc(S("at_s"), 1)

                    def transposes(u):
                        pe.wait_ge(S("at_n"), it * 8 + (u + 1))
                        pe.wait_ge(S("at_pT"), it * 8 + (u + 1))
                        for t in range(KEYS // P):
                            mm = pe.transpose(ps[:, 4 + t // 3, (t % 3) * P:(t % 3 + 1) * P], a_p[u % 2][:, t * P:(t + 1) * P], ident[:, :])
                        mm.then_inc(S("at_T"), 1)

                    def values(y):
                        pe.wait_ge(S("at_q"), it * 3 + 3)
                        pe.wait_ge(S("at_pT"), it * 8 + (4 * y + 5))
                        if y == 0:
                            pe.wait_ge(S("at_lo"), it + 1)
                        for t in range(KEYS // P):
                            mm = pe.matmul(ps[64 * y:64 * y + 64, 6, :], a_vst[:, t, :], a_pT[y][:, t, :], start=(t == 0), stop=(t == KEYS // P - 1))
                        mm.then_inc(S("at_o"), 1)

                    scores(0)
                    for u in range(8):
                        if u < 7:
                            scores(u + 1)
                        transposes(u)
                        if u in (4, 7):
                            values(u // 7)

        def act_att(act):
            act.sem_inc(S("at_e"), 2)
            act.sem_inc(S("at_pT"), 1)
            with act.Fori(0, AKV) as kv:
                with act.Fori(0, 2) as m:
                    it = kv * 2 + m

                    def exps(u):
                        act.wait_ge(S("at_m"), it * 8 + (u + 1))
                        act.wait_ge(S("at_T"), it * 8 + (u + 1))
                        act.activation(a_p[u % 2][:, :].rearrange("p (a t) -> p a t", a=2), ps[:, 2 * (u % 2):2 * (u % 2) + 2, 0:KEYS // 2], ACT.Exp,
                                       bias=a_nm[u % 2][:, 0:1], scale=AHD ** -0.5, accum_out=a_sum[u % 2][:, 0:1]).then_inc(S("at_e"), 1)

                    exps(0)
                    for u in range(8):
                        if u < 7:
                            exps(u + 1)
                        y, b = UNITS[u]
                        act.wait_ge(S("at_T"), it * 8 + (u + 3))
                        if b == 0:
                            act.wait_ge(S("at_o"), it * 2 + (y + 1))
                        act.activation(a_pT[y][:, :, b * P:(b + 1) * P].rearrange("p (n a) t -> p n a t", n=2),
                                       ps[:, 4:6, 0:KEYS // 2].rearrange("p n (a t) -> p n a t", t=P), ACT.Copy).then_inc(S("at_pT"), 1)
                    fixed_wait(act)
                    act.wait_ge(S("at_o"), it * 2 + 4)
                    act.activation(flat(xb_hi[:, bass.ds(it + RH, 1)].rearrange("p a t -> p (a t)"), LATE), ps[:, 6, :], ACT.Copy)\
                        .then_inc(S("at_hi"), 1)

        def dve_att(dve):
            dve.sem_inc(S("at_lo"), 1)
            with dve.Fori(0, AKV) as kv:
                with dve.Fori(0, 2) as m:
                    it = kv * 2 + m
                    for u in range(9):
                        if u:
                            c = (u - 1) % 2
                            dve.wait_ge(S("at_e"), it * 8 + (u + 2))
                            dve.reciprocal(a_inv[c][:, 0:1], a_sum[c][:, 0:1]).then_inc(S("at_r"), 1)
                            dve.wait_ge(S("at_r"), it * 8 + u)
                            dve.tensor_scalar(a_p[c][:, :], a_p[c][:, :], a_inv[c][:, 0:1], None, ALU.mult).then_inc(S("at_n"), 1)
                        if u < 8:
                            c = u % 2
                            dve.wait_ge(S("at_s"), it * 8 + (u + 1))
                            dve.tensor_reduce(a_mx[c][:, 0:1], ps[:, 2 * c:2 * c + 2, 0:KEYS // 2], mybir.AxisListType.XY, ALU.max).then_inc(S("at_mx"), 1)
                            dve.wait_ge(S("at_mx"), it * 8 + (u + 1))
                            dve.tensor_scalar(a_nm[c][:, 0:1], a_mx[c][:, 0:1], -AHD ** -0.5, None, ALU.mult).then_inc(S("at_m"), 1)
                    dve.wait_ge(S("at_hi"), it + 1)
                    lo = flat(xb_lo[:, bass.ds(it + RH, 1)].rearrange("p a t -> p (a t)"), LATE)
                    hi = flat(xb_hi[:, bass.ds(it + RH, 1)].rearrange("p a t -> p (a t)"), LATE)
                    dve.tensor_tensor(lo, ps[:, 6, :], hi.bitcast(F32), ALU.subtract).then_inc(S("at_lo"), 1)

        def pe_b2_out(pe):
            for j in range(4):
                pe_hb(pe, HalfBlock(HB_B2_OUT + j), xb_hi, xb_lo, LATE, "out_ev", KT + 2 * j)

        def act_b2_out(act):
            for j in range(4):
                act_split(act, HalfBlock(HB_B2_OUT + j + 2))

        def dve_b2_out(dve):
            for j in range(4):
                dve_down(dve, "out_ev", HalfBlock(HB_B2_OUT + j), j, LATE, lambda k: mod_col("gate1", k))

        def dve_final(dve):
            dve_norm_stats(dve, (7, None), LATE)
            for k in range(KT):
                x = cols(h[:, k], LATE)
                dve.scalar_tensor_tensor(x, x, prm("final_g", k), root(LATE), ALU.mult, ALU.mult).then_inc(S("norm_y"), 1)

        def sp_final(sp):
            for k in range(KT):
                sp.wait_ge(S("norm_y"), 8 * KT + k + 1)
                sp.dma_start(out[:, k, :], flat(h[:, k], LATE)).then_inc(S("out"), 16)
            sp.wait_ge(S("out"), 16 * KT)

        @block.sync
        def _(sp):
            def load(turn, slot, index):
                sp.dma_start(raw[:, slot].rearrange("p k c -> p (k c)"), A["weights"][bass.ds(index, 1), :, :].rearrange("a p n -> (a p) n"))\
                    .then_inc(S(f"w_raw{slot}"), 16)
            load(0, 0, 0)
            load(0, 1, 1)
            with sp.Fori(1, N_HB // 2) as i:
                for s in range(2):
                    sp.wait_ge(S("w_lo"), i * 2 + (s - 1))
                    load(i, s, i * 2 + s)
            if N_HB % 2:
                sp.wait_ge(S("w_lo"), N_HB - 2)
                load(N_HB // 2, 0, N_HB - 1)
            sp_final(sp)

        @block.gpsimd
        def _(pool):
            st = Stages(pool, "POOL")
            pool.memset(ones[:, :], 1.0).then_inc(S("set"), 1)
            pool.memset(conv_in[:, :, 0:3], 0.0).then_inc(S("set"), 1)
            for step in [
                lambda: (pool_gdn_gates(pool), pool_norm(pool, 0, FULL)),
                lambda: (pool.memset(qkv[:, :, T:TP], 0.0).then_inc(S("set"), 1), pool.memset(g_S[:, :, :], 0.0).then_inc(S("set"), 1)),
                lambda: pool_gdn(pool),
                lambda: (pool_norm(pool, 1, FULL), pool_norm(pool, 2, FULL), pool_mls_gates(pool)),
                lambda: (pool_mls_state(pool), pool_mls(pool)),
                lambda: (pool_norm(pool, 3, LATE), pool_norm(pool, 4, LATE), pool_norm(pool, 5, CTXP, sq=ctx_sq), pool_b2_in(pool)),
                lambda: None,
                lambda: pool_rope(pool),
                lambda: pool_ret(pool),
                lambda: None,
                lambda: pool_att(pool),
                lambda: (pool_norm(pool, 6, LATE), pool_norm(pool, 7, LATE)),
            ]:
                step()
                st.end()

        @block.scalar
        def _(act):
            st = Stages(act, "ACT")
            act.dma_start(h[:, :, :], A["x_in"]).then_inc(S("in"), 16)
            act.dma_start(par[:, :], A["params"]).then_inc(S("in"), 16)
            act.dma_start(ident[:, :], A["ident"]).then_inc(S("in"), 16)
            act.wait_ge(S("in"), IN_FIRST)
            act_split(act, HalfBlock(0))
            act_split(act, HalfBlock(1))
            for step in [
                lambda: (act_norm(act, (0, 0), h, FULL), act_gdn_in(act)),
                lambda: (act_gdn_masks(act), act_headnorm(act, 0, 0, 16, FULL)),
                lambda: act_gdn(act),
                lambda: (act_head_squares(act, 16, 16, qkv, 16, on_sq, FULL, bufs=16),
                         act_norm(act, (0, 1), h, FULL, stats=False),
                         act_headnorm(act, 1, 16, 16, FULL),
                         act_two_layers(act, 0, HB_GDN_OUT, 2, FULL, ACT.Silu),
                         act_norm(act, (1, 2), h, FULL, ready=after_group(2)),
                         act_two_layers(act, 2, HB_MLP0, 4, FULL, ACT.Relu),
                         act_norm(act, (2, 3), h, FULL, ready=after_group(6)),
                         act_mls_in(act)),
                lambda: act_mls(act),
                lambda: (act_head_squares(act, 32, 8, ml, 8, mh_sq, FULL, bufs=8),
                         act_headnorm(act, 2, 32, 8, FULL),
                         act_mls_out(act),
                         act_norm(act, (3, 4), h, LATE, ready=("out_ev", 2)),
                         act_mod_c(act),
                         act_two_layers(act, 6, HB_MLP1, 4, LATE, ACT.Relu, beside=act_mod_load),
                         act_norm(act, (4, 5), h, LATE, ready=after_group(10)),
                         act_norm(act, (5, 6), b_ctx, CTXP, dst=(bc_hi, bc_lo), sq=ctx_sq),
                         act_b2_in(act)),
                lambda: (act_head_squares(act, 40, 6, b_qk, 0, hn_sq, TOK, bufs=6), act_decays(act), act_headnorm(act, 3, 40, 6, TOK, heads=2)),
                lambda: None,
                lambda: act_ret(act),
                lambda: (act.wait_ge(S("rn_c"), RH), act_head_squares(act, 46, 4, b_q, 0, hn_sq, TOK, bufs=4), act_headnorm(act, 4, 46, 4, TOK), act_ret_gate(act)),
                lambda: (act_att_keys(act), act_att(act)),
                lambda: (act_b2_out(act),
                         act_norm(act, (6, 7), h, LATE, ready=("out_ev", KT + 2)),
                         act_two_layers(act, 10, HB_MLP2, 4, LATE, ACT.Relu, peel=True),
                         act_norm_stats(act, (7, None), h, LATE, ready=after_group(14))),
            ]:
                step()
                st.end()

        @block.vector
        def _(dve):
            st = Stages(dve, "DVE")
            dve.wait_ge(S("in"), IN_FIRST)
            dve_split(dve, HalfBlock(0))
            dve_split(dve, HalfBlock(1))
            for step in [
                lambda: (dve_norm(dve, (0, 0), h, FULL, lambda k: prm("attn_norm0", k), keep=True), dve_gdn_in(dve)),
                lambda: dve_headnorm(dve, 0, 0, 16, qkv, 0, FULL, 1.0, lambda i: prm_dyn("l2_gain", i)),
                lambda: dve_gdn(dve),
                lambda: (dve_norm(dve, (0, 1), h, FULL, lambda k: prm("attn_norm0", k), stats=False),
                         dve_headnorm(dve, 1, 16, 16, qkv, 16, FULL, 1.0 / P, lambda i: prm("gdn_norm", 0)),
                         dve_two_layers(dve, 0, HB_GDN_OUT, 2, FULL,
                                        gate=lambda i, t: qkv[:, bass.ds(i * 8 + (16 + t), 1), 0:T].rearrange("p a t -> p (a t)")),
                         dve_norm(dve, (1, 2), h, FULL, lambda k: prm("ffn_norm0", k)),
                         dve_two_layers(dve, 2, HB_MLP0, 4, FULL),
                         dve_norm(dve, (2, 3), h, FULL, lambda k: prm("attn_norm1", k)),
                         dve_mls_in(dve)),
                lambda: dve_mls(dve),
                lambda: (dve_headnorm(dve, 2, 32, 8, ml, 8, FULL, 1.0 / P, lambda i: prm_dyn("mls_norm", i)),
                         dve_mls_out(dve),
                         dve_norm(dve, (3, 4), h, LATE, lambda k: prm("ffn_norm1", k)),
                         dve_mod_start(dve),
                         dve_two_layers(dve, 6, HB_MLP1, 4, LATE, beside=dve_mod_sums),
                         dve_mod(dve),
                         dve_norm(dve, (4, 5), h, LATE, lambda k: gain_col(0, k), shift=(lambda k: mod_col("shift1", k), 0)),
                         dve_norm(dve, (5, 6), b_ctx, CTXP, lambda k: gain_col(1, k), shift=(ctx_shift, 1), dst=(bc_hi, bc_lo), at_=5),
                         dve_b2_in(dve)),
                lambda: (dve_decays(dve), dve_headnorm(dve, 3, 40, 6, b_qk, 0, TOK, 1.0 / AHD, lambda i: prm_dyn("qk_norm", i), heads=2)),
                lambda: dve_rope(dve),
                lambda: dve_ret(dve),
                lambda: (dve_centre(dve), dve_headnorm(dve, 4, 46, 4, b_q, 0, TOK, 1.0 / P, lambda i: prm_dyn("ret_gn", i)), dve_ret_gate(dve)),
                lambda: dve_att(dve),
                lambda: (dve_b2_out(dve),
                         dve_norm(dve, (6, 7), h, LATE, lambda k: gain_col(2, k), shift=(lambda k: mod_col("shift2", k), 2)),
                         dve_two_layers(dve, 10, HB_MLP2, 4, LATE, scale=lambda k: mod_col("gate2", k), peel=True),
                         dve_final(dve)),
            ]:
                step()
                st.end()

        @block.tensor
        def _(pe):
            st = Stages(pe, "PE")
            pe.wait_ge(S("set"), 2)
            pe.wait_ge(S("in"), IN_FIRST)
            for step in [
                lambda: (pe_norm(pe, (0, 0), FULL), pe_gdn_in(pe)),
                lambda: pe_headnorm(pe, 0, 16, l2_sq, FULL, sums=False),
                lambda: pe_gdn(pe),
                lambda: (pe_headnorm(pe, 16, 16, on_sq, FULL, bufs=16),
                         pe_two_layers(pe, 0, HB_GDN_OUT, 2, FULL, norm=1),
                         pe_norm(pe, (1, 2), FULL),
                         pe_two_layers(pe, 2, HB_MLP0, 4, FULL, norm=2),
                         pe_norm(pe, (2, 3), FULL),
                         pe_mls_in(pe)),
                lambda: pe_mls(pe),
                lambda: (pe_headnorm(pe, 32, 8, mh_sq, FULL, bufs=8),
                         pe_mls_out(pe),
                         pe_norm(pe, (3, 4), LATE),
                         pe_two_layers(pe, 6, HB_MLP1, 4, LATE, norm=4),
                         pe_norm(pe, (4, 5), LATE),
                         pe_b2_in(pe)),
                lambda: (pe.wait_ge(S("in"), IN_ALL), pe_headnorm(pe, 40, 6, hn_sq, TOK, heads=2, bufs=6)),
                lambda: pe_rope(pe),
                lambda: pe_ret(pe),
                lambda: (pe_centre(pe), pe_headnorm(pe, 46, 4, hn_sq, TOK, bufs=4)),
                lambda: (pe_att_keys(pe), pe_att(pe)),
                lambda: (pe_b2_out(pe),
                         pe_norm(pe, (6, 7), LATE),
                         pe_two_layers(pe, 10, HB_MLP2, 4, LATE, norm=7, peel=True),
                         pe_norm(pe, (7, None), LATE)),
            ]:
                step()
                st.end()


def tiles_of(v):
    return np.ascontiguousarray(v.reshape(-1, P).T)


def half_blocks(w):
    n = w.shape[1] // HB_COLS
    return w.reshape(KT, P, n, HB_COLS).transpose(2, 1, 0, 3).reshape(n, P, HB_ELEMS)


def gate_block(parts):
    out = np.zeros((D, HB_COLS), np.float32)
    for i, w in enumerate(parts):
        out[:, 32 * i:32 * i + w.shape[1]] = w
    return half_blocks(out)


def two_layers(up, down):
    out = []
    for g in range(up.shape[1] // D):
        out += [half_blocks(up[:, g * D:(g + 1) * D]), half_blocks(down[g * D:(g + 1) * D])]
    return np.concatenate(out)


def mod_order(x):
    return x[[t for g in range(MOD_GROUPS) for t in [4 * g + n for n in range(4)] + [16 + 8 * g + n for n in range(8)]]]


def host_arrays(v):
    gi, gq = v["gdn_in"][0], 4096
    mi, bi = v["mlstm_in"][0], v["w_in_2"][0]
    weights = [
        gate_block([gi[:, gq + 2048 + GH:], gi[:, gq + 2048:gq + 2048 + GH]]), half_blocks(gi[:, :gq]),
        two_layers(gi[:, gq:gq + 2048], v["gdn_out"][0]),
        two_layers(v["ff_up"][0], v["ff_down"][0]),
        gate_block([mi[:, 3072:3072 + MH], mi[:, 3072 + MH:]]), half_blocks(mi[:, :3072]),
        half_blocks(v["mlstm_out"][0]),
        two_layers(v["ff_up"][1], v["ff_down"][1]),
        half_blocks(bi), half_blocks(v["w_out_2"][0]),
        two_layers(v["w_ff1_2"][0], v["w_ff2_2"][0]),
    ]
    params = np.zeros((P, N_PARAMS), np.float32)

    def put(name, x, rows=slice(0, P)):
        a, n = PARAMS[name]
        params[rows, a:a + n] = x

    for i in range(2):
        put(f"attn_norm{i}", tiles_of(v["attn_norm"][i]))
        put(f"ffn_norm{i}", tiles_of(v["ffn_norm"][i]))
    put("conv", v["gdn_conv"][0].reshape(4, 32, P).transpose(2, 1, 0).reshape(P, 128))
    put("gdn_norm", tiles_of(v["gdn_norm"][0]))
    put("mls_norm", tiles_of(v["mlstm_norm"][0]))
    put("a_log", v["gdn_a_log"][0][:, None], slice(0, GH))
    put("dt_bias", v["gdn_dt_bias"][0][:, None], slice(0, GH))
    put("gate_bias", v["mlstm_gate_bias"][0][:MH, None], slice(0, MH))
    put("gate_bias", v["mlstm_gate_bias"][0][MH:, None], slice(32, 32 + MH))
    for name, key in (("norm1_g", "norm1_g_2"), ("norm2_g", "norm2_g_2"), ("ret_gn", "ret_gn_g_2")):
        put(name, tiles_of(v[key][0]))
    put("final_g", tiles_of(v["final_norm_g_2"]))
    put("b_mod", mod_order(v["b_mod_2"][0].reshape(48, P)).T)
    for y in range(2):
        gains = [v["q_norm_g_2"][0]] * 4 + [v["k_norm_g_2"][0]] * 2
        put("qk_norm", np.stack(gains, 1), slice(64 * y, 64 * y + 64))
    put("l2_gain", np.repeat(np.float32([P ** -0.5, 1.0]), GQK)[None, :])
    put("ret_rate", v["ret_log_rate_2"][0].reshape(1, 8))
    tokens = np.concatenate([v["meta_tokens"], v["x"][0]])
    return {
        "weights": np.concatenate(weights),
        "weights_mod": mod_order(v["w_mod_2"][0].T.reshape(48, P, D)).reshape(24, 2, P, D).transpose(0, 2, 1, 3).reshape(24, P, 2 * D),
        "c_in": np.broadcast_to(np.stack([v["c_2"][0], v["c_ctx_2"]])[None], (P, 2, D)),
        "x_in": tokens.T.reshape(KT, P, T).transpose(1, 0, 2),
        "ctx_in": v["ctx_2"][0].T.reshape(KT, P, CTX).transpose(1, 0, 2),
        "params": params,
    }


def host_constants():
    i = np.arange(CH)
    lower = []
    for l in range(LEVELS):
        n = 1 << l
        same = (i[:, None] // (2 * n)) == (i[None, :] // (2 * n))
        lower.append(same & (i[:, None] // n % 2 == 1) & (i[None, :] // n % 2 == 0))
    mask_u = np.stack([m.T for m in lower], 1).astype(np.uint32)
    neg = np.where(i[None, :] >= i[:, None], 0.0, -1e30).astype(np.float32)
    sel = np.zeros((MH, P + 4), np.float32)
    for k in range(MH):
        sel[k, 64 * (k % 2):64 * (k % 2) + 64] = 1.0
        sel[k, P + k // 2] = 1.0
    pair = np.zeros((MH, 4, P), np.float32)
    for k in range(MH):
        pair[k, k // 2, 64 * (k % 2):64 * (k % 2) + 64] = 1.0
    t = np.arange(SEQ, dtype=np.float32)
    ret_f = np.float32(10000.0) ** (-np.arange(64, dtype=np.float32) / np.float32(64))
    att_f = np.float32(10000.0) ** (-np.arange(16, dtype=np.float32) / np.float32(16))
    ret_ang = t[:, None] * ret_f
    att_ang = np.concatenate([(t // 64)[:, None] * att_f, (t % 64)[:, None] * att_f], 1)
    rope, perm = np.zeros((P, 4, SEQ), np.float32), np.zeros((P, 2, P), np.float32)
    for n, ang in enumerate((ret_ang, att_ang)):
        w = ang.shape[1]
        for p in range(P):
            upper = p % (2 * w) >= w
            rope[p, 2 * n] = np.cos(ang[:, p % w])
            rope[p, 2 * n + 1] = np.sin(ang[:, p % w]) * (1.0 if upper else -1.0)
            perm[p - w if upper else p + w, n, p] = 1.0
    tau = (np.arange(SEQ + 3 * P)[None, :] - 3 * P - np.arange(P)[:, None]).astype(np.float32)
    pos = np.broadcast_to(np.stack([t + 1, SEQ - t])[None], (P, 2, SEQ))
    l = np.arange(P)[:, None] + P * np.arange(2)[None, :]
    half = (np.arange(P)[:, None] // 64 == np.arange(2)[None, :]).astype(np.float32)
    return {"rope": rope, "perm": perm, "tau": np.stack([np.maximum(tau, 0), np.maximum(-tau, 0)], 1),
            "pos": pos, "lpos": np.stack([CTX - 1 - l, l], 1).astype(np.float32), "half": half, "mls_pair": pair, "ident": np.eye(P, dtype=np.float32), "mask_u": mask_u, "neg": neg, "mls_sel": sel}


def kernel(**inputs):
    import concourse.bacc as _bacc
    from concourse.bass_utils import run_bass_kernel_spmd as _run

    v = {k: np.asarray(a) for k, a in inputs.items()}
    arrays = {k: np.ascontiguousarray(a) for k, a in {**host_arrays(v), **host_constants()}.items()}
    nc = _bacc.Bacc("TRN2", target_bir_lowering=False, num_devices=1)
    A = {k: nc.dram_tensor(k, a.shape, mybir.dt.from_np(a.dtype), kind="ExternalInput").ap() for k, a in arrays.items()}
    out = nc.dram_tensor("out", (P, KT, SEQ), F32, kind="ExternalOutput").ap()
    build_program(nc, A, out)
    r = _run(nc, [arrays], core_ids=[0])
    got = r.results[0]["out"]
    return np.ascontiguousarray(got.transpose(2, 1, 0).reshape(1, SEQ, D))
```

```python
from contextlib import ExitStack

import numpy as np

import concourse.bass as bass
from concourse import mybir

F32 = mybir.dt.float32
F32R = mybir.dt.float32r
U32 = mybir.dt.uint32
ALU = mybir.AluOpType
ACT = mybir.ActivationFunctionType

P = 128
D = 1024
KT = D // P
N_META, SEQ, CTX = 16, 512, 256
T = N_META + SEQ
EPS = 1e-6

CH = 106
NCH = -(-T // CH)
TP = CH * NCH
LEVELS = 7

GH, GQK = 16, 8
MH, MDK = 8, 64
GATE_CAP = 15.0
RH = 4
AH, AKV, AHD = 8, 2, 64
KEYS = SEQ + CTX

HB_COLS = 256
HB_ELEMS = KT * HB_COLS
HB_GDN_GATES = 0
HB_GDN_IN = HB_GDN_GATES + 1
N_GDN_IN = 4096 // HB_COLS
HB_GDN_OUT = HB_GDN_IN + N_GDN_IN
HB_MLP0 = HB_GDN_OUT + 16
HB_MLS_GATES = HB_MLP0 + 32
HB_MLS_IN = HB_MLS_GATES + 1
N_MLS_IN = 3072 // HB_COLS
HB_MLS_OUT = HB_MLS_IN + N_MLS_IN
HB_MLP1 = HB_MLS_OUT + 4
HB_B2_IN = HB_MLP1 + 32
N_B2_IN = 2816 // HB_COLS
HB_B2_OUT = HB_B2_IN + N_B2_IN
HB_MLP2 = HB_B2_OUT + 4
N_HB = HB_MLP2 + 32
MOD_GROUPS = 4

PARAMS = {}


def _param(name, n):
    PARAMS[name] = (sum(w for _, w in PARAMS.values()), n)


for _name, _n in [("attn_norm0", 8), ("attn_norm1", 8), ("ffn_norm0", 8), ("ffn_norm1", 8), ("conv", 128),
                  ("gdn_norm", 1), ("mls_norm", 8), ("a_log", 1), ("dt_bias", 1), ("gate_bias", 1),
                  ("norm1_g", 8), ("norm2_g", 8), ("final_g", 8), ("ret_gn", 4), ("qk_norm", 6),
                  ("b_mod", 48), ("ret_rate", 8), ("l2_gain", 16)]:
    _param(_name, _n)
N_PARAMS = sum(w for _, w in PARAMS.values())

SB0 = 16512
SB_RAW = SB0
SB_WHI = SB_RAW + 2 * HB_ELEMS * 4
SB_WLO = SB_WHI + 2 * HB_ELEMS * 4
SB_H = SB_WLO + 2 * HB_ELEMS * 4
SB_CONST = SB_H + KT * T * 4
CONST_BYTES = 5376
SB_XA = SB_CONST + CONST_BYTES
X_BYTES = KT * T * 4
SB_XB = SB_XA + 2 * X_BYTES
SB_G = SB_XB + 2 * X_BYTES
SB_END = 229368


class HalfBlock:

    def __init__(self, first, i=0, step=0):
        assert step % 2 == 0
        self.index = first + i * step if step else first
        self.turn = first // 2 + i * (step // 2) if step else first // 2
        self.slot = first % 2
        self.first, self.fixed = first, step == 0

    def after(self, n):
        out = HalfBlock(self.first + n)
        if not self.fixed:
            out.index, out.turn = self.index + n, self.turn - self.first // 2 + (self.first + n) // 2
            out.fixed = False
        return out

    def exists(self):
        return not self.fixed or self.first < N_HB


def build_program(nc, A, out):
    with ExitStack() as ctx:
        sems = {}

        def S(name):
            if name not in sems:
                sems[name] = ctx.enter_context(nc.semaphore(name))
            return sems[name]

        def at(name, shape, offset, dt=F32):
            assert offset + int(np.prod(shape[1:])) * 4 <= SB_END, (name, offset)
            return nc.alloc_sbuf_tensor_at(name, shape, dt, offset=offset)

        class Region:

            def __init__(self, start, end):
                self.next, self.end = start, end

            def take(self, name, shape, dt=F32):
                t = at(name, shape, self.next, dt)
                self.next += -(-int(np.prod(shape[1:])) * 4 // 32) * 32
                assert self.next <= self.end, (name, self.next - self.end)
                return t

        raw = at("raw", [P, 2, KT, HB_COLS], SB_RAW)
        whi = at("whi", [P, 2, KT, HB_COLS], SB_WHI, F32R)
        wlo = at("wlo", [P, 2, KT, HB_COLS], SB_WLO, F32R)
        h = at("h", [P, KT, T], SB_H)
        con = Region(SB_CONST, SB_XA)
        ident = con.take("ident", [P, P])
        ones = con.take("ones", [P, P])
        par = con.take("par", [P, N_PARAMS])
        rstd = con.take("rstd", [P, T])
        misc = con.take("misc", [P, 8])
        stat = con.take("stat", [P, 8])
        head_stat = con.take("head_stat", [P, 96])
        head_st = [con.take(f"head_st{c}", [P, 8], F32R) for c in range(2)]
        xa_hi = at("xa_hi", [P, KT, T], SB_XA, F32R)
        xa_lo = at("xa_lo", [P, KT, T], SB_XA + X_BYTES, F32R)
        xb_hi = at("xb_hi", [P, KT, T], SB_XB, F32R)
        xb_lo = at("xb_lo", [P, KT, T], SB_XB + X_BYTES, F32R)
        ps = ctx.enter_context(nc.psum_tensor("ps", [P, 8, 512], F32))

        def prm(name, i=None):
            a, n = PARAMS[name]
            return par[:, a:a + n] if i is None else par[:, a + i:a + i + 1]

        def prm_dyn(name, i):
            return par[:, bass.ds(i + PARAMS[name][0], 1)]

        def head_roots(name, offset):
            return at(name + "_root", [P, T], offset), at(name + "_hi", [P, T], offset + T * 4, F32R), at(name + "_lo", [P, T], offset, F32R)

        qkv = at("qkv", [P, 32, TP], SB_G)
        conv_r = Region(SB_XB, SB_G)
        conv_in = conv_r.take("conv_in", [P, 2, 3 + T])
        conv_acc = conv_r.take("conv_acc", [P, 2, T])
        l2_roots = head_roots("l2", conv_r.next)
        l2_sq = conv_r.take("l2_sq", [P, 2, T])
        gt_a = conv_r.take("gt_a", [P, T])
        gt_r2 = conv_r.take("gt_r", [P, T])
        gt_g = conv_r.take("gt_g", [P, TP])
        gt_one = conv_r.take("gt_one", [P, CH])
        gt_e = conv_r.take("gt_e", [P, GH, NCH])
        GATE_BYTES = 5120
        gate_r = Region(SB_G - GATE_BYTES, SB_G)
        g_row = gate_r.take("g_row", [P, TP])
        g_tok = gate_r.take("g_tok", [P, NCH, P])
        g_lastB = gate_r.take("g_lastB", [P, GH, NCH])
        assert conv_r.next <= SB_G - GATE_BYTES
        on_sq = at("on_sq", [P, GH, T], SB_XB)
        on_roots = head_roots("on", SB_XB)
        at_r = Region(SB_XA, SB_G - GATE_BYTES)
        g_maskU = at_r.take("g_maskU", [P, LEVELS, CH], U32)
        g_neg = at_r.take("g_neg", [P, CH])
        g_kst = at_r.take("g_kst", [P, GQK, CH])
        g_vst = at_r.take("g_vst", [P, GH, CH])
        g_S = at_r.take("g_S", [P, GH, P])
        g_B1, g_AT, g_AN, g_TV, g_U, g_EC, g_VT, g_KD = ([at_r.take(f"g_{n}{x}", [P, 4, w]) for x in range(2)]
                                                        for n, w in (("B1", P), ("AT", CH), ("AN", CH), ("TV", P), ("U", CH),
                                                                     ("EC", CH), ("VT", P), ("KD", P)))
        nt_r = Region(SB_G, SB_END)
        n_sq = nt_r.take("n_sq", [P, KT, T])
        n_y = nt_r.take("n_y", [P, 2, T])
        m_act = nt_r.take("m_act", [P, 2, T])
        m_y = nt_r.take("m_y", [P, 2, T])

        block = ctx.enter_context(nc.Block())

        ENGINES = ("PE", "ACT", "DVE", "POOL")

        class Stages:

            def __init__(self, eng, name):
                self.eng, self.name, self.n = eng, name, 0

            def end(self):
                self.eng.drain().then_inc(S("stage_" + self.name), 1)
                self.n += 1
                for other in ENGINES:
                    if other != self.name:
                        self.eng.wait_ge(S("stage_" + other), self.n)

        FULL = [(0, 0, T // 2), (1, T // 2, T // 2)]
        LATE = [(0, N_META, SEQ)]

        IN_ALL = (2 + 2 + 3 + 2 + 6) * 16
        IN_FIRST = 2 * 16

        def fixed_wait(eng):
            eng.wait_ge(S("in"), IN_FIRST)

        def pair(c, pieces):
            n = pieces[0][2]
            return ps[:, 2 * c:2 * c + len(pieces), 0:n]

        def cols(x, pieces):
            a, n = pieces[0][1], pieces[0][2]
            return x[:, a:a + n * len(pieces)].rearrange("p (a b) -> p a b", b=n)

        def flat(x, pieces):
            a = pieces[0][1]
            return x[:, a:a + pieces[0][2] * len(pieces)]

        def pe_hb(pe, hb, xhi, xlo, pieces, evac, tile, tiles=2, per_k=None, extra=None):
            pe.wait_ge(S("w_lo"), hb.index + 1)
            for c in range(tiles):
                pe.wait_ge(S(evac), tile + c + 1)
                for k in range(KT):
                    if per_k is not None and c == 0:
                        pe.wait_ge(S(per_k[0]), per_k[1] + k + 1)
                    terms = [(whi, xhi), (whi, xlo), (wlo, xhi)]
                    for n, (w, x) in enumerate(terms):
                        for bank, t0, tn in pieces:
                            mm = pe.matmul(ps[:, 2 * c + bank, 0:tn], w[:, hb.slot, k, c * P:(c + 1) * P],
                                           x[:, k, t0:t0 + tn], start=(k == 0 and n == 0), stop=(k == KT - 1 and n == 2))
                        if extra is not None:
                            ehi, elo, en = extra
                            mm = pe.matmul(ps[:, 2 * c + 1, 0:en], w[:, hb.slot, k, c * P:(c + 1) * P],
                                           (elo if n == 1 else ehi)[:, k, 0:en],
                                           start=(k == 0 and n == 0), stop=(k == KT - 1 and n == 2))
                mm.then_inc(S("tiles_done"), 1 if tiles == 2 else 2)

        def act_split(act, hb):
            if not hb.exists():
                return
            act.wait_ge(S(f"w_raw{hb.slot}"), hb.turn * 16 + 16)
            if not (hb.fixed and hb.first < 2):
                act.wait_ge(S("tiles_done"), hb.index * 2 - 2)
            act.activation(whi[:, hb.slot], raw[:, hb.slot], ACT.Copy).then_inc(S("w_hi"), 1)

        def dve_split(dve, hb):
            if not hb.exists():
                return
            dve.wait_ge(S("w_hi"), hb.index + 1)
            dve.tensor_tensor(wlo[:, hb.slot], raw[:, hb.slot], whi[:, hb.slot].bitcast(F32),
                              ALU.subtract).then_inc(S("w_lo"), 1)

        def token_chunks(pieces):
            n = pieces[0][2]
            size = next(n // m for m in range(1, n) if n % m == 0 and n // m <= P)
            return [(bank, a, t0 + a) for bank, t0, tn in pieces for a in range(0, tn, size)], size

        def pe_norm(pe, turn, pieces, sq=n_sq, to=6):
            chunks, size = token_chunks(pieces)
            pe.wait_ge(S("norm_sq"), turn[0] * KT + KT)
            pe.wait_ge(S("norm_acc"), turn[0] * (KT - 2) + KT - 2)
            for n, (_, _, t) in enumerate(chunks):
                for k in (0, KT - 1):
                    mm = pe.matmul(ps[0:size, 4, n:n + 1], sq[:, k, t:t + size], ones[:, 0:1], start=(k == 0), stop=(k != 0))
            mm.then_inc(S("norm_sum"), 1)
            pe.wait_ge(S("norm_rstd"), turn[0] + 1)
            for n, (bank, a, _) in enumerate(chunks):
                mm = pe.matmul(ps[:, to + bank, a:a + size], stat[0:size, n:n + 1].to_broadcast([size, P]), ident[0:size, 0:size],
                               start=True, stop=True)
            mm.then_inc(S("norm_all"), 1)

        def pool_norm(pool, turn, pieces, sq=n_sq):
            for k in range(1, KT - 1):
                pool.wait_ge(S("norm_sq"), turn * KT + k + 1)
                if k > 1:
                    pool.wait_ge(S("norm_acc"), turn * (KT - 2) + k - 1)
                pool.tensor_tensor(flat(sq[:, 0], pieces), flat(sq[:, 0], pieces), flat(sq[:, k], pieces), ALU.add)\
                    .then_inc(S("norm_acc"), 1)

        def act_squares(act, turn, src, pieces, ready=None, tiles=range(KT), sq=n_sq):
            for k in tiles:
                if ready:
                    act.wait_ge(S(ready[0]), ready[1] + k + 1)
                act.activation(flat(sq[:, k], pieces), flat(src[:, k], pieces), ACT.Square).then_inc(S("norm_sq"), 1)

        def act_norm_stats(act, turn, pieces):
            chunks, size = token_chunks(pieces)
            act.wait_ge(S("norm_inv"), turn[0] * 2 + 2)
            act.activation(stat[0:size, 0:len(chunks)], stat[0:size, 0:len(chunks)], ACT.Sqrt).then_inc(S("norm_rstd"), 1)

        def act_norm(act, turn, pieces, stats=True, dst=None, beside=None):
            hi = (dst or (xa_hi, xa_lo))[0]
            if stats:
                act_norm_stats(act, turn, pieces)
            if beside:
                beside()
            for k in range(KT):
                act.wait_ge(S("norm_y"), turn[1] * KT + k + 1)
                act.activation(flat(hi[:, k], pieces), flat(n_y[:, k % 2], pieces), ACT.Copy).then_inc(S("norm_hi"), 1)

        def dve_norm_stats(dve, turn, pieces, split=None):
            chunks, size = token_chunks(pieces)
            x = stat[0:size, 0:len(chunks)]
            dve.wait_ge(S("norm_sum"), turn[0] + 1)
            dve.tensor_scalar(x, ps[0:size, 4, 0:len(chunks)], 1.0 / D, EPS, ALU.mult, ALU.add).then_inc(S("norm_inv"), 1)
            dve.wait_ge(S("norm_inv"), turn[0] * 2 + 1)
            dve.reciprocal(x, x).then_inc(S("norm_inv"), 1)
            if split:
                dve_split(dve, split)
            dve.wait_ge(S("norm_all"), turn[0] + 1)

        def root(pieces, at_=6):
            return ps[:, at_:at_ + len(pieces), 0:pieces[0][2]]

        def dve_norm(dve, turn, src, pieces, gain, shift=None, stats=True, keep=False, dst=None, at_=6, split=None):
            hi, lo = dst or (xa_hi, xa_lo)
            if stats:
                dve_norm_stats(dve, turn, pieces, split)
            r = root(pieces, at_) if stats else cols(rstd, pieces)
            if keep:
                dve.tensor_copy(cols(rstd, pieces), r)

            def low(k):
                dve.wait_ge(S("norm_hi"), turn[1] * KT + k + 1)
                dve.tensor_tensor(flat(lo[:, k], pieces), flat(n_y[:, k % 2], pieces),
                                  flat(hi[:, k], pieces).bitcast(F32), ALU.subtract).then_inc(S("norm_lo"), 1)

            for k in range(KT):
                y = flat(n_y[:, k % 2], pieces)
                if k >= 2:
                    dve.wait_ge(S("norm_lo"), turn[1] * KT + k - 1)
                ins = dve.scalar_tensor_tensor(cols(n_y[:, k % 2], pieces), cols(src[:, k], pieces), gain(k), r, ALU.mult, ALU.mult)
                if shift is not None:
                    ins.then_inc(S("norm_scaled"), 1)
                    dve.wait_ge(S("norm_scaled"), shift[1] * KT + k + 1)
                    ins = dve.tensor_scalar(y, y, shift[0](k), None, ALU.add)
                ins.then_inc(S("norm_y"), 1)
                if k:
                    low(k - 1)
            low(KT - 1)

        def pe_head_sums(pe, base, i, first, n, sq, buf, pieces, heads=1):
            chunks, size = token_chunks(pieces)
            pe.wait_ge(S("head_sq"), base)
            for j, (_, _, t) in enumerate(chunks):
                mm = pe.matmul(ps[0:size, 4, bass.ds(i * (2 * heads) + (j * n * heads + first * heads), heads)], sq[:, buf, t:t + size],
                               ones[:, 0:1] if heads == 1 else b_half[:, :], start=True, stop=True)
            mm.then_inc(S("head_sums"), 1)

        def pe_headnorm(pe, turn, base, n, sq, roots, pieces, heads=1, bufs=2, sums=True):
            chunks, size = token_chunks(pieces)
            if sums:
                with pe.Fori(0, n // bufs) as i:
                    for c in range(bufs):
                        pe_head_sums(pe, i * bufs + (base + c + 1), i * (bufs // 2), c, n, sq, c, pieces, heads)
            rows = n * heads
            pe.wait_ge(S("head_inv"), 2 * turn + 2)
            for j, (bank, a, _) in enumerate(chunks):
                mm = pe.transpose(ps[0:rows, 6 + bank, a:a + size],
                                  head_stat[0:size, j * rows:(j + 1) * rows], ident[0:size, 0:size])
            mm.then_inc(S("head_rows"), 1)
            if base == 0:
                pe.sem_inc(S("head_all"), 2)
            pe.wait_ge(S("head_lo"), turn + 1)
            _, hi, lo = roots
            with pe.Fori(0, n // 2) as i:
                for c in range(2):
                    pe.wait_ge(S("head_st"), i * 2 + (base + c + 1))
                    pe.wait_ge(S("head_out"), i * 2 + (base + c + 1))
                    for bank, t0, tn in pieces:
                        for part in (hi, lo):
                            mm = pe.matmul(ps[:, 4 + 2 * c + bank, 0:tn],
                                           head_st[c][0:rows, 0:1].to_broadcast([rows, P]) if heads == 1 else hn_st[c][0:rows, :],
                                           part[0:rows, t0:t0 + tn], start=part is hi, stop=part is lo)
                    mm.then_inc(S("head_all"), 1)

        def act_head_squares(act, base, n, src, first, sq, pieces, bufs=2):
            with act.Fori(0, n // bufs) as i:
                for c in range(bufs):
                    if bufs != n:
                        fixed_wait(act)
                        act.wait_ge(S("head_sums"), i * bufs + (base + c + 1 - bufs))
                    act.activation(flat(sq[:, c], pieces), flat(src[:, bass.ds(i * bufs + (first + c), 1)].rearrange("p a t -> p (a t)"), pieces),
                                   ACT.Square).then_inc(S("head_sq"), 1)

        def act_headnorm(act, turn, base, n, roots, pieces, heads=1):
            rows = n * heads
            act.wait_ge(S("head_rows"), turn + 1)
            for to in roots[:2]:
                act.activation(cols(to[0:rows], pieces), ps[0:rows, 6:6 + len(pieces), 0:pieces[0][2]], ACT.Sqrt).then_inc(S("head_rstd"), 1)
            with act.Fori(0, n // 2) as i:
                for c in range(2):
                    fixed_wait(act)
                    act.wait_ge(S("head_all"), i * 2 + (base + c + 1))
                    row = ident[0:rows, bass.ds(i * (2 * heads) + c * heads, heads)]
                    to = head_st[c][0:rows, 0:1]
                    if heads > 1:
                        to = hn_st[c][0:rows].rearrange("p (y t) -> p y t", y=heads)
                        row = row[:, :, None].to_broadcast([rows, heads, P // heads])
                    act.activation(to, row, ACT.Copy)\
                        .then_inc(S("head_st"), 1)

        def dve_headnorm(dve, turn, base, n, roots, src, first, pieces, mean, gain, heads=1, split=None):
            chunks, size = token_chunks(pieces)
            x = head_stat[0:size, 0:n * len(chunks) * heads]
            if turn == 0:
                dve.sem_inc(S("head_out"), 2)
            dve.wait_ge(S("head_sums"), base + n)
            dve.tensor_scalar(x, ps[0:size, 4, 0:n * len(chunks) * heads], mean, EPS, ALU.mult, ALU.add).then_inc(S("head_inv"), 1)
            dve.wait_ge(S("head_inv"), 2 * turn + 1)
            dve.reciprocal(x, x).then_inc(S("head_inv"), 1)
            if split:
                dve_split(dve, split)
            root_, hi, lo = (flat(x[0:n * heads], pieces) for x in roots)
            dve.wait_ge(S("head_rstd"), 2 * turn + 2)
            dve.tensor_tensor(lo, root_, hi.bitcast(F32), ALU.subtract).then_inc(S("head_lo"), 1)
            with dve.Fori(0, n // 2) as i:
                for c in range(2):
                    dve.wait_ge(S("head_all"), i * 2 + (base + c + 3))
                    x = cols(src[:, bass.ds(i * 2 + (first + c), 1)].rearrange("p a t -> p (a t)"), pieces)
                    dve.scalar_tensor_tensor(x, x, gain(i * 2 + c), ps[:, 4 + 2 * c:4 + 2 * c + len(pieces), 0:pieces[0][2]],
                                             ALU.mult, ALU.mult).then_inc(S("head_out"), 1)

        def after_group(n):
            return ("two_ev", 16 * n - KT + 2)

        def pe_two_layers(pe, base, first, groups, pieces, norm, peel=False):
            def group(i, hb):
                for j in range(4):
                    pe_hb(pe, hb.after(j), xa_hi, xa_lo, pieces, "two_ev", i * 16 + (16 * base + 2 * j),
                          per_k=("norm_lo", norm * KT) if j == 0 else None)
                for j in range(4):
                    pe_hb(pe, hb.after(4 + j), xb_hi, xb_lo, pieces, "two_ev", i * 16 + (16 * base + 8 + 2 * j),
                          per_k=("two_lo", i * 8 + (8 * base + 2)) if j == 0 else None)
            run_groups(pe, group, first, groups, peel)

        def run_groups(eng, group, first, groups, peel):
            with eng.Fori(0, groups - peel) as i:
                group(i, HalfBlock(first, i, 8))
            if peel:
                group(groups - 1, HalfBlock(first + 8 * (groups - 1)))

        def act_down(act, hb, turn, pieces, ready, step=None):
            for j in range(4):
                if j < 3:
                    act_split(act, hb.after(j + 2))
                act_squares(act, turn, h, pieces, ready, (2 * j, 2 * j + 1))
                if j == 3:
                    act_split(act, hb.after(j + 2))
                if step:
                    step(j)

        def act_two_layers(act, base, first, groups, pieces, func, turn, beside=None):
            def group(i, hb, last=False):
                for j in range(4):
                    for c in range(2):
                        t = 2 * j + c
                        act.wait_ge(S("tiles_done"), hb.index * 2 + (t + 1))
                        act.wait_ge(S("two_ev"), i * 16 + (16 * base + t + 1))
                        act.activation(cols(m_act[:, c], pieces), pair(c, pieces), func).then_inc(S("two_act"), 1)
                        act.wait_ge(S("two_ev"), i * 16 + (16 * base + t + 3))
                        act.activation(flat(xb_hi[:, t], pieces), flat(m_y[:, c], pieces), ACT.Copy).then_inc(S("two_hi"), 1)
                    act_split(act, hb.after(j + 2))
                    if beside:
                        beside(act, i, j)
                if last:
                    act_down(act, hb.after(4), turn, pieces, after_group(base + groups), beside and (lambda j: beside(act, i, 4 + j)))
                else:
                    for j in range(4):
                        act_split(act, hb.after(4 + j + 2))
                        if beside:
                            beside(act, i, 4 + j)
            with act.Fori(0, groups - 1) as i:
                group(i, HalfBlock(first, i, 8))
            group(groups - 1, HalfBlock(first + 8 * (groups - 1)), last=True)

        def dve_two_layers(dve, base, first, groups, pieces, gate=None, scale=None, beside=None):
            if gate:
                dve.wait_ge(S("head_out"), 32 + 2)
            if base == 0:
                dve.sem_inc(S("two_ev"), 2)
                dve.sem_inc(S("two_lo"), 2)

            def group(i, hb, last=False):
                for j in range(4):
                    for c in range(2):
                        t = 2 * j + c
                        dve.wait_ge(S("two_act"), i * 8 + (8 * base + t + 1))
                        dve.wait_ge(S("two_lo"), i * 8 + (8 * base + t + 1))
                        other = pair(c, pieces) if gate is None else cols(gate(i, t), pieces)
                        dve.tensor_tensor(cols(m_y[:, c], pieces), cols(m_act[:, c], pieces), other, ALU.mult)\
                            .then_inc(S("two_ev"), 1)
                        dve.wait_ge(S("two_hi"), i * 8 + (8 * base + t + 1))
                        dve.tensor_tensor(flat(xb_lo[:, t], pieces), flat(m_y[:, c], pieces),
                                          flat(xb_hi[:, t], pieces).bitcast(F32), ALU.subtract).then_inc(S("two_lo"), 1)
                    dve_split(dve, hb.after(j + 2))
                    if beside:
                        beside(dve, i, j)
                for j in range(4):
                    dve_down(dve, "two_ev", hb.after(4 + j), j, pieces, scale, split=not (last and j == 3))
                    if beside:
                        beside(dve, i, 4 + j)
            with dve.Fori(0, groups - 1) as i:
                group(i, HalfBlock(first, i, 8))
            group(groups - 1, HalfBlock(first + 8 * (groups - 1)), last=True)

        def dve_down(dve, evac, hb, j, pieces, scale=None, split=True):
            for c in range(2):
                dve.wait_ge(S("tiles_done"), hb.index * 2 + (c + 1))
                x = cols(h[:, 2 * j + c], pieces)
                if scale is None:
                    ins = dve.tensor_tensor(x, pair(c, pieces), x, ALU.add)
                else:
                    ins = dve.scalar_tensor_tensor(x, pair(c, pieces), scale(2 * j + c), x, ALU.mult, ALU.add)
                ins.then_inc(S(evac), 1)
            if split:
                dve_split(dve, hb.after(2))

        def chunk_of(x, i):
            return x[:, :, bass.ds(i * CH, CH)]

        HALF_IN = N_GDN_IN // 4

        def gdn_hb(i, s):
            return HalfBlock(HB_GDN_IN, i, 2).after(s) if not isinstance(i, int) else HalfBlock(HB_GDN_IN + 2 * i + s)

        def pe_gdn_in(pe):
            def project(i, s):
                pe_hb(pe, gdn_hb(i, s), xa_hi, xa_lo, FULL, "conv_x", i * 4 + 2 * s)

            def sums(i, s, ahead=0):
                for c in range(2):
                    n = 2 * s + c - ahead
                    pe_head_sums(pe, i * 4 + (n + 1), i * 2, n, 2 * GQK, l2_sq, c, FULL)

            pe_hb(pe, HalfBlock(HB_GDN_GATES), xa_hi, xa_lo, FULL, "conv_x", 0, tiles=1, per_k=("norm_lo", 0))
            pe.wait_ge(S("gates_a"), 3)
            project(0, 0)
            project(0, 1)
            sums(0, 0)
            with pe.Fori(1, HALF_IN) as i:
                project(i, 0)
                sums(i, 1, ahead=4)
                project(i, 1)
                sums(i, 0)
            project(HALF_IN, 0)
            sums(HALF_IN, 1, ahead=4)
            pe_gdn_gates(pe)
            project(HALF_IN, 1)
            with pe.Fori(HALF_IN + 1, 2 * HALF_IN) as i:
                project(i, 0)
                project(i, 1)

        def act_gdn_in(act):
            act.sem_inc(S("conv_silu"), 2)
            act.wait_ge(S("tiles_done"), 2 * HB_GDN_GATES + 2)
            act_gdn_gates(act)

            def convolved(i, s, squares, split=True):
                hb = gdn_hb(i, s)
                for c in range(2):
                    act.wait_ge(S("tiles_done"), hb.index * 2 + (c + 1))
                    act.wait_ge(S("conv_out"), i * 4 + (2 * s + c + 1))
                    act.activation(cols(conv_in[:, c, 3:], FULL), pair(c, FULL), ACT.Copy).then_inc(S("conv_x"), 1)
                for c in range(2):
                    fixed_wait(act)
                    act.wait_ge(S("conv_out"), i * 4 + (2 * s + c + 3))
                    act.activation(qkv[:, bass.ds(i * 4 + (2 * s + c), 1), 0:T].rearrange("p a t -> p (a t)"),
                                   conv_acc[:, c, :], ACT.Silu).then_inc(S("conv_silu"), 1)
                if squares and (s or not isinstance(i, int)):
                    act.wait_ge(S("head_sums"), i * 4 + 2 * s)
                if split:
                    act_split(act, hb.after(2))
                if squares:
                    for c in range(2):
                        n = 2 * s + c
                        fixed_wait(act)
                        act.wait_ge(S("conv_silu"), i * 4 + (n + 3))
                        act.activation(l2_sq[:, c, :], qkv[:, bass.ds(i * 4 + n, 1), 0:T].rearrange("p a t -> p (a t)"), ACT.Square)\
                            .then_inc(S("head_sq"), 1)

            for s in range(2):
                convolved(0, s, True)
            with act.Fori(1, HALF_IN) as i:
                for s in range(2):
                    convolved(i, s, True)
            act_gdn_gates_rows(act)
            with act.Fori(HALF_IN, 2 * HALF_IN - 1) as i:
                for s in range(2):
                    convolved(i, s, False)
            for s in range(2):
                convolved(2 * HALF_IN - 1, s, False, split=s == 0)

        def dve_gdn_in(dve):
            dve.sem_inc(S("conv_out"), 2)
            dve_split(dve, HalfBlock(HB_GDN_GATES + 2))
            dve_gdn_gates(dve)

            def convolved(i, s, split=True):
                for c in range(2):
                    dve.wait_ge(S("conv_x"), i * 4 + (2 * s + c + 3))
                    dve.wait_ge(S("conv_silu"), i * 4 + (2 * s + c + 1))
                    for j in range(4):
                        w = prm_dyn("conv", i * 16 + (4 * (2 * s + c) + 3 - j))
                        x = conv_in[:, c, 3 - j:3 - j + T]
                        if j == 0:
                            ins = dve.tensor_scalar(conv_acc[:, c, :], x, w, None, ALU.mult)
                        else:
                            dve.wait_ge(S("conv_part"), i * 12 + (3 * (2 * s + c) + j))
                            ins = dve.scalar_tensor_tensor(conv_acc[:, c, :], x, w, conv_acc[:, c, :], ALU.mult, ALU.add)
                        ins.then_inc(S("conv_out" if j == 3 else "conv_part"), 1)
                if split:
                    dve_split(dve, gdn_hb(i, s).after(2))

            with dve.Fori(0, HALF_IN) as i:
                for s in range(2):
                    convolved(i, s)
            dve_gdn_gates_tokens(dve)
            with dve.Fori(HALF_IN, 2 * HALF_IN - 1) as i:
                for s in range(2):
                    convolved(i, s)
            for s in range(2):
                convolved(2 * HALF_IN - 1, s, split=s == 0)

        def by_chunk(x):
            return x.rearrange("p (n t) -> p n t", n=NCH)

        def pool_gdn_gates(pool):
            pool.memset(g_row[:, :], 0.0).then_inc(S("set"), 1)
            pool.memset(gt_g[0:GH, :], 0.0).then_inc(S("set"), 1)
            pool.memset(gt_one[0:GH, :], 1.0).then_inc(S("set"), 1)

        def act_gdn_gates(act):
            a_pre, b_pre = ps[0:GH, 0:2, 0:T // 2], ps[32:32 + GH, 0:2, 0:T // 2]
            dt = prm("dt_bias", 0)[0:GH]
            act.activation(cols(gt_a[0:GH], FULL), a_pre, ACT.Abs, bias=dt).then_inc(S("gates_a"), 1)
            act.activation(cols(gt_r2[0:GH], FULL), a_pre, ACT.Relu, bias=dt).then_inc(S("gates_a"), 1)
            act.activation(cols(gt_r2[32:32 + GH], FULL), b_pre, ACT.Sigmoid).then_inc(S("gates_a"), 1)
            act_split(act, HalfBlock(HB_GDN_GATES + 2))
            act.wait_ge(S("gates_a"), 1)
            act.activation(gt_a[0:GH, :], gt_a[0:GH, :], ACT.Exp, scale=-1.0).then_inc(S("gates_a"), 1)
            act.activation(misc[0:GH, 0:1], prm("a_log", 0)[0:GH], ACT.Exp).then_inc(S("gates_a"), 1)
            act.wait_ge(S("gates_a"), 4)
            act.activation(gt_a[0:GH, :], gt_a[0:GH, :], ACT.Ln, bias=1.0).then_inc(S("gates_a"), 1)

        def act_gdn_gates_rows(act):
            act.wait_ge(S("gates_d"), 10)
            act.activation(g_row[64:64 + GH, :], g_row[0:GH, :], ACT.Exp).then_inc(S("gates_a"), 1)
            act.activation(g_row[96:96 + GH, :], gt_g[0:GH, :], ACT.Exp).then_inc(S("gates_a"), 1)

        def dve_gdn_gates(dve):
            dve.wait_ge(S("set"), 2 + 3)
            dve.wait_ge(S("gates_a"), 6)
            dve.tensor_scalar(misc[0:GH, 1:2], misc[0:GH, 0:1], -1.0, None, ALU.mult).then_inc(S("gates_d"), 1)
            dve.tensor_tensor(gt_a[0:GH, :], gt_a[0:GH, :], gt_r2[0:GH, :], ALU.add).then_inc(S("gates_d"), 1)
            dve.wait_ge(S("gates_d"), 2)
            dve.tensor_scalar(gt_g[0:GH, 0:T], gt_a[0:GH, :], misc[0:GH, 1:2], None, ALU.mult).then_inc(S("gates_d"), 1)
            dve.wait_ge(S("gates_d"), 3)
            for n in range(NCH):
                t = slice(n * CH, n * CH + CH)
                dve.tensor_tensor_scan(g_row[0:GH, t], gt_one[0:GH, :], gt_g[0:GH, t], 0.0, ALU.mult, ALU.add)\
                    .then_inc(S("gates_d"), 1)
            dve.tensor_scalar(g_row[32:32 + GH, 0:T], gt_r2[32:32 + GH, :], -1.0, None, ALU.mult).then_inc(S("gates_d"), 1)
            dve.wait_ge(S("gates_d"), 8)
            cum = by_chunk(g_row[0:GH, :])
            dve.tensor_tensor(by_chunk(gt_g[0:GH, :]), cum[:, :, CH - 1:CH].to_broadcast([GH, NCH, CH]), cum,
                              ALU.subtract).then_inc(S("gates_d"), 1)

        def dve_gdn_gates_tokens(dve):
            dve.wait_ge(S("gates_a"), 7)
            dve.tensor_tensor(gt_e[64:64 + GH], ident[64:64 + GH, 64:64 + GH, None].to_broadcast([GH, GH, NCH]),
                              by_chunk(g_row[64:64 + GH, :])[:, None, :, CH - 1].to_broadcast([GH, GH, NCH]),
                              ALU.mult).then_inc(S("gates_d"), 1)
            dve.wait_ge(S("gates_p"), 1)
            dve.tensor_copy(g_tok[0:CH, 0:4, :], ps[0:CH, 5, :].rearrange("p (n q) -> p n q", n=4))
            dve.tensor_copy(g_tok[0:CH, 4, :], ps[0:CH, 6, 0:P])
            dve.tensor_copy(g_lastB[:, :, :], ps[:, 7, 0:GH * NCH].rearrange("p (h n) -> p h n", h=GH))

        def act_gdn_masks(act):
            act.dma_start(g_maskU[0:CH], A["mask_u"]).then_inc(S("in"), 16)
            act.dma_start(g_neg[0:CH, :], A["neg"]).then_inc(S("in"), 16)

        def pe_gdn_gates(pe):
            pe.wait_ge(S("gates_a"), 8)
            pe.wait_ge(S("gates_d"), 11)
            for n in range(NCH):
                pe.transpose(ps[0:CH, 5 + n // 4, (n % 4) * P:(n % 4 + 1) * P], g_row[:, n * CH:(n + 1) * CH], ident[:, :])
            pe.matmul(ps[:, 7, 0:GH * NCH], ones[64:64 + GH, :], gt_e[64:64 + GH].rearrange("p h n -> p (h n)"),
                      start=True, stop=True).then_inc(S("gates_p"), 1)

        def gdn_chunks(eng, chunk):
            with eng.Fori(0, NCH - 1) as i:
                chunk(i, False)
            chunk(NCH - 1, True)

        def gdn_pairs(last):
            return [(p, [(x, 2 * p + x) for x in range(2)], p == 0 or not last) for p in range(2)]

        def chunk_after(i, p):
            return i if p == 0 else i + 1

        def pe_gdn(pe):
            def early(i, p):
                for x in range(2):
                    for q in range(4):
                        hd = 8 * p + 4 * x + q
                        mm = pe.matmul(ps[:, 4 * x + 1, q * CH:(q + 1) * CH], ident[0:GH, hd:hd + 1].to_broadcast([GH, P]),
                                       g_row[0:GH, bass.ds(i * CH, CH)], start=True, stop=True)
                    mm.then_inc(S("g_cum"), 1)

            def transposed(i, p, l, x, g):
                if l:
                    pe.wait_ge(S("g_Uup"), i * 24 + (12 * p + 2 * (l - 1) + x + 1))
                else:
                    pe.wait_ge(S("g_U0"), i * 4 + g + 1)
                    pe.wait_ge(S("g_ec"), i * 4 + g + 1)
                for q in range(4):
                    mm = pe.transpose(ps[0:CH, 4 * x + 1, q * CH:(q + 1) * CH], g_U[x][0:CH, q, :], ident[0:CH, 0:CH])
                mm.then_inc(S("g_uT"), 1)

            def times_A(i, p, l, x, g):
                pe.wait_ge(S("g_T"), i * 24 + (12 * p + 2 * (l - 1) + x + 1))
                if l == 1:
                    pe.wait_ge(S("g_kd"), i * 4 + g + 1)
                for q in range(4):
                    mm = pe.matmul(ps[0:CH, 4 * x, q * CH:(q + 1) * CH], g_AT[x][0:CH, q, :], g_TV[x][0:CH, q, 0:CH],
                                   start=True, stop=True)
                mm.then_inc(S("g_P"), 1)

            def chunk(i, last):
                for p, gs, more in gdn_pairs(last):
                    if p == 0:
                        pe.wait_ge(S("g_kst"), i + 1)
                    for x, g in gs:
                        for m in range(2):
                            k = g_kst[:, 2 * g + m, :]
                            pe.matmul(ps[0:CH, 4 * x + 2, m * CH:(m + 1) * CH], k, k, start=True, stop=True)
                            mm = pe.matmul(ps[0:CH, 4 * x + 2, (2 + m) * CH:(3 + m) * CH], k,
                                           qkv[:, 2 * g + m, bass.ds(i * CH, CH)], start=True, stop=True)
                        mm.then_inc(S("g_kq"), 1)
                    if p == 0:
                        pe.wait_ge(S("g_vst"), i + 1)
                    for x, g in gs:
                        pe.wait_ge(S("g_oev"), i * 4 + g + 1)
                        for q in range(4):
                            mm = pe.transpose(ps[0:CH, 4 * x + 3, q * P:(q + 1) * P], g_vst[:, 4 * g + q, :], ident[:, :])
                        mm.then_inc(S("g_vT"), 1)
                    for x, g in gs:
                        pe.wait_ge(S("g_state"), i * 4 + g + 1)
                        for m in range(2):
                            mm = pe.transpose(ps[0:CH, 4 * x, m * P:(m + 1) * P], g_kst[:, 2 * g + m, :], ident[:, :])
                        mm.then_inc(S("g_kT"), 1)
                    for x, g in gs:
                        transposed(i, p, 0, x, g)
                        times_A(i, p, 1, x, g)
                    for l in range(1, LEVELS):
                        if l > 1:
                            for x, g in gs:
                                times_A(i, p, l, x, g)
                        for x, g in gs:
                            pe.wait_ge(S("g_Pc"), i * 24 + (12 * p + 2 * (l - 1) + x + 1))
                            if l == 1:
                                pe.wait_ge(S("g_an"), i * 4 + g + 1)
                            for q in range(4):
                                mm = pe.matmul(ps[0:CH, 4 * x + 2, q * CH:(q + 1) * CH], g_B1[x][0:CH, q, 0:CH],
                                               g_U[x][0:CH, q, :], start=True, stop=True)
                            mm.then_inc(S(f"g_XU{l}"), 1)
                        if l in (2, 3):
                            x, g = gs[l - 2]
                            pe.wait_ge(S("g_vt"), i * 4 + g + 1)
                            for q in range(4):
                                mm = pe.matmul(ps[0:CH, 4 * x + 3, q * P:(q + 1) * P], g_kst[:, 2 * g + q // 2, :], g_S[:, 4 * g + q, :],
                                               start=True, stop=True)
                            mm.then_inc(S("g_kS"), 1)
                        if l < LEVELS - 1:
                            for x, g in gs:
                                transposed(i, p, l, x, g)
                    for x, g in gs:
                        pe.wait_ge(S("g_r"), i * 4 + g + 1)
                        pe.wait_ge(S("g_Uup"), i * 24 + (12 * p + 2 * (LEVELS - 2) + x + 1))
                        for q in range(4):
                            mm = pe.matmul(ps[0:CH, 4 * x + 2, q * P:(q + 1) * P], g_U[x][0:CH, q, :], g_VT[x][0:CH, q, :],
                                           start=True, stop=True)
                        mm.then_inc(S("g_Tr"), 1)
                    if more:
                        early(chunk_after(i, p), 1 - p)
                    for x, g in gs:
                        pe.wait_ge(S("g_vn"), i * 4 + g + 1)
                        pe.wait_ge(S("g_qd"), i * 4 + g + 1)
                        for q in range(4):
                            o = ps[:, 4 * x + 3, q * CH:(q + 1) * CH]
                            pe.matmul(o, g_S[:, 4 * g + q, :], g_EC[x][:, q, :], start=True, stop=False)
                            mm = pe.matmul(o, g_TV[x][0:CH, q, :], g_AN[x][0:CH, q, :], start=False, stop=True)
                        mm.then_inc(S("g_o"), 1)
                        for q in range(4):
                            mm = pe.matmul(ps[:, 4 * x, q * P:(q + 1) * P], g_KD[x][0:CH, q, :], g_TV[x][0:CH, q, :],
                                           start=True, stop=True)
                        mm.then_inc(S("g_inc"), 1)

            early(0, 0)
            gdn_chunks(pe, chunk)

        def act_gdn(act):
            def decays(i, g, x):
                act.wait_ge(S("g_dif"), i * 4 + g + 1)
                act.activation(g_B1[x][0:CH, :, 0:CH], g_B1[x][0:CH, :, 0:CH], ACT.Exp).then_inc(S("g_dec"), 1)

            def decay(x):
                act.activation(g_EC[x][:, :, :], ps[:, 4 * x + 1, 0:4 * CH].rearrange("p (a t) -> p a t", a=4), ACT.Exp)\
                    .then_inc(S("g_ec"), 1)

            def values(i):
                act.activation(g_vst[:, :, :], chunk_of(qkv[:, 16:32], i), ACT.Copy).then_inc(S("g_vst"), 1)

            def transposed(i, p, l, x):
                act.wait_ge(S("g_uT"), i * 24 + (12 * p + 2 * l + x + 1))
                act.activation(g_TV[x][0:CH, :, 0:CH], ps[0:CH, 4 * x + 1, 0:4 * CH].rearrange("p (a t) -> p a t", a=4),
                               ACT.Copy).then_inc(S("g_T"), 1)

            def times_A(i, p, l, x, g):
                if l == 0:
                    act.wait_ge(S("g_an"), i * 4 + g + 1)
                act.wait_ge(S("g_P"), i * 24 + (12 * p + 2 * l + x + 1))
                act.activation(g_B1[x][0:CH, :, 0:CH], ps[0:CH, 4 * x, 0:4 * CH].rearrange("p (a t) -> p a t", a=4),
                               ACT.Copy).then_inc(S("g_Pc"), 1)

            def chunk(i, last):
                for p, gs, more in gdn_pairs(last):
                    for x, g in gs:
                        act.wait_ge(S("g_vT"), i * 4 + g + 1)
                        act.activation(g_VT[x][0:CH], ps[0:CH, 4 * x + 3, :].rearrange("p (a t) -> p a t", a=4), ACT.Copy)\
                            .then_inc(S("g_vt"), 1)
                    for x, g in gs:
                        transposed(i, p, 0, x)
                        times_A(i, p, 0, x, g)
                    for l in range(1, LEVELS - 1):
                        for x, g in gs:
                            transposed(i, p, l, x)
                        if l == 3 and p == 1 and more:
                            values(i + 1)
                        for x, g in gs:
                            times_A(i, p, l, x, g)
                    if more:
                        for x, g in gs:
                            decays(i, g + 2, x)
                    for x, g in gs:
                        fixed_wait(act)
                        act.wait_ge(S("g_o"), i * 4 + g + 1)
                        act.activation(chunk_of(qkv[:, 16 + 4 * g:20 + 4 * g], i),
                                       ps[:, 4 * x + 3, 0:4 * CH].rearrange("p (a t) -> p a t", a=4), ACT.Copy)\
                            .then_inc(S("g_oev"), 1)
                        if more:
                            decay(x)

            act.sem_inc(S("g_oev"), 2)
            values(0)
            for x in range(2):
                decays(0, x, x)
                decay(x)
            gdn_chunks(act, chunk)

        def dve_gdn(dve):
            def tok(i, row, g, w):
                return g_tok[0:CH, bass.ds(i, 1), row + 4 * g:row + 4 * g + 4].rearrange("p n a -> p (n a)")[:, :, None]\
                    .to_broadcast([CH, 4, w])

            def per_pair(x):
                return x.rearrange("p (m t) -> p m t", m=2)[:, :, None, :]

            def early(i, p, n):
                for x in range(2):
                    dve.wait_ge(S("g_cum"), n + (x + 1))
                    dve.tensor_tensor(g_B1[x][0:CH, :, 0:CH], ps[0:CH, 4 * x + 1, 0:4 * CH].rearrange("p (a t) -> p a t", a=4),
                                      tok(i, 0, 2 * p + x, CH), ALU.subtract).then_inc(S("g_dif0"), 1)
                for x in range(2):
                    d = g_B1[x][0:CH, :, 0:CH]
                    dve.wait_ge(S("g_dif0"), n + (x + 1))
                    dve.tensor_tensor(d, d, g_neg[0:CH, None, :].to_broadcast([CH, 4, CH]), ALU.add).then_inc(S("g_dif"), 1)
                for x in range(2):
                    dve.tensor_copy(g_U[x][0:CH], ident[0:CH, None, 0:CH].to_broadcast([CH, 4, CH]))

            def decayed(i, p, x):
                dve.tensor_tensor(g_AN[x][0:CH].rearrange("p (m r) t -> p m r t", m=2),
                                  per_pair(ps[0:CH, 4 * x + 2, 2 * CH:4 * CH]).to_broadcast([CH, 2, 2, CH]),
                                  g_B1[x][0:CH, :, 0:CH].rearrange("p (m r) t -> p m r t", m=2), ALU.mult).then_inc(S("g_an"), 1)

            def chunk(i, last):
                for p, gs, more in gdn_pairs(last):
                    for x, g in gs:
                        dve.wait_ge(S("g_kq"), i * 4 + g + 1)
                        dve.wait_ge(S("g_dec"), i * 4 + g + 1)
                        dve.tensor_tensor(g_AT[x][0:CH].rearrange("p (m r) t -> p m r t", m=2),
                                          per_pair(ps[0:CH, 4 * x + 2, 0:2 * CH]).to_broadcast([CH, 2, 2, CH]),
                                          g_B1[x][0:CH, :, 0:CH].rearrange("p (m r) t -> p m r t", m=2), ALU.mult)\
                            .then_inc(S("g_A0"), 1)
                        if x:
                            decayed(i, p, 0)
                        dve.wait_ge(S("g_A0"), i * 4 + g + 1)
                        dve.tensor_tensor(g_AT[x][0:CH], g_AT[x][0:CH], tok(i, 32, g, CH), ALU.mult).then_inc(S("g_A"), 1)
                        fixed_wait(dve)
                        dve.wait_ge(S("g_A"), i * 4 + g + 1)
                        dve.copy_predicated(g_U[x][0:CH], g_maskU[0:CH, 0:1, :].to_broadcast([CH, 4, CH]), g_AT[x][0:CH])\
                            .then_inc(S("g_U0"), 1)
                        dve.wait_ge(S("g_kT"), i * 4 + g + 1)
                        dve.tensor_tensor(g_KD[x][0:CH].rearrange("p (m r) t -> p m r t", m=2),
                                          per_pair(ps[0:CH, 4 * x, 0:2 * P]).to_broadcast([CH, 2, 2, P]),
                                          tok(i, 96, g, P).rearrange("p (m r) t -> p m r t", m=2), ALU.mult).then_inc(S("g_kd"), 1)
                        if x:
                            decayed(i, p, 1)
                    for x, g in gs:
                        dve.wait_ge(S("g_ec"), i * 4 + g + 1)
                        ec = g_EC[x][:, :, :].rearrange("p (m r) t -> p m r t", m=2)
                        dve.tensor_tensor(ec, qkv[:, 2 * g:2 * g + 2, bass.ds(i * CH, CH)][:, :, None, :].to_broadcast([P, 2, 2, CH]),
                                          ec, ALU.mult).then_inc(S("g_qd"), 1)
                    for l in range(1, LEVELS):
                        for x, g in gs:
                            fixed_wait(dve)
                            dve.wait_ge(S(f"g_XU{l}"), i * 4 + g + 1)
                            dve.copy_predicated(g_U[x][0:CH], g_maskU[0:CH, l:l + 1, :].to_broadcast([CH, 4, CH]),
                                                ps[0:CH, 4 * x + 2, 0:4 * CH].rearrange("p (a t) -> p a t", a=4))\
                                .then_inc(S("g_Uup"), 1)
                        if l in (2, 3):
                            x, g = gs[l - 2]
                            dve.wait_ge(S("g_kS"), i * 4 + g + 1)
                            for q in range(4):
                                e = g_tok[0:CH, bass.ds(i, 1), 64 + 4 * g + q:65 + 4 * g + q].rearrange("p n a -> p (n a)")
                                ins = dve.scalar_tensor_tensor(g_VT[x][0:CH, q, :], ps[0:CH, 4 * x + 3, q * P:(q + 1) * P], e,
                                                               g_VT[x][0:CH, q, :], ALU.mult, ALU.subtract)
                            ins.then_inc(S("g_r"), 1)
                    for x, g in gs:
                        dve.wait_ge(S("g_Tr"), i * 4 + g + 1)
                        dve.tensor_tensor(g_TV[x][0:CH], ps[0:CH, 4 * x + 2, :].rearrange("p (a t) -> p a t", a=4),
                                          tok(i, 32, g, P), ALU.mult).then_inc(S("g_vn"), 1)
                    if more:
                        early(chunk_after(i, p), 1 - p, i * 4 + (2 * p + 2))
                    for x, g in gs:
                        dve.wait_ge(S("g_inc"), i * 4 + g + 1)
                        dve.wait_ge(S("g_sdec"), i * 4 + g + 1)
                        dve.tensor_tensor(g_S[:, 4 * g:4 * g + 4, :], ps[:, 4 * x, :].rearrange("p (a t) -> p a t", a=4),
                                          g_S[:, 4 * g:4 * g + 4, :], ALU.add).then_inc(S("g_state"), 1)

            dve.sem_inc(S("g_state"), 2)
            dve.wait_ge(S("in"), IN_FIRST + 32)
            early(0, 0, 0)
            gdn_chunks(dve, chunk)

        def pool_gdn(pool):
            def keys(i):
                pool.tensor_copy(g_kst[:, :, :], chunk_of(qkv[:, 8:16], i)).then_inc(S("g_kst"), 1)

            def chunk(i, last):
                for p, gs, more in gdn_pairs(last):
                    if p == 1 and more:
                        pool.wait_ge(S("g_kS"), i * 4 + 4)
                        keys(i + 1)
                    for x, g in gs:
                        pool.wait_ge(S("g_o"), i * 4 + g + 1)
                        pool.tensor_tensor(g_S[:, 4 * g:4 * g + 4, :], g_S[:, 4 * g:4 * g + 4, :],
                                           g_lastB[:, 4 * g:4 * g + 4, bass.ds(i, 1)].to_broadcast([P, 4, P]), ALU.mult)\
                            .then_inc(S("g_sdec"), 1)

            keys(0)
            gdn_chunks(pool, chunk)

        ml = at("ml", [P, 24, TP], SB_G)
        mh_sq = at("mh_sq", [P, 8, T], SB_XA)
        mh_roots = head_roots("mh", SB_XA)
        mh_y = at("mh_y", [P, 2, T], SB_XA + 8 * T * 4)
        ma_r = Region(SB_XA, SB_XB)
        mg_r = Region(SB_XB, SB_G)
        c_neg = mg_r.take("c_neg", [P, CH])
        c_sel = mg_r.take("c_sel", [P, P + 4])
        c_pair = mg_r.take("c_pair", [P, 4, P])
        c_R1 = mg_r.take("c_R1", [P, TP])
        c_R2 = mg_r.take("c_R2", [P, TP])
        c_tok = mg_r.take("c_tok", [P, NCH, 64])
        c_keep = mg_r.take("c_keep", [P, NCH, 4])
        c_qst = ma_r.take("c_qst", [P, 8, CH])
        c_kst = ma_r.take("c_kst", [P, 4, CH])
        c_vst = ma_r.take("c_vst", [P, 8, CH])
        c_rst = ma_r.take("c_rst", [P, CH])
        c_C = ma_r.take("c_C", [P, 4, 2 * P])
        c_DA = [mg_r.take(f"c_DA{x}", [P, 4, CH]) for x in range(2)]
        c_B1, c_W, c_QS, c_VA, c_KW = ([ma_r.take(f"c_{n}{x}", [P] + w) for x in range(2)]
                                             for n, w in (("B1", [4, CH]), ("W", [4, CH]), ("QS", [4, CH]), ("VA", [4, 2 * P]),
                                                          ("KW", [4, MDK])))
        c_i, c_f, c_ln, c_mn, c_cum, c_M, c_t = (mg_r.take("c_" + n, [P, TP]) for n in ("i", "f", "ln", "mn", "cum", "M", "t"))
        c_one = mg_r.take("c_one", [P, CH])
        c_mp = mg_r.take("c_mp", [P, 8])
        c_kp = mg_r.take("c_kp", [P, NCH])
        c_kd = mg_r.take("c_kd", [P, NCH, 4])

        def pe_mls_in(pe):
            pe_hb(pe, HalfBlock(HB_MLS_GATES), xa_hi, xa_lo, FULL, "in_ev", 0, tiles=1, per_k=("norm_lo", 3 * KT))
            pe.wait_ge(S("gates_a"), GDN_A + 2)
            for first, last in ((0, 2), (2, N_MLS_IN // 2)):
                if first:
                    pe_mls_gates(pe)
                with pe.Fori(first, last) as i:
                    for s in range(2):
                        pe_hb(pe, HalfBlock(HB_MLS_IN, i, 2).after(s), xa_hi, xa_lo, FULL, "in_ev", i * 4 + 2 * s)

        def act_mls_in(act):
            act_mls_consts(act)
            act.wait_ge(S("tiles_done"), 2 * HB_MLS_GATES + 2)
            act_mls_gates(act)

            def evacuate(i, first, s, func, scale, split=True):
                hb = HalfBlock(HB_MLS_IN + first, i, 2).after(s) if not isinstance(i, int) else HalfBlock(HB_MLS_IN + first + 2 * i + s)
                for c in range(2):
                    fixed_wait(act)
                    act.wait_ge(S("tiles_done"), hb.index * 2 + (c + 1))
                    dst = ml[:, bass.ds(i * 4 + (2 * first + 2 * s + c), 1), 0:T].rearrange("p a t -> p (a t)")
                    act.activation(cols(dst, FULL), pair(c, FULL), func, scale=scale).then_inc(S("in_ev"), 1)
                if split:
                    act_split(act, hb.after(2))

            def evacuate_all(first, loops, func, scale):
                with act.Fori(0, loops) as i:
                    for s in range(2):
                        evacuate(i, first, s, func, scale)
            evacuate_all(0, 1, ACT.Copy, MDK ** -0.5)
            evacuate_all(2, 1, ACT.Copy, 1.0)
            act_mls_gates_rows(act)
            evacuate_all(4, 2, ACT.Copy, 1.0)
            evacuate_all(8, 1, ACT.Sigmoid, 1.0)
            for s in range(2):
                evacuate(1, 8, s, ACT.Sigmoid, 1.0, split=s == 0)

        def dve_mls_in(dve):
            dve.tensor_scalar(misc[0:40, 2:3], prm("gate_bias", 0)[0:40], 1.0 / GATE_CAP, None, ALU.mult).then_inc(S("gates_d"), 1)
            dve_split(dve, HalfBlock(HB_MLS_GATES + 2))
            dve_mls_gates(dve)
            for first, last in ((0, 2), (2, N_MLS_IN // 2 - 1)):
                if first:
                    dve_mls_gates_tokens(dve)
                with dve.Fori(first, last) as i:
                    for s in range(2):
                        dve_split(dve, HalfBlock(HB_MLS_IN, i, 2).after(s + 2))
            dve_split(dve, HalfBlock(HB_MLS_OUT))

        GDN_A, GDN_D, GDN_P = 8, 11, 1

        def pool_mls_gates(pool):
            pool.wait_ge(S("norm_sum"), 3)
            pool.memset(c_R1[:, :], 0.0).then_inc(S("set"), 1)
            pool.memset(c_R2[:, :], 0.0).then_inc(S("set"), 1)
            pool.memset(c_i[:, :], 0.0).then_inc(S("set"), 1)
            pool.memset(c_ln[:, :], 0.0).then_inc(S("set"), 1)
            pool.memset(c_mn[:, :], 0.0).then_inc(S("set"), 1)
            pool.memset(c_one[:, :], 1.0).then_inc(S("set"), 1)
            pool.memset(c_mp[:, :], 0.0).then_inc(S("set"), 1)

        def pool_mls_state(pool):
            for x in range(2):
                pool.memset(c_VA[x][:, :, P:2 * P], 1.0)
            pool.memset(c_C[:, :, :], 0.0).then_inc(S("set"), 1)

        def act_mls_consts(act):
            act.dma_start(c_neg[0:CH, :], A["neg"]).then_inc(S("in"), 16)
            act.dma_start(c_sel[0:MH, :], A["mls_sel"]).then_inc(S("in"), 16)
            act.dma_start(c_pair[32:32 + MH], A["mls_pair"]).then_inc(S("in"), 16)

        def act_mls_gates(act):
            act.wait_ge(S("set"), 7 + 7)
            act.wait_ge(S("gates_d"), GDN_D + 1)
            for a in (0, 32):
                act.activation(cols((c_i if a == 0 else c_f)[a:a + MH], FULL), ps[a:a + MH, 0:2, 0:T // 2], ACT.Tanh,
                               bias=misc[a:a + MH, 2:3], scale=1.0 / GATE_CAP).then_inc(S("gates_a"), 1)
            act_split(act, HalfBlock(HB_MLS_GATES + 2))
            f, ln = c_f[32:40, 0:T], c_ln[32:40, 0:T]
            act.wait_ge(S("gates_a"), GDN_A + 2)
            act.activation(ln, f, ACT.Abs, scale=GATE_CAP).then_inc(S("gates_a"), 1)
            act.wait_ge(S("gates_a"), GDN_A + 3)
            act.activation(ln, ln, ACT.Exp, scale=-1.0).then_inc(S("gates_a"), 1)
            act.wait_ge(S("gates_a"), GDN_A + 4)
            act.activation(ln, ln, ACT.Ln, bias=1.0).then_inc(S("gates_a"), 1)

        def act_mls_gates_rows(act):
            act.wait_ge(S("gates_d"), GDN_D + 26)
            act.activation(c_R1[32:40, :], c_t[0:8, :], ACT.Exp).then_inc(S("gates_a"), 1)
            act.activation(c_R1[64:72, :], c_cum[0:8, :], ACT.Exp, scale=-1.0).then_inc(S("gates_a"), 1)
            act.activation(c_R2[32:40, :], c_f[0:8, :], ACT.Exp).then_inc(S("gates_a"), 1)
            act.activation(c_kp[0:8, :], c_kp[0:8, :], ACT.Exp).then_inc(S("gates_a"), 1)

        def dve_mls_gates(dve):
            dve.wait_ge(S("set"), 7 + 7)
            dve.wait_ge(S("gates_a"), GDN_A + 2)
            dve.tensor_scalar(c_i[0:8, 0:T], c_i[0:8, 0:T], GATE_CAP, None, ALU.mult).then_inc(S("gates_d"), 1)
            dve.tensor_scalar(c_mn[32:40, 0:T], c_f[32:40, 0:T], GATE_CAP, 0.0, ALU.mult, ALU.min).then_inc(S("gates_d"), 1)
            dve.wait_ge(S("gates_a"), GDN_A + 5)
            dve.wait_ge(S("gates_d"), GDN_D + 3)
            dve.tensor_tensor(c_mn[32:40, :], c_mn[32:40, :], c_ln[32:40, :], ALU.subtract).then_inc(S("gates_d"), 1)
            dve.wait_ge(S("gates_d"), GDN_D + 4)
            for n in range(NCH):
                t = slice(n * CH, n * CH + CH)
                dve.tensor_tensor_scan(c_cum[0:8, t], c_one[32:40, :], c_mn[32:40, t], 0.0, ALU.mult, ALU.add)\
                    .then_inc(S("gates_d"), 1)
            dve.wait_ge(S("gates_d"), GDN_D + 9)
            dve.tensor_tensor(c_i[0:8, :], c_i[0:8, :], c_cum[0:8, :], ALU.subtract).then_inc(S("gates_d"), 1)
            for n in range(NCH):
                t = slice(n * CH, n * CH + CH)
                dve.wait_ge(S("gates_d"), GDN_D + 10 + 2 * n)
                dve.tensor_tensor_scan(c_M[0:8, t], c_i[0:8, t], c_i[0:8, t], c_mp[0:8, n:n + 1], ALU.max, ALU.max)\
                    .then_inc(S("gates_d"), 1)
                dve.wait_ge(S("gates_d"), GDN_D + 11 + 2 * n)
                last = (n + 1) * CH - 1
                dve.tensor_tensor(c_mp[0:8, n + 1:n + 2], c_cum[0:8, last:last + 1], c_M[0:8, last:last + 1], ALU.add)\
                    .then_inc(S("gates_d"), 1)
            dve.wait_ge(S("gates_d"), GDN_D + 20)
            top = by_chunk(c_M[0:8, :])[:, :, CH - 1:CH]
            dve.tensor_scalar(c_R1[0:8, :], c_M[0:8, :], -1.0, None, ALU.mult).then_inc(S("gates_d"), 1)
            dve.tensor_tensor(by_chunk(c_t[0:8, :]), c_mp[0:8, 0:NCH, None].to_broadcast([8, NCH, CH]), by_chunk(c_M[0:8, :]),
                              ALU.subtract).then_inc(S("gates_d"), 1)
            dve.tensor_tensor(c_cum[0:8, :], c_cum[0:8, :], c_M[0:8, :], ALU.add).then_inc(S("gates_d"), 1)
            dve.tensor_tensor(by_chunk(c_f[0:8, :]), by_chunk(c_i[0:8, :]), top.to_broadcast([8, NCH, CH]), ALU.subtract)\
                .then_inc(S("gates_d"), 1)
            dve.tensor_tensor(c_kp[0:8, :], c_mp[0:8, 0:NCH], top.rearrange("p n t -> p (n t)"), ALU.subtract).then_inc(S("gates_d"), 1)
            dve.tensor_copy(c_R2[0:8, :], c_i[0:8, :]).then_inc(S("gates_d"), 1)

        def dve_mls_gates_tokens(dve):
            dve.wait_ge(S("gates_a"), GDN_A + 9)
            dve.wait_ge(S("in"), IN_FIRST + 32 + 48)
            dve.tensor_tensor(c_kd[0:8], c_kp[0:8, :, None].to_broadcast([8, NCH, 4]),
                              c_sel[0:8, None, P:P + 4].to_broadcast([8, NCH, 4]), ALU.mult).then_inc(S("gates_d"), 1)
            dve.wait_ge(S("gates_p"), GDN_P + 1)
            dve.tensor_copy(c_tok[0:CH], ps[0:CH, 4, 0:NCH * 64].rearrange("p (n q) -> p n q", n=NCH))
            dve.tensor_copy(c_keep[:, :, :], ps[:, 5, 0:NCH * 4].rearrange("p (n m) -> p n m", n=NCH))

        def pe_mls_gates(pe):
            pe.wait_ge(S("gates_a"), GDN_A + 9)
            pe.wait_ge(S("gates_d"), GDN_D + 27)
            for n in range(NCH):
                pe.transpose(ps[0:CH, 4, n * 64:(n + 1) * 64], c_R2[0:64, n * CH:(n + 1) * CH], ident[0:64, 0:64])
            pe.matmul(ps[:, 5, 0:NCH * 4], c_sel[0:8, 0:P], c_kd[0:8].rearrange("p n m -> p (n m)"),
                      start=True, stop=True).then_inc(S("gates_p"), 1)

        def four(bank, w=CH, rows=P):
            return ps[0:rows, bank, 0:4 * w].rearrange("p (a t) -> p a t", a=4)

        def pe_mls(pe):
            with pe.Fori(0, NCH) as i:
                pe.wait_ge(S("c_st"), i * 4 + 1)
                for x in range(2):
                    pe.wait_ge(S("c_state"), i * 2 + x + 1)
                    pe.wait_ge(S("c_hs"), i * 2 + x + 1)
                    for q in range(4):
                        mm = pe.matmul(ps[0:CH, 4 * x, q * CH:(q + 1) * CH],
                                       ident[0:8, 4 * x + q:4 * x + q + 1].to_broadcast([8, CH]), c_rst[0:8, :], start=True, stop=True)
                    mm.then_inc(S("c_nm"), 1)
                    for m in range(2):
                        mm = pe.matmul(ps[:, 4 * x + 1, m * CH:(m + 1) * CH],
                                       c_pair[32:40, 2 * x + m, :], c_rst[32:40, :], start=True, stop=True)
                    mm.then_inc(S("c_si"), 1)
                    if x == 0:
                        pe.wait_ge(S("c_st"), i * 4 + 4)
                    for q in range(4):
                        mm = pe.matmul(ps[0:CH, 4 * x + 3, q * CH:(q + 1) * CH], c_kst[:, 2 * x + q // 2, :],
                                       c_qst[:, 4 * x + q, :], start=True, stop=True)
                    mm.then_inc(S("c_qk"), 1)
                    for q in range(4):
                        mm = pe.matmul(ps[:, 4 * x + 2, q * CH:(q + 1) * CH],
                                       ident[64:72, 64 + 4 * x + q:65 + 4 * x + q].to_broadcast([8, P]), c_rst[64:72, :],
                                       start=True, stop=True)
                    mm.then_inc(S("c_fl"), 1)
                pe.wait_ge(S("c_vst"), i + 1)
                for x in range(2):
                    pe.wait_ge(S("c_qs"), i * 2 + x + 1)
                    for m in range(2):
                        mm = pe.transpose(ps[0:CH, 4 * x + 1, m * P:(m + 1) * P], c_kst[:, 2 * x + m, :], ident[:, :])
                    mm.then_inc(S("c_kT"), 1)
                    pe.wait_ge(S("c_d0"), i * 2 + x + 1)
                    for q in range(4):
                        mm = pe.transpose(ps[0:CH, 4 * x, q * P:(q + 1) * P], c_vst[:, 4 * x + q, :], ident[:, :])
                    mm.then_inc(S("c_vT"), 1)
                pe.wait_ge(S("set"), 7 + 8)
                for x in range(2):
                    pe.wait_ge(S("c_va"), i * 2 + x + 1)
                    pe.wait_ge(S("c_w"), i * 2 + x + 1)
                    for bank, col, name in ((3, 0, "c_num"), (0, P, "c_den")):
                        for q in range(4):
                            o = ps[:, 4 * x + bank, q * CH:(q + 1) * CH]
                            pe.matmul(o, c_C[:, 2 * x + q // 2, col:col + P], c_QS[x][:, q, :], start=True, stop=False)
                            mm = pe.matmul(o, c_VA[x][0:CH, q, col:col + P], c_W[x][0:CH, q, :], start=False, stop=True)
                        mm.then_inc(S(name), 1)
                    pe.wait_ge(S("c_kw"), i * 2 + x + 1)
                    for q in range(4):
                        y = 64 * (q % 2)
                        mm = pe.matmul(ps[y:y + 64, 4 * x + 1, (q // 2) * 2 * P:(q // 2 + 1) * 2 * P], c_KW[x][0:CH, q, :],
                                       c_VA[x][0:CH, q, :], start=True, stop=True)
                    mm.then_inc(S("c_inc"), 1)

        def act_mls(act):
            def values(i):
                act.activation(c_vst[:, :, :], chunk_of(ml[:, 8:16], i), ACT.Copy).then_inc(S("c_vst"), 1)

            def chunk(i, last):
                for x in range(2):
                    act.wait_ge(S("c_d"), i * 2 + x + 1)
                    act.activation(c_B1[x][0:CH], c_B1[x][0:CH], ACT.Exp).then_inc(S("c_e"), 1)
                for x in range(2):
                    act.wait_ge(S("c_vT"), i * 2 + x + 1)
                    act.activation(c_VA[x][0:CH, :, 0:P], four(4 * x, P, CH), ACT.Copy).then_inc(S("c_va"), 1)
                if not last:
                    values(i + 1)
                for x in range(2):
                    act.wait_ge(S("c_den"), i * 2 + x + 1)
                    act.activation(c_DA[x][:, :, :], four(4 * x), ACT.Abs).then_inc(S("c_da"), 1)

            values(0)
            act_split(act, HalfBlock(HB_MLS_OUT + 1))
            with act.Fori(0, NCH - 1) as i:
                chunk(i, False)
            chunk(NCH - 1, True)

        def dve_mls(dve):
            dve_split(dve, HalfBlock(HB_MLS_OUT + 1))
            dve.sem_inc(S("c_state"), 2)
            dve.sem_inc(S("c_hs"), 2)

            def tok(i, row, x, w):
                return c_tok[0:CH, bass.ds(i, 1), row + 4 * x:row + 4 * x + 4].rearrange("p n a -> p (n a)")[:, :, None]\
                    .to_broadcast([CH, 4, w])

            with dve.Fori(0, NCH) as i:
                for x in range(2):
                    n = i * 2 + x + 1
                    dve.wait_ge(S("c_nm"), n)
                    dve.tensor_tensor(c_B1[x][0:CH], four(4 * x, CH, CH), tok(i, 0, x, CH), ALU.add).then_inc(S("c_d0"), 1)
                    dve.wait_ge(S("c_d0"), n)
                    dve.tensor_tensor(c_B1[x][0:CH], c_B1[x][0:CH], c_neg[0:CH, None, :].to_broadcast([CH, 4, CH]), ALU.add)\
                        .then_inc(S("c_d"), 1)
                    if x == 0:
                        dve.wait_ge(S("c_st"), i * 4 + 4)
                    dve.wait_ge(S("c_si"), n)
                    dve.tensor_tensor(c_QS[x][:, :, :].rearrange("p (m r) t -> p m r t", m=2),
                                      ps[:, 4 * x + 1, 0:2 * CH].rearrange("p (a t) -> p a t", a=2)[:, :, None, :].to_broadcast([P, 2, 2, CH]),
                                      c_qst[:, 4 * x:4 * x + 4, :].rearrange("p (m r) t -> p m r t", m=2), ALU.mult).then_inc(S("c_qs"), 1)
                for x in range(2):
                    n = i * 2 + x + 1
                    dve.wait_ge(S("c_qk"), n)
                    dve.wait_ge(S("c_e"), n)
                    dve.tensor_tensor(c_W[x][0:CH], four(4 * x + 3, CH, CH), c_B1[x][0:CH], ALU.mult).then_inc(S("c_w"), 1)
                    dve.wait_ge(S("c_kT"), n)
                    dve.tensor_tensor(c_KW[x][0:CH], ps[0:CH, 4 * x + 1, 0:4 * MDK].rearrange("p (a t) -> p a t", a=4),
                                      tok(i, 32, x, MDK), ALU.mult).then_inc(S("c_kw"), 1)
                for x in range(2):
                    n = i * 2 + x + 1
                    dve.wait_ge(S("c_da"), n)
                    dve.wait_ge(S("c_fl"), n)
                    dve.tensor_tensor(c_DA[x][:, :, :], four(4 * x + 2), c_DA[x][:, :, :], ALU.max).then_inc(S("c_mx"), 1)
                    dve.wait_ge(S("c_mx"), n)
                    dve.reciprocal(c_DA[x][:, :, :], c_DA[x][:, :, :]).then_inc(S("c_rc"), 1)
                    dve.wait_ge(S("c_inc"), n)
                    for m in range(2):
                        s = c_C[:, 2 * x + m, :]
                        ins = dve.scalar_tensor_tensor(s, s, c_keep[:, bass.ds(i, 1), 2 * x + m:2 * x + m + 1].rearrange("p n a -> p (n a)"),
                                                       ps[:, 4 * x + 1, m * 2 * P:(m + 1) * 2 * P], ALU.mult, ALU.add)
                    ins.then_inc(S("c_state"), 1)
                    dve.wait_ge(S("c_rc"), n)
                    dve.tensor_tensor(chunk_of(ml[:, 8 + 4 * x:12 + 4 * x], i), four(4 * x + 3), c_DA[x][:, :, :], ALU.mult)\
                        .then_inc(S("c_hs"), 1)

        def pool_mls(pool):
            def stage(i):
                pool.tensor_copy(c_rst[:, :], c_R1[:, bass.ds(i * CH, CH)]).then_inc(S("c_st"), 1)
                pool.tensor_copy(c_kst[:, :, :], chunk_of(ml[:, 4:8], i)).then_inc(S("c_st"), 1)
                pool.wait_ge(S("c_st"), i * 4 + 2)
                for y in range(2):
                    half = slice(64 * y, 64 * y + 64)
                    pool.tensor_copy(c_qst[half].rearrange("p (m r) t -> p m r t", m=4)[:, :, y, :], chunk_of(ml[half, 0:4], i))\
                        .then_inc(S("c_st"), 1)

            pool.memset(c_qst[:, :, :], 0.0)
            pool.memset(ml[:, :, T:TP], 0.0)
            stage(0)
            pool.wait_ge(S("c_st"), 4)
            pool_mls_state(pool)
            with pool.Fori(0, NCH - 1) as i:
                pool.wait_ge(S("c_kT"), i * 2 + 2)
                stage(i + 1)

        def act_mls_out(act):
            for t in range(8):
                act.wait_ge(S("gated_y"), t + 1)
                act.activation(flat(xb_hi[:, t], LATE), flat(mh_y[:, t % 2], LATE), ACT.Copy).then_inc(S("gated_hi"), 1)
            act_mod(act)
            act_down(act, HalfBlock(HB_MLS_OUT), 3, LATE, ("out_ev", 2))

        def dve_mls_out(dve):
            dve.sem_inc(S("out_ev"), 2)
            dve.wait_ge(S("head_out"), 40 + 2)
            for t in range(8):
                if t >= 2:
                    dve.wait_ge(S("gated_lo"), t - 1)
                dve.tensor_tensor(flat(mh_y[:, t % 2], LATE), ml[:, 8 + t, N_META:T], ml[:, 16 + t, N_META:T], ALU.mult)\
                    .then_inc(S("gated_y"), 1)
                dve.wait_ge(S("gated_hi"), t + 1)
                dve.tensor_tensor(flat(xb_lo[:, t], LATE), flat(mh_y[:, t % 2], LATE), flat(xb_hi[:, t], LATE).bitcast(F32),
                                  ALU.subtract).then_inc(S("gated_lo"), 1)
            for j in range(4):
                dve_down(dve, "out_ev", HalfBlock(HB_MLS_OUT + j), j, LATE, split=j < 3)

        def pe_mls_out(pe):
            for j in range(4):
                pe_hb(pe, HalfBlock(HB_MLS_OUT + j), xb_hi, xb_lo, LATE, "out_ev", 2 * j, per_k=("gated_lo", 0) if j == 0 else None)

        TOK = [(0, 0, SEQ)]
        CTXP = [(0, 0, CTX)]
        b2_r = Region(SB_G, SB_END)
        b_rope = b2_r.take("b_rope", [P, 4, SEQ])
        b2_r = Region(SB_G + 4 * 2 * T * 2, SB_END)
        b_q = b2_r.take("b_q", [P, RH, SEQ])
        b_kv = b2_r.take("b_kv", [P, RH, 2 * KEYS])
        b_g = b2_r.take("b_g", [P, RH, SEQ])
        b_qk = b2_r.take("b_qk", [P, 6, SEQ])
        b_av = b2_r.take("b_av", [P, KEYS])
        b_ctx_at = b2_r.next
        b_ctx = b2_r.take("b_ctx", [P, KT, CTX])
        b_mod = b2_r.take("b_mod", [P, MOD_GROUPS, 12])
        b_modc = b2_r.take("b_modc", [P, MOD_GROUPS, 4])
        mod_r = b2_r.take("mod_r", [P, 16])
        b_gain = b2_r.take("b_gain", [P, 3, KT])
        bc_r = Region(b_ctx_at, b_ctx_at + KT * CTX * 4)
        b_pos = bc_r.take("b_pos", [P, 2, SEQ])
        b_lpos = bc_r.take("b_lpos", [P, 2, 2])
        b_dec = bc_r.take("b_dec", [P, 2, RH, 2])
        b_lg = bc_r.take("b_lg", [P, 2 * RH])
        b_e, b_s, b_big = (bc_r.take("b_" + n, [P, 2 * RH]) for n in ("e", "s", "big"))
        b_half = bc_r.take("b_half", [P, 2])
        md_r = Region(SB_G + (KT + 6) * T * 4, SB_END)
        mod_w = md_r.take("mod_w", [P, 3, 2, D])
        mod_c = md_r.take("mod_c", [P, 2, D])
        mod_x = at("mod_x", [P, 2, D], SB_G)
        assert md_r.next <= b_ctx_at
        ctx_sq = at("ctx_sq", [P, KT, CTX], SB_G + (KT + 6) * T * 4)
        bc_hi = at("bc_hi", [P, KT, CTX], SB_XB, F32R)
        bc_lo = at("bc_lo", [P, KT, CTX], SB_XB + KT * CTX * 4, F32R)
        bt_r = Region(SB_XB + 2 * KT * CTX * 4, SB_G)
        b_tau = bt_r.take("b_tau", [P, 2, SEQ + 3 * P])
        b_perm = bt_r.take("b_perm", [P, 2, P])
        r_qd = [[bt_r.take(f"r_qd{x}{d}", [P, SEQ]) for d in range(2)] for x in range(2)]
        r_w = [at(f"r_w{x}", [P, 4, SEQ], SB_XB + x * 4 * SEQ * 4) for x in range(2)]
        rt_r = Region(SB_XA, SB_XB)
        r_st, r_tt, r_vT, r_ck, r_cv, r_S = ([rt_r.take(f"r_{n}{x}", [P] + w) for x in range(2)]
                                             for n, w in (("st", [2 * KEYS]), ("tt", [SEQ + 3 * P]), ("vT", [4, P]), ("ck", [2, 2, P]),
                                                          ("cv", [2, P]), ("S", [2, P])))
        rr_r = Region(SB_XA, SB_XB)
        rope_c = rr_r.take("rope_c", [P, 2, SEQ])
        rope_s = rr_r.take("rope_s", [P, 2, SEQ])
        hn_roots = head_roots("hn", rr_r.next)
        hn_sq = rr_r.take("hn_sq", [P, 6, T])
        hn_st = [rr_r.take(f"hn_st{c}", [P, P], F32R) for c in range(2)]
        ret_y = at("ret_y", [P, SEQ], SB_G)
        aa_r = Region(SB_XA, SB_XB)
        a_kd = aa_r.take("a_kd", [P, AKV, KEYS])
        a_vt = aa_r.take("a_vt", [P, KEYS // P, P])
        a_qst = [aa_r.take(f"a_qst{y}", [P, SEQ]) for y in range(2)]
        a_vst = aa_r.take("a_vst", [P, KEYS // P, AHD])
        a_p = [aa_r.take(f"a_p{c}", [P, KEYS]) for c in range(2)]
        a_mx, a_nm, a_sum, a_inv = ([aa_r.take(f"a_{n}{c}", [P, 1]) for c in range(2)] for n in ("mx", "nm", "sum", "inv"))
        a_pT = [at(f"a_pT{y}", [P, KEYS // P, SEQ], SB_G + 4 * 2 * T * 2 + RH * SEQ * 4 + y * KEYS // P * SEQ * 4) for y in range(2)]

        MOD_SUMS = 16
        MOD_LOADS = 6

        def act_mod(act):
            act.dma_start(b_ctx[:, :, :], A["ctx_in"]).then_inc(S("in"), 16)
            act.dma_start(mod_c[:, :, :], A["c_in"]).then_inc(S("in"), 16)

        def act_mod_c(act):
            act.wait_ge(S("in"), IN_FIRST + 32 + 48 + 32)
            act.activation(mod_c[:, :, :], mod_c[:, :, :], ACT.Silu).then_inc(S("mod_c"), 1)

        def mod_sums_before(m):
            return 4 * m if m < 2 else 2 * m + 4

        def act_mod_load(act, i, j):
            if j < MOD_LOADS:
                if j >= 3:
                    act.wait_ge(S("mod_sum"), i * MOD_SUMS + (mod_sums_before(j - 2) + 4))
                else:
                    act.wait_ge(S("mod_sum"), i * MOD_SUMS + (mod_sums_before(j + 4) - MOD_SUMS + 4))
                act.dma_start(mod_w[:, j % 3].rearrange("p a n -> p (a n)"),
                              A["weights_mod"][bass.ds(i * MOD_LOADS + j, 1), :, :].rearrange("a p n -> (a p) n"))\
                    .then_inc(S(f"mod_w{j % 3}"), 16)

        def dve_mod_start(dve):
            dve.sem_inc(S("mod_sum"), 4)
            dve.wait_ge(S("mod_c"), 1)

        def dve_mod_sums(dve, i, j):
            m = j // 2 if j < 4 else j - 2
            if j >= 4 or j % 2 == 0:
                dve.wait_ge(S(f"mod_w{m % 3}"), i * 32 + 16 * (m // 3 + 1))
            for x in range(2):
                c, who = (j % 2, x) if j < 4 else (x, 0)
                n = 2 * j + x
                to = 12 + 2 * m + c if who else 2 * m + c
                dve.wait_ge(S("mod_sum"), i * MOD_SUMS + (n + 3))
                dve.scalar_tensor_tensor(mod_x[:, n % 2] if j < 4 else mod_w[:, m % 3, c], mod_w[:, m % 3, c], 1.0, mod_c[:, who], ALU.mult, ALU.mult,
                                         accum_out=mod_r[:, to:to + 1]).then_inc(S("mod_sum"), 1)
            if j == 7:
                dve.wait_ge(S("mod_sum"), i * MOD_SUMS + (MOD_SUMS + 4))
                bias = prm("b_mod").rearrange("p (g n) -> p g n", g=MOD_GROUPS)[:, bass.ds(i, 1), :].rearrange("p a n -> p (a n)")
                dve.tensor_tensor(b_mod[:, bass.ds(i, 1), :].rearrange("p a n -> p (a n)"), mod_r[:, 0:12], bias, ALU.add)\
                    .then_inc(S("mod_d"), 1)
                dve.tensor_tensor(b_modc[:, bass.ds(i, 1), :].rearrange("p a n -> p (a n)"), mod_r[:, 12:16], bias[:, 0:4], ALU.add)\
                    .then_inc(S("mod_d"), 1)

        def mod_tiles(what):
            if what in ("shift1", "scale1"):
                g = 0 if what == "shift1" else 2
                return b_mod[:, g:g + 2, 0:4]
            return b_mod[:, ["gate1", "shift2", "scale2", "gate2"].index(what), None, 4:12]

        def mod_col(what, k):
            x = mod_tiles(what)
            w = x.shape[2]
            return x[:, k // w, k % w:k % w + 1]

        def ctx_shift(k):
            return b_modc[:, k // 4, k % 4:k % 4 + 1]

        def gain_col(n, k):
            return b_gain[:, n, k:k + 1]

        def dve_mod(dve):
            dve.wait_ge(S("mod_d"), 2 * MOD_GROUPS)
            for n, (scale, g) in enumerate(((mod_tiles("scale1"), "norm1_g"), (b_modc[:, 2:4, :], "norm1_g"), (mod_tiles("scale2"), "norm2_g"))):
                w = scale.shape[2]
                dve.scalar_tensor_tensor(b_gain[:, n, :].rearrange("p (a b) -> p a b", b=w), scale, 1.0,
                                         prm(g).rearrange("p (a b) -> p a b", b=w), ALU.add, ALU.mult).then_inc(S("mod_d"), 1)
            dve.wait_ge(S("mod_d"), 2 * MOD_GROUPS + 3)

        N_IN_BEFORE = 2 * N_MLS_IN

        def pe_b2_in(pe):
            ctx_of = (bc_hi, bc_lo, CTX)
            pe_hb(pe, HalfBlock(HB_B2_IN), xa_hi, xa_lo, LATE, "in_ev", N_IN_BEFORE, per_k=("norm_lo", 5 * KT))
            pe_norm(pe, (5, 6), CTXP, sq=ctx_sq, to=5)
            pe_hb(pe, HalfBlock(HB_B2_IN + 1), xa_hi, xa_lo, LATE, "in_ev", N_IN_BEFORE + 2)
            pe.wait_ge(S("norm_lo"), 7 * KT)
            with pe.Fori(0, 2) as i:
                for s in range(2):
                    pe_hb(pe, HalfBlock(HB_B2_IN + 2, i, 2).after(s), xa_hi, xa_lo, LATE, "in_ev", i * 4 + (N_IN_BEFORE + 4 + 2 * s), extra=ctx_of)
            with pe.Fori(0, 2) as i:
                for s in range(2):
                    pe_hb(pe, HalfBlock(HB_B2_IN + 6, i, 2).after(s), xa_hi, xa_lo, LATE, "in_ev", i * 4 + (N_IN_BEFORE + 12 + 2 * s))
            pe_hb(pe, HalfBlock(HB_B2_IN + 10), xa_hi, xa_lo, LATE, "in_ev", N_IN_BEFORE + 20, extra=ctx_of)

        def act_b2_loads(act):
            for n, (to, name) in enumerate(((b_rope, "rope"), (b_tau, "tau"), (b_perm, "perm"), (b_pos, "pos"),
                                            (b_lpos, "lpos"), (b_half, "half"))):
                act.dma_start(to[:, :, :] if len(to.shape) == 3 else to[:, :], A[name]).then_inc(S("in"), 16)

        def act_b2_in(act, first, last):
            for t in range(first, last):
                n, func, scale, ctx_to = t % 4, ACT.Copy, 1.0, None
                if t < 4:
                    to, scale = b_q[:, n, :], P ** -0.5
                elif t < 8:
                    to, ctx_to = b_kv[:, n, 0:SEQ], b_kv[:, n, 2 * SEQ:2 * SEQ + CTX]
                elif t < 12:
                    to, ctx_to = b_kv[:, n, SEQ:2 * SEQ], b_kv[:, n, 2 * SEQ + CTX:2 * KEYS]
                elif t < 16:
                    to, func = b_g[:, n, :], ACT.Silu
                elif t < 20:
                    to = b_qk[:, n, :]
                elif t == 20:
                    to, ctx_to = b_qk[:, 4, :], b_qk[:, 5, 0:CTX]
                else:
                    to, ctx_to = b_av[:, CTX:KEYS], b_av[:, 0:CTX]
                act.wait_ge(S("tiles_done"), (HB_B2_IN * 2 + t + 1))
                if ctx_to is not None:
                    act.activation(ctx_to, ps[:, 2 * (t % 2) + 1, 0:CTX], ACT.Copy)
                act.activation(to, ps[:, 2 * (t % 2), :], func, scale=scale).then_inc(S("in_ev"), 1)
                if t % 2 and t < 2 * N_B2_IN - 1:
                    act_split(act, HalfBlock(HB_B2_IN + t // 2 + 2))

        def dve_b2_in(dve):
            for j in range(N_B2_IN - 1):
                dve_split(dve, HalfBlock(HB_B2_IN + j + 2))

        def pool_b2_in(pool):
            pool.memset(b_qk[:, 5, CTX:SEQ], 0.0)

        MLS_A, MLS_D = GDN_A + 9, GDN_D + 27

        def act_decays(act):
            act.wait_ge(S("in"), IN_ALL)
            act.activation(b_e[:, :], prm("ret_rate"), ACT.Exp).then_inc(S("gates_a"), 1)
            act.wait_ge(S("gates_a"), MLS_A + 1)
            act.activation(b_lg[:, :], b_e[:, :], ACT.Ln, bias=1.0, scale=-1.0).then_inc(S("gates_a"), 1)
            act.wait_ge(S("gates_d"), MLS_D + N_SERIES + 6)
            act.activation(b_dec[:, :, :, :], b_dec[:, :, :, :], ACT.Exp).then_inc(S("gates_a"), 1)

        N_SERIES = 8

        def dve_decays(dve):
            dve.wait_ge(S("in"), IN_ALL)
            dve.wait_ge(S("gates_a"), MLS_A + 2)
            dve.tensor_scalar(b_big[:, :], b_e[:, :], 0.0625, None, ALU.is_ge).then_inc(S("gates_d"), 1)
            dve.tensor_scalar(b_s[:, :], b_e[:, :], 1.0 / N_SERIES, None, ALU.mult).then_inc(S("gates_d"), 1)
            for n in range(N_SERIES - 1, 0, -1):
                dve.wait_ge(S("gates_d"), MLS_D + N_SERIES - n + 1)
                dve.scalar_tensor_tensor(b_s[:, :], b_s[:, :], 1.0 / n, b_e[:, :], ALU.add, ALU.mult).then_inc(S("gates_d"), 1)
            dve.wait_ge(S("gates_d"), MLS_D + N_SERIES + 1)
            dve.tensor_tensor(b_lg[:, :], b_lg[:, :], b_s[:, :], ALU.add).then_inc(S("gates_d"), 1)
            dve.wait_ge(S("gates_d"), MLS_D + N_SERIES + 2)
            dve.tensor_tensor(b_lg[:, :], b_lg[:, :], b_big[:, :], ALU.mult).then_inc(S("gates_d"), 1)
            dve.wait_ge(S("gates_d"), MLS_D + N_SERIES + 3)
            dve.tensor_tensor(b_lg[:, :], b_lg[:, :], b_s[:, :], ALU.subtract).then_inc(S("gates_d"), 1)
            dve.wait_ge(S("gates_d"), MLS_D + N_SERIES + 4)
            for d in range(2):
                dve.tensor_tensor(b_dec[:, d], b_lg[:, d * RH:(d + 1) * RH, None].to_broadcast([P, RH, 2]),
                                  b_lpos[:, d, None, :].to_broadcast([P, RH, 2]), ALU.mult).then_inc(S("gates_d"), 1)

        ROPES = [(b_q[:, t, :], 0) for t in range(RH)] + [(b_kv[:, t, 0:SEQ], 0) for t in range(RH)] + \
                [(b_qk[:, t, :], 1) for t in range(5)]

        def pe_rope(pe):
            for t, (x, kind) in enumerate(ROPES):
                if t >= 4:
                    pe.wait_ge(S("rope_s"), t - 3)
                pe.matmul(ps[:, t % 4, :], b_perm[:, kind, :], x, start=True, stop=True).then_inc(S("rope_x"), 1)

        def pool_rope(pool):
            for t, (x, kind) in enumerate(ROPES):
                if t >= 2:
                    pool.wait_ge(S("rope_o"), t - 1)
                pool.tensor_tensor(rope_c[:, t % 2], x, b_rope[:, 2 * kind], ALU.mult).then_inc(S("rope_c"), 1)

        def dve_rope(dve):
            for t, (x, kind) in enumerate(ROPES):
                dve.wait_ge(S("rope_x"), t + 1)
                if t >= 2:
                    dve.wait_ge(S("rope_o"), t - 1)
                dve.tensor_tensor(rope_s[:, t % 2], ps[:, t % 4, :], b_rope[:, 2 * kind + 1], ALU.mult).then_inc(S("rope_s"), 1)
                dve.wait_ge(S("rope_s"), t + 1)
                dve.wait_ge(S("rope_c"), t + 1)
                dve.tensor_tensor(x, rope_c[:, t % 2], rope_s[:, t % 2], ALU.add).then_inc(S("rope_o"), 1)

        def pool_ret(pool):
            with pool.Fori(0, RH // 2) as i:
                for x in range(2):
                    q = b_q[:, bass.ds(i * 2 + x, 1), :].rearrange("p a t -> p (a t)")
                    pool.wait_ge(S("r_qe"), i * 4 + (2 * x + 2))
                    pool.sem_inc(S("pool_steps"), 1)
                    for d in range(2):
                        pool.tensor_tensor(r_qd[x][d][:, :], r_qd[x][d][:, :], q, ALU.mult).then_inc(S("r_qd"), 1)

        def act_ret(act):
            act.sem_inc(S("r_out"), 2)
            with act.Fori(0, RH // 2) as i:
                for x in range(2):
                    act.wait_ge(S("r_o"), i * 2 + (x + 1))
                    for d in range(2):
                        act.activation(r_qd[x][d][:, :], b_pos[:, d, :], ACT.Exp, scale=b_lg[:, bass.ds(i * 2 + (RH * d + x), 1)])\
                            .then_inc(S("r_qe"), 1)
                    act.wait_ge(S("r_t"), i * 2 + (x + 1))
                    act.activation(r_tt[x][:, :], r_tt[x][:, :], ACT.Exp).then_inc(S("r_te"), 1)
                for x in range(2):
                    act.wait_ge(S("r_vT"), i * 2 + (x + 1))
                    act.activation(r_vT[x][:, :, :], ps[:, 4 * x, :].rearrange("p (a t) -> p a t", a=4), ACT.Copy).then_inc(S("r_v"), 1)
                for x in range(2):
                    act.wait_ge(S("r_sd"), i * 2 + (x + 1))
                    act.activation(r_S[x][:, :, :], ps[:, 4 * x, 0:2 * P].rearrange("p (a t) -> p a t", a=2), ACT.Copy).then_inc(S("r_S"), 1)
                for x in range(2):
                    fixed_wait(act)
                    act.wait_ge(S("r_o"), i * 2 + (x + 3))
                    act.activation(b_q[:, bass.ds(i * 2 + x, 1), :].rearrange("p a t -> p (a t)"), ps[:, 4 * x + 1, :], ACT.Copy)\
                        .then_inc(S("r_out"), 1)

        def dve_ret(dve):
            with dve.Fori(0, RH // 2) as i:
                for x in range(2):
                    fixed_wait(dve)
                    dve.wait_ge(S("r_o"), i * 2 + (x + 1))
                    dve.tensor_copy(r_st[x][:, :], b_kv[:, bass.ds(i * 2 + x, 1), :].rearrange("p a t -> p (a t)")).then_inc(S("r_st"), 1)
                for x in range(2):
                    lg = [b_lg[:, bass.ds(i * 2 + (RH * d + x), 1)] for d in range(2)]
                    dve.wait_ge(S("r_o"), i * 2 + (x + 1))
                    dve.tensor_scalar(r_tt[x][:, :], b_tau[:, 0, :], lg[0], None, ALU.mult).then_inc(S("r_t0"), 1)
                    dve.wait_ge(S("r_t0"), i * 2 + (x + 1))
                    dve.scalar_tensor_tensor(r_tt[x][:, :], b_tau[:, 1, :], lg[1], r_tt[x][:, :], ALU.mult, ALU.add).then_inc(S("r_t"), 1)
                for x in range(2):
                    c = ps[:, 4 * x + 1, :].rearrange("p (a l t) -> p a l t", a=2, l=2)
                    dve.wait_ge(S("r_cT"), i * 2 + (x + 1))
                    for d in range(2):
                        w = b_dec[:, d, bass.ds(i * 2 + x, 1), :].rearrange("p a l -> p (a l)")[:, :, None].to_broadcast([P, 2, P])
                        dve.tensor_tensor(r_ck[x][:, d], c[:, 0], w, ALU.mult)
                    dve.tensor_copy(r_cv[x][:, :, :], c[:, 1]).then_inc(S("r_c"), 1)
                    dve.wait_ge(S("r_te"), i * 2 + (x + 1))
                    dve.tensor_tensor(r_tt[x][:, 3 * P:4 * P], r_tt[x][:, 3 * P:4 * P], ident[:, :], ALU.add).then_inc(S("r_tab"), 1)
                for j in range(4):
                    for x in range(2):
                        dve.wait_ge(S("r_s"), i * 8 + (2 * j + x + 1))
                        if j == 0:
                            dve.wait_ge(S("r_tab"), i * 2 + (x + 1))
                        dve.tensor_tensor(r_w[x][:, j, :], ps[:, 4 * x + 2 + j % 2, :], r_tt[x][:, (3 - j) * P:(3 - j) * P + SEQ], ALU.mult)\
                            .then_inc(S("r_w"), 1)

        def pe_ret(pe):
            pe.sem_inc(S("r_o"), 2)
            with pe.Fori(0, RH // 2) as i:
                for x in range(2):
                    pe.wait_ge(S("r_st"), i * 2 + (x + 1))
                    if x == 0:
                        pe.wait_ge(S("r_out"), i * 2 + 2)
                    for j in range(4):
                        mm = pe.transpose(ps[:, 4 * x, j * P:(j + 1) * P], r_st[x][:, SEQ + j * P:SEQ + (j + 1) * P], ident[:, :])
                    mm.then_inc(S("r_vT"), 1)
                    for j in range(4):
                        mm = pe.transpose(ps[:, 4 * x + 1, j * P:(j + 1) * P], r_st[x][:, 2 * SEQ + j * P:2 * SEQ + (j + 1) * P], ident[:, :])
                    mm.then_inc(S("r_cT"), 1)
                for j in range(4):
                    for x in range(2):
                        if j >= 2:
                            pe.wait_ge(S("r_w"), i * 8 + (2 * (j - 2) + x + 1))
                        pe.matmul(ps[:, 4 * x + 2 + j % 2, :], r_st[x][:, j * P:(j + 1) * P],
                                  b_q[:, bass.ds(i * 2 + x, 1), :].rearrange("p a t -> p (a t)"), start=True, stop=True).then_inc(S("r_s"), 1)
                    if j == 1:
                        for x in range(2):
                            pe.wait_ge(S("r_v"), i * 2 + (x + 1))
                            pe.wait_ge(S("r_c"), i * 2 + (x + 1))
                            for d in range(2):
                                for l in range(2):
                                    mm = pe.matmul(ps[:, 4 * x, d * P:(d + 1) * P], r_ck[x][:, d, l, :], r_cv[x][:, l, :],
                                                   start=(l == 0), stop=(l == 1))
                            mm.then_inc(S("r_sd"), 1)
                for x in range(2):
                    pe.wait_ge(S("r_S"), i * 2 + (x + 1))
                    pe.wait_ge(S("r_qd"), i * 4 + (2 * x + 2))
                    for d in range(2):
                        pe.matmul(ps[:, 4 * x + 1, :], r_S[x][:, d, :], r_qd[x][d][:, :], start=(d == 0), stop=False)
                    for j in range(4):
                        pe.wait_ge(S("r_w"), i * 8 + (2 * j + x + 1))
                        mm = pe.matmul(ps[:, 4 * x + 1, :], r_vT[x][:, j, :], r_w[x][:, j, :], start=False, stop=(j == 3))
                    mm.then_inc(S("r_o"), 1)

        def pe_centre(pe):
            for t in range(RH):
                pe.matmul(ps[:, t, :], ones[:, :], b_q[:, t, :], start=True, stop=True).then_inc(S("rn_sum"), 1)

        def dve_centre(dve):
            for t in range(RH):
                dve.wait_ge(S("rn_sum"), t + 1)
                dve.scalar_tensor_tensor(b_q[:, t, :], ps[:, t, :], -1.0 / P, b_q[:, t, :], ALU.mult, ALU.add).then_inc(S("rn_c"), 1)
            dve.wait_ge(S("rn_c"), RH)

        HEAD_TILES = 50

        def pe_att_keys(pe):
            for t in range(KEYS // P):
                mm = pe.transpose(ps[:, t // 4, (t % 4) * P:(t % 4 + 1) * P], b_av[:, t * P:(t + 1) * P], ident[:, :])
            mm.then_inc(S("at_vT"), 1)

        def act_att_keys(act):
            for kv in range(AKV):
                for y in range(2):
                    to, at_ = slice(64 * y, 64 * y + 64), slice(64 * kv, 64 * kv + 64)
                    act.activation(a_kd[to, kv, 0:CTX], b_qk[at_, 5, 0:CTX], ACT.Copy)
                    act.activation(a_kd[to, kv, CTX:KEYS], b_qk[at_, 4, :], ACT.Copy)
            act.wait_ge(S("at_vT"), 1)
            for n, m in ((0, 4), (1, 2)):
                act.activation(a_vt[:, 4 * n:4 * n + m, :], ps[:, n, 0:m * P].rearrange("p (a t) -> p a t", a=m), ACT.Copy).then_inc(S("at_keys"), 1)

        UNITS = [(y, b) for y in range(2) for b in range(4)]

        def pool_att(pool):
            pool.wait_ge(S("at_keys"), 2)
            with pool.Fori(0, AKV) as kv:
                with pool.Fori(0, 2) as m:
                    it = kv * 2 + m
                    pool.wait_ge(S("at_s"), it * 8)
                    pool.sem_inc(S("pool_steps"), 1)
                    for y in range(2):
                        pool.tensor_tensor(a_qst[y][:, :], b_qk[:, bass.ds(it, 1), :].rearrange("p a t -> p (a t)"),
                                           b_half[:, y:y + 1].to_broadcast([P, SEQ]), ALU.mult).then_inc(S("at_q"), 1)
                    pool.wait_ge(S("at_o"), it * 2 + 2)
                    pool.sem_inc(S("pool_steps"), 1)
                    pool.tensor_copy(a_vst[:, :, :], a_vt[:, :, bass.ds(kv * AHD, AHD)]).then_inc(S("at_q"), 1)

        def pe_att(pe):
            pe.wait_ge(S("at_keys"), 2)
            pe.sem_inc(S("at_o"), 2)
            pe.sem_inc(S("at_T"), 2)
            with pe.Fori(0, AKV) as kv:
                with pe.Fori(0, 2) as m:
                    it = kv * 2 + m

                    def scores(u):
                        y, b = UNITS[u]
                        pe.wait_ge(S("at_q"), it * 3 + (1 if u < 4 else 2))
                        pe.wait_ge(S("at_e"), it * 8 + (u + 1))
                        for n in range(2):
                            mm = pe.matmul(ps[:, 2 * (u % 2) + n, 0:KEYS // 2], a_qst[y][:, b * P:(b + 1) * P],
                                           a_kd[:, bass.ds(kv, 1), n * (KEYS // 2):(n + 1) * (KEYS // 2)].rearrange("p a t -> p (a t)"),
                                           start=True, stop=True)
                        mm.then_inc(S("at_s"), 1)

                    def transposes(u):
                        pe.wait_ge(S("at_n"), it * 8 + (u + 1))
                        pe.wait_ge(S("at_pT"), it * 8 + (u + 1))
                        for t in range(KEYS // P):
                            mm = pe.transpose(ps[:, 4 + t // 3, (t % 3) * P:(t % 3 + 1) * P], a_p[u % 2][:, t * P:(t + 1) * P], ident[:, :])
                        mm.then_inc(S("at_T"), 1)

                    def values(y):
                        pe.wait_ge(S("at_q"), it * 3 + 3)
                        pe.wait_ge(S("at_pT"), it * 8 + (4 * y + 5))
                        if y == 0:
                            pe.wait_ge(S("at_lo"), it + 1)
                        for t in range(KEYS // P):
                            mm = pe.matmul(ps[64 * y:64 * y + 64, 6, :], a_vst[:, t, :], a_pT[y][:, t, :], start=(t == 0), stop=(t == KEYS // P - 1))
                        mm.then_inc(S("at_o"), 1)

                    scores(0)
                    scores(1)
                    for u in range(8):
                        if u < 6:
                            scores(u + 2)
                        transposes(u)
                        if u in (4, 7):
                            values(u // 7)

        def act_att(act):
            act.sem_inc(S("at_e"), 2)
            act.sem_inc(S("at_pT"), 1)
            with act.Fori(0, AKV) as kv:
                with act.Fori(0, 2) as m:
                    it = kv * 2 + m

                    def exps(u):
                        act.wait_ge(S("at_m"), it * 8 + (u + 1))
                        act.wait_ge(S("at_T"), it * 8 + (u + 1))
                        act.activation(a_p[u % 2][:, :].rearrange("p (a t) -> p a t", a=2), ps[:, 2 * (u % 2):2 * (u % 2) + 2, 0:KEYS // 2], ACT.Exp,
                                       bias=a_nm[u % 2][:, 0:1], scale=AHD ** -0.5, accum_out=a_sum[u % 2][:, 0:1]).then_inc(S("at_e"), 1)

                    exps(0)
                    for u in range(8):
                        if u < 7:
                            exps(u + 1)
                        if u == 3:
                            fixed_wait(act)
                            act.wait_ge(S("gated_y"), it + (KT + 1))
                            act.activation(flat(xb_hi[:, bass.ds(it, 1)].rearrange("p a t -> p (a t)"), LATE), ret_y[:, :], ACT.Copy)\
                                .then_inc(S("gated_hi"), 1)
                        y, b = UNITS[u]
                        act.wait_ge(S("at_T"), it * 8 + (u + 3))
                        if b == 0:
                            act.wait_ge(S("at_o"), it * 2 + (y + 1))
                        act.activation(a_pT[y][:, :, b * P:(b + 1) * P].rearrange("p (n a) t -> p n a t", n=2),
                                       ps[:, 4:6, 0:KEYS // 2].rearrange("p n (a t) -> p n a t", t=P), ACT.Copy).then_inc(S("at_pT"), 1)
                    fixed_wait(act)
                    act.wait_ge(S("at_o"), it * 2 + 4)
                    act.activation(flat(xb_hi[:, bass.ds(it + RH, 1)].rearrange("p a t -> p (a t)"), LATE), ps[:, 6, :], ACT.Copy)\
                        .then_inc(S("at_hi"), 1)

        def dve_att(dve):
            dve.sem_inc(S("at_lo"), 1)
            dve.wait_ge(S("head_out"), HEAD_TILES + 2)
            with dve.Fori(0, AKV) as kv:
                with dve.Fori(0, 2) as m:
                    it = kv * 2 + m
                    for u in range(9):
                        if u == 2:
                            fixed_wait(dve)
                            dve.wait_ge(S("gated_lo"), it + KT)
                            dve.tensor_tensor(ret_y[:, :], b_q[:, bass.ds(it, 1), :].rearrange("p a t -> p (a t)"),
                                              b_g[:, bass.ds(it, 1), :].rearrange("p a t -> p (a t)"), ALU.mult).then_inc(S("gated_y"), 1)
                        if u == 6:
                            dve.wait_ge(S("gated_hi"), it + (KT + 1))
                            dve.tensor_tensor(flat(xb_lo[:, bass.ds(it, 1)].rearrange("p a t -> p (a t)"), LATE), ret_y[:, :],
                                              flat(xb_hi[:, bass.ds(it, 1)].rearrange("p a t -> p (a t)"), LATE).bitcast(F32), ALU.subtract)\
                                .then_inc(S("gated_lo"), 1)
                        if u < 8:
                            c = u % 2
                            dve.wait_ge(S("at_s"), it * 8 + (u + 1))
                            dve.tensor_reduce(a_mx[c][:, 0:1], ps[:, 2 * c:2 * c + 2, 0:KEYS // 2], mybir.AxisListType.XY, ALU.max)\
                                .then_inc(S("at_mx"), 1)
                            dve.wait_ge(S("at_mx"), it * 8 + (u + 1))
                            dve.tensor_scalar(a_nm[c][:, 0:1], a_mx[c][:, 0:1], -AHD ** -0.5, None, ALU.mult).then_inc(S("at_m"), 1)
                        if u:
                            c = (u - 1) % 2
                            dve.wait_ge(S("at_e"), it * 8 + (u + 2))
                            dve.reciprocal(a_inv[c][:, 0:1], a_sum[c][:, 0:1]).then_inc(S("at_r"), 1)
                            dve.wait_ge(S("at_r"), it * 8 + u)
                            dve.tensor_scalar(a_p[c][:, :], a_p[c][:, :], a_inv[c][:, 0:1], None, ALU.mult).then_inc(S("at_n"), 1)
                    dve.wait_ge(S("at_hi"), it + 1)
                    lo = flat(xb_lo[:, bass.ds(it + RH, 1)].rearrange("p a t -> p (a t)"), LATE)
                    hi = flat(xb_hi[:, bass.ds(it + RH, 1)].rearrange("p a t -> p (a t)"), LATE)
                    dve.tensor_tensor(lo, ps[:, 6, :], hi.bitcast(F32), ALU.subtract).then_inc(S("at_lo"), 1)

        def pe_b2_out(pe):
            for j in range(4):
                pe_hb(pe, HalfBlock(HB_B2_OUT + j), xb_hi, xb_lo, LATE, "out_ev", KT + 2 * j)

        def act_b2_out(act):
            act_down(act, HalfBlock(HB_B2_OUT), 6, LATE, ("out_ev", KT + 2))

        def dve_b2_out(dve):
            for j in range(4):
                dve_down(dve, "out_ev", HalfBlock(HB_B2_OUT + j), j, LATE, lambda k: mod_col("gate1", k), split=j < 3)

        def dve_final(dve):
            dve_norm_stats(dve, (7, None), LATE)
            for k in range(KT):
                x = cols(h[:, k], LATE)
                dve.scalar_tensor_tensor(x, x, prm("final_g", k), root(LATE), ALU.mult, ALU.mult).then_inc(S("norm_y"), 1)

        def sp_final(sp):
            for k in range(KT):
                sp.wait_ge(S("norm_y"), 8 * KT + k + 1)
                sp.dma_start(out[:, k, :], flat(h[:, k], LATE)).then_inc(S("out"), 16)
            sp.wait_ge(S("out"), 16 * KT)

        @block.sync
        def _(sp):
            def load(turn, slot, index):
                sp.dma_start(raw[:, slot].rearrange("p k c -> p (k c)"), A["weights"][bass.ds(index, 1), :, :].rearrange("a p n -> (a p) n"))\
                    .then_inc(S(f"w_raw{slot}"), 16)
            sp.dma_start(ident[:, :], A["ident"]).then_inc(S("in"), 16)
            sp.dma_start(par[:, :], A["params"]).then_inc(S("in"), 16)
            load(0, 0, 0)
            load(0, 1, 1)
            with sp.Fori(1, N_HB // 2) as i:
                for s in range(2):
                    sp.wait_ge(S("w_lo"), i * 2 + (s - 1))
                    load(i, s, i * 2 + s)
            if N_HB % 2:
                sp.wait_ge(S("w_lo"), N_HB - 2)
                load(N_HB // 2, 0, N_HB - 1)
            sp_final(sp)

        @block.gpsimd
        def _(pool):
            st = Stages(pool, "POOL")
            pool.memset(ones[:, :], 1.0).then_inc(S("set"), 1)
            pool.memset(conv_in[:, :, 0:3], 0.0).then_inc(S("set"), 1)
            for step in [
                lambda: (pool_gdn_gates(pool), pool_norm(pool, 0, FULL)),
                lambda: (pool.memset(qkv[:, :, T:TP], 0.0).then_inc(S("set"), 1), pool.memset(g_S[:, :, :], 0.0).then_inc(S("set"), 1)),
                lambda: pool_gdn(pool),
                lambda: (pool_norm(pool, 1, FULL), pool_norm(pool, 2, FULL), pool_mls_gates(pool)),
                lambda: pool_mls(pool),
                lambda: (pool_norm(pool, 3, LATE), pool_norm(pool, 4, LATE), pool_norm(pool, 5, CTXP, sq=ctx_sq), pool_b2_in(pool)),
                lambda: None,
                lambda: pool_rope(pool),
                lambda: pool_ret(pool),
                lambda: None,
                lambda: pool_att(pool),
                lambda: (pool_norm(pool, 6, LATE), pool_norm(pool, 7, LATE)),
            ]:
                step()
                st.end()

        @block.scalar
        def _(act):
            st = Stages(act, "ACT")
            act.dma_start(h[:, :, :], A["x_in"]).then_inc(S("x_in"), 16)
            act.sem_inc(S("conv_x"), 2)
            act.sem_inc(S("in_ev"), 2)
            act.wait_ge(S("x_in"), 16)
            act_squares(act, 0, h, FULL)
            act.wait_ge(S("in"), IN_FIRST)
            act_split(act, HalfBlock(0))
            act_split(act, HalfBlock(1))
            for step in [
                lambda: (act_norm(act, (0, 0), FULL), act_gdn_in(act)),
                lambda: (act_gdn_masks(act), act_split(act, HalfBlock(HB_GDN_OUT + 1)), act_headnorm(act, 0, 0, 16, l2_roots, FULL)),
                lambda: act_gdn(act),
                lambda: (act_head_squares(act, 16, 16, qkv, 16, on_sq, FULL, bufs=16),
                         act_norm(act, (0, 1), FULL, stats=False),
                         act_headnorm(act, 1, 16, 16, on_roots, FULL),
                         act_two_layers(act, 0, HB_GDN_OUT, 2, FULL, ACT.Silu, 1),
                         act_norm(act, (1, 2), FULL),
                         act_two_layers(act, 2, HB_MLP0, 4, FULL, ACT.Relu, 2),
                         act_norm(act, (2, 3), FULL),
                         act_mls_in(act)),
                lambda: act_mls(act),
                lambda: (act_head_squares(act, 32, 8, ml, 8, mh_sq, FULL, bufs=8),
                         act_headnorm(act, 2, 32, 8, mh_roots, FULL),
                         act_mls_out(act),
                         act_norm(act, (3, 4), LATE),
                         act_mod_c(act),
                         act_two_layers(act, 6, HB_MLP1, 4, LATE, ACT.Relu, 4, beside=act_mod_load),
                         act_norm(act, (4, 5), LATE, beside=lambda: act_squares(act, 5, b_ctx, CTXP, sq=ctx_sq)),
                         act_b2_in(act, 0, 2),
                         act_norm(act, (5, 6), CTXP, dst=(bc_hi, bc_lo)),
                         act_b2_loads(act),
                         act_b2_in(act, 2, 2 * N_B2_IN)),
                lambda: (act_head_squares(act, 40, 6, b_qk, 0, hn_sq, TOK, bufs=6),
                         act_split(act, HalfBlock(HB_B2_OUT + 1)), act_decays(act),
                         act_headnorm(act, 3, 40, 6, hn_roots, TOK, heads=2)),
                lambda: None,
                lambda: act_ret(act),
                lambda: (act.wait_ge(S("rn_c"), RH), act_head_squares(act, 46, 4, b_q, 0, hn_sq, TOK, bufs=4),
                         act_headnorm(act, 4, 46, 4, hn_roots, TOK)),
                lambda: (act_att_keys(act), act_att(act)),
                lambda: (act_b2_out(act),
                         act_norm(act, (6, 7), LATE),
                         act_two_layers(act, 10, HB_MLP2, 4, LATE, ACT.Relu, 7),
                         act_norm_stats(act, (7, None), LATE)),
            ]:
                step()
                st.end()

        @block.vector
        def _(dve):
            st = Stages(dve, "DVE")
            dve.wait_ge(S("in"), IN_FIRST)
            dve_split(dve, HalfBlock(0))
            dve_split(dve, HalfBlock(1))
            for step in [
                lambda: (dve_norm(dve, (0, 0), h, FULL, lambda k: prm("attn_norm0", k), keep=True), dve_gdn_in(dve)),
                lambda: dve_headnorm(dve, 0, 0, 16, l2_roots, qkv, 0, FULL, 1.0, lambda i: prm_dyn("l2_gain", i), split=HalfBlock(HB_GDN_OUT + 1)),
                lambda: dve_gdn(dve),
                lambda: (dve_norm(dve, (0, 1), h, FULL, lambda k: prm("attn_norm0", k), stats=False),
                         dve_headnorm(dve, 1, 16, 16, on_roots, qkv, 16, FULL, 1.0 / P, lambda i: prm("gdn_norm", 0)),
                         dve_two_layers(dve, 0, HB_GDN_OUT, 2, FULL,
                                        gate=lambda i, t: qkv[:, bass.ds(i * 8 + (16 + t), 1), 0:T].rearrange("p a t -> p (a t)")),
                         dve_norm(dve, (1, 2), h, FULL, lambda k: prm("ffn_norm0", k), split=HalfBlock(HB_MLP0 + 1)),
                         dve_two_layers(dve, 2, HB_MLP0, 4, FULL),
                         dve_norm(dve, (2, 3), h, FULL, lambda k: prm("attn_norm1", k), split=HalfBlock(HB_MLS_GATES + 1)),
                         dve_mls_in(dve)),
                lambda: dve_mls(dve),
                lambda: (dve_headnorm(dve, 2, 32, 8, mh_roots, ml, 8, FULL, 1.0 / P, lambda i: prm_dyn("mls_norm", i)),
                         dve_mls_out(dve),
                         dve_norm(dve, (3, 4), h, LATE, lambda k: prm("ffn_norm1", k), split=HalfBlock(HB_MLP1 + 1)),
                         dve_mod_start(dve),
                         dve_two_layers(dve, 6, HB_MLP1, 4, LATE, beside=dve_mod_sums),
                         dve_mod(dve),
                         dve_norm(dve, (4, 5), h, LATE, lambda k: gain_col(0, k),
                                  shift=(lambda k: mod_col("shift1", k), 0), split=HalfBlock(HB_B2_IN + 1)),
                         dve_norm(dve, (5, 6), b_ctx, CTXP, lambda k: gain_col(1, k), shift=(ctx_shift, 1), dst=(bc_hi, bc_lo), at_=5),
                         dve_b2_in(dve)),
                lambda: (dve_decays(dve),
                         dve_headnorm(dve, 3, 40, 6, hn_roots, b_qk, 0, TOK, 1.0 / AHD, lambda i: prm_dyn("qk_norm", i), heads=2,
                                      split=HalfBlock(HB_B2_OUT + 1))),
                lambda: dve_rope(dve),
                lambda: dve_ret(dve),
                lambda: (dve_centre(dve), dve_headnorm(dve, 4, 46, 4, hn_roots, b_q, 0, TOK, 1.0 / P, lambda i: prm_dyn("ret_gn", i))),
                lambda: dve_att(dve),
                lambda: (dve_b2_out(dve),
                         dve_norm(dve, (6, 7), h, LATE, lambda k: gain_col(2, k),
                                  shift=(lambda k: mod_col("shift2", k), 2), split=HalfBlock(HB_MLP2 + 1)),
                         dve_two_layers(dve, 10, HB_MLP2, 4, LATE, scale=lambda k: mod_col("gate2", k)),
                         dve_final(dve)),
            ]:
                step()
                st.end()

        @block.tensor
        def _(pe):
            st = Stages(pe, "PE")
            pe.wait_ge(S("set"), 2)
            pe.wait_ge(S("in"), IN_FIRST)
            for step in [
                lambda: (pe_norm(pe, (0, 0), FULL), pe_gdn_in(pe)),
                lambda: pe_headnorm(pe, 0, 0, 16, l2_sq, l2_roots, FULL, sums=False),
                lambda: pe_gdn(pe),
                lambda: (pe_headnorm(pe, 1, 16, 16, on_sq, on_roots, FULL, bufs=16),
                         pe_two_layers(pe, 0, HB_GDN_OUT, 2, FULL, norm=1),
                         pe_norm(pe, (1, 2), FULL),
                         pe_two_layers(pe, 2, HB_MLP0, 4, FULL, norm=2),
                         pe_norm(pe, (2, 3), FULL),
                         pe_mls_in(pe)),
                lambda: pe_mls(pe),
                lambda: (pe_headnorm(pe, 2, 32, 8, mh_sq, mh_roots, FULL, bufs=8),
                         pe_mls_out(pe),
                         pe_norm(pe, (3, 4), LATE),
                         pe_two_layers(pe, 6, HB_MLP1, 4, LATE, norm=4),
                         pe_norm(pe, (4, 5), LATE),
                         pe_b2_in(pe)),
                lambda: (pe.wait_ge(S("in"), IN_ALL), pe_headnorm(pe, 3, 40, 6, hn_sq, hn_roots, TOK, heads=2, bufs=6)),
                lambda: pe_rope(pe),
                lambda: pe_ret(pe),
                lambda: (pe_centre(pe), pe_headnorm(pe, 4, 46, 4, hn_sq, hn_roots, TOK, bufs=4)),
                lambda: (pe_att_keys(pe), pe_att(pe)),
                lambda: (pe_b2_out(pe),
                         pe_norm(pe, (6, 7), LATE),
                         pe_two_layers(pe, 10, HB_MLP2, 4, LATE, norm=7, peel=True),
                         pe_norm(pe, (7, None), LATE)),
            ]:
                step()
                st.end()


def tiles_of(v):
    return np.ascontiguousarray(v.reshape(-1, P).T)


def half_blocks(w):
    n = w.shape[1] // HB_COLS
    return w.reshape(KT, P, n, HB_COLS).transpose(2, 1, 0, 3).reshape(n, P, HB_ELEMS)


def gate_block(parts):
    out = np.zeros((D, HB_COLS), np.float32)
    for i, w in enumerate(parts):
        out[:, 32 * i:32 * i + w.shape[1]] = w
    return half_blocks(out)


def two_layers(up, down):
    out = []
    for g in range(up.shape[1] // D):
        out += [half_blocks(up[:, g * D:(g + 1) * D]), half_blocks(down[g * D:(g + 1) * D])]
    return np.concatenate(out)


def mod_order(x):
    return x[[t for g in range(MOD_GROUPS) for t in [4 * g + n for n in range(4)] + [16 + 8 * g + n for n in range(8)]]]


def host_arrays(v):
    gi, gq = v["gdn_in"][0], 4096
    mi, bi = v["mlstm_in"][0], v["w_in_2"][0]
    weights = [
        gate_block([gi[:, gq + 2048 + GH:], gi[:, gq + 2048:gq + 2048 + GH]]), half_blocks(gi[:, :gq]),
        two_layers(gi[:, gq:gq + 2048], v["gdn_out"][0]),
        two_layers(v["ff_up"][0], v["ff_down"][0]),
        gate_block([mi[:, 3072:3072 + MH], mi[:, 3072 + MH:]]), half_blocks(mi[:, :3072]),
        half_blocks(v["mlstm_out"][0]),
        two_layers(v["ff_up"][1], v["ff_down"][1]),
        half_blocks(bi), half_blocks(v["w_out_2"][0]),
        two_layers(v["w_ff1_2"][0], v["w_ff2_2"][0]),
    ]
    params = np.zeros((P, N_PARAMS), np.float32)

    def put(name, x, rows=slice(0, P)):
        a, n = PARAMS[name]
        params[rows, a:a + n] = x

    for i in range(2):
        put(f"attn_norm{i}", tiles_of(v["attn_norm"][i]))
        put(f"ffn_norm{i}", tiles_of(v["ffn_norm"][i]))
    put("conv", v["gdn_conv"][0].reshape(4, 32, P).transpose(2, 1, 0).reshape(P, 128))
    put("gdn_norm", tiles_of(v["gdn_norm"][0]))
    put("mls_norm", tiles_of(v["mlstm_norm"][0]))
    put("a_log", v["gdn_a_log"][0][:, None], slice(0, GH))
    put("dt_bias", v["gdn_dt_bias"][0][:, None], slice(0, GH))
    put("gate_bias", v["mlstm_gate_bias"][0][:MH, None], slice(0, MH))
    put("gate_bias", v["mlstm_gate_bias"][0][MH:, None], slice(32, 32 + MH))
    for name, key in (("norm1_g", "norm1_g_2"), ("norm2_g", "norm2_g_2"), ("ret_gn", "ret_gn_g_2")):
        put(name, tiles_of(v[key][0]))
    put("final_g", tiles_of(v["final_norm_g_2"]))
    put("b_mod", mod_order(v["b_mod_2"][0].reshape(48, P)).T)
    for y in range(2):
        gains = [v["q_norm_g_2"][0]] * 4 + [v["k_norm_g_2"][0]] * 2
        put("qk_norm", np.stack(gains, 1), slice(64 * y, 64 * y + 64))
    put("l2_gain", np.repeat(np.float32([P ** -0.5, 1.0]), GQK)[None, :])
    put("ret_rate", v["ret_log_rate_2"][0].reshape(1, 8))
    tokens = np.concatenate([v["meta_tokens"], v["x"][0]])
    return {
        "weights": np.concatenate(weights),
        "weights_mod": mod_order(v["w_mod_2"][0].T.reshape(48, P, D)).reshape(24, 2, P, D).transpose(0, 2, 1, 3).reshape(24, P, 2 * D),
        "c_in": np.broadcast_to(np.stack([v["c_2"][0], v["c_ctx_2"]])[None], (P, 2, D)),
        "x_in": tokens.T.reshape(KT, P, T).transpose(1, 0, 2),
        "ctx_in": v["ctx_2"][0].T.reshape(KT, P, CTX).transpose(1, 0, 2),
        "params": params,
    }


def host_constants():
    i = np.arange(CH)
    lower = []
    for l in range(LEVELS):
        n = 1 << l
        same = (i[:, None] // (2 * n)) == (i[None, :] // (2 * n))
        lower.append(same & (i[:, None] // n % 2 == 1) & (i[None, :] // n % 2 == 0))
    mask_u = np.stack([m.T for m in lower], 1).astype(np.uint32)
    neg = np.where(i[None, :] >= i[:, None], 0.0, -1e30).astype(np.float32)
    sel = np.zeros((MH, P + 4), np.float32)
    for k in range(MH):
        sel[k, 64 * (k % 2):64 * (k % 2) + 64] = 1.0
        sel[k, P + k // 2] = 1.0
    pair = np.zeros((MH, 4, P), np.float32)
    for k in range(MH):
        pair[k, k // 2, 64 * (k % 2):64 * (k % 2) + 64] = 1.0
    t = np.arange(SEQ, dtype=np.float32)
    ret_f = np.float32(10000.0) ** (-np.arange(64, dtype=np.float32) / np.float32(64))
    att_f = np.float32(10000.0) ** (-np.arange(16, dtype=np.float32) / np.float32(16))
    ret_ang = t[:, None] * ret_f
    att_ang = np.concatenate([(t // 64)[:, None] * att_f, (t % 64)[:, None] * att_f], 1)
    rope, perm = np.zeros((P, 4, SEQ), np.float32), np.zeros((P, 2, P), np.float32)
    for n, ang in enumerate((ret_ang, att_ang)):
        w = ang.shape[1]
        for p in range(P):
            upper = p % (2 * w) >= w
            rope[p, 2 * n] = np.cos(ang[:, p % w])
            rope[p, 2 * n + 1] = np.sin(ang[:, p % w]) * (1.0 if upper else -1.0)
            perm[p - w if upper else p + w, n, p] = 1.0
    tau = (np.arange(SEQ + 3 * P)[None, :] - 3 * P - np.arange(P)[:, None]).astype(np.float32)
    pos = np.broadcast_to(np.stack([t + 1, SEQ - t])[None], (P, 2, SEQ))
    l = np.arange(P)[:, None] + P * np.arange(2)[None, :]
    half = (np.arange(P)[:, None] // 64 == np.arange(2)[None, :]).astype(np.float32)
    return {"rope": rope, "perm": perm, "tau": np.stack([np.maximum(tau, 0), np.maximum(-tau, 0)], 1),
            "pos": pos, "lpos": np.stack([CTX - 1 - l, l], 1).astype(np.float32), "half": half, "mls_pair": pair,
            "ident": np.eye(P, dtype=np.float32), "mask_u": mask_u, "neg": neg, "mls_sel": sel}


def kernel(**inputs):
    import concourse.bacc as _bacc
    from concourse.bass_utils import run_bass_kernel_spmd as _run

    v = {k: np.asarray(a) for k, a in inputs.items()}
    arrays = {k: np.ascontiguousarray(a) for k, a in {**host_arrays(v), **host_constants()}.items()}
    nc = _bacc.Bacc("TRN2", target_bir_lowering=False, num_devices=1)
    A = {k: nc.dram_tensor(k, a.shape, mybir.dt.from_np(a.dtype), kind="ExternalInput").ap() for k, a in arrays.items()}
    out = nc.dram_tensor("out", (P, KT, SEQ), F32, kind="ExternalOutput").ap()
    build_program(nc, A, out)
    r = _run(nc, [arrays], core_ids=[0])
    got = r.results[0]["out"]
    return np.ascontiguousarray(got.transpose(2, 1, 0).reshape(1, SEQ, D))
```
